# Optimizing a Trainium2 kernel written in Bass

```python
import math
import jax
import jax.numpy as jnp
from jax import lax
import numpy as np
import jax, jax.numpy as jnp

D_MODEL = 1024
BATCH = 1
SEQ = 256
DEPTH = 1

GRID_W = 64
CTX_LEN = 256

DA_HEADS = 4
DA_HEAD_DIM = 64
DA_V_DIM = 2 * DA_HEAD_DIM
DA_WIDTH = DA_HEADS * DA_V_DIM
HG_HEADS = 4
HG_HEAD_DIM = 128
HG_WIDTH = HG_HEADS * HG_HEAD_DIM
MIX_WIDTH = DA_WIDTH + HG_WIDTH
IN_WIDTH = 3 * DA_WIDTH + 5 * HG_WIDTH
SPLITS = (DA_WIDTH, 2 * DA_WIDTH, 3 * DA_WIDTH, 3 * DA_WIDTH + HG_WIDTH,
          3 * DA_WIDTH + 2 * HG_WIDTH, 3 * DA_WIDTH + 3 * HG_WIDTH, 3 * DA_WIDTH + 4 * HG_WIDTH)
CTX_KV_END = 3 * DA_WIDTH + 3 * HG_WIDTH
CTX_SPLITS = (DA_WIDTH, 2 * DA_WIDTH, 2 * DA_WIDTH + HG_WIDTH, 2 * DA_WIDTH + 2 * HG_WIDTH)
CHUNK = 64
Q_BLOCK = 128
N_EXPERTS = 16
CAPACITY_FACTOR = 2
EXPERT_FF = 1024
ROPE_THETA = 10000.0
NORM_EPS = 1e-6


def rmsnorm(x, g):
    xf = x.astype(jnp.float32)
    y = xf * lax.rsqrt(jnp.mean(xf * xf, axis=-1, keepdims=True) + NORM_EPS)
    return (y * g.astype(jnp.float32)).astype(x.dtype)

def modulate(h, shift, scale):
    return h * (1.0 + scale) + shift

def axial_rope_tables(rows):
    half = DA_HEAD_DIM // 2
    inv_freq = 1.0 / (ROPE_THETA ** (jnp.arange(0, half, 2, dtype=jnp.float32) / half))
    r, col = jnp.meshgrid(jnp.arange(rows, dtype=jnp.float32),
                          jnp.arange(GRID_W, dtype=jnp.float32), indexing="ij")
    ang_r = r.reshape(-1)[:, None] * inv_freq
    ang_c = col.reshape(-1)[:, None] * inv_freq
    ang = jnp.concatenate([ang_r, ang_r, ang_c, ang_c], axis=-1)
    return jnp.cos(ang), jnp.sin(ang)

def apply_axial_rope(x, cos, sin):
    xf = x.astype(jnp.float32)
    x1, x2, x3, x4 = jnp.split(xf, 4, axis=-1)
    rot = jnp.concatenate([-x2, x1, -x4, x3], axis=-1)
    return (xf * cos + rot * sin).astype(x.dtype)

def qk_heads(a):
    b, t = a.shape[:2]
    return a.reshape(b, t, DA_HEADS, 2, DA_HEAD_DIM).transpose(0, 2, 3, 1, 4)

def to_heads(a, n_heads, dim):
    b, t = a.shape[:2]
    return a.reshape(b, t, n_heads, dim).transpose(0, 2, 1, 3)

def merge_heads(o):
    b, h, t, d = o.shape
    return o.transpose(0, 2, 1, 3).reshape(b, t, h * d)

def diff_attend(q, k, v, lam):
    s = jnp.einsum("bhiqd,bhikd->bhiqk", q, k).astype(jnp.float32) * (DA_HEAD_DIM ** -0.5)
    p = jax.nn.softmax(s, axis=-1)
    a = p[:, :, 0] - lam * p[:, :, 1]
    return jnp.einsum("bhqk,bhkd->bhqd", a.astype(v.dtype), v)

def hgrn2_chunk_scan(k, v, log_f, s0, q=None):
    b_, h_, t_, _ = k.shape
    dv = v.shape[-1]
    n = t_ // CHUNK

    def chunks(a):
        return jnp.moveaxis(a.astype(jnp.float32).reshape(b_, h_, n, CHUNK, a.shape[-1]), 2, 0)

    lower = jnp.tril(jnp.ones((CHUNK, CHUNK), dtype=bool))[:, :, None]

    def step(S, inp):
        kc, vc, lc = inp[0], inp[1], inp[2]
        bcum = jnp.cumsum(lc, axis=2)
        b_end = bcum[:, :, -1:, :]
        S_next = (jnp.exp(b_end[:, :, 0, :, None]) * S
                  + jnp.einsum("bhsk,bhsv->bhkv", kc * jnp.exp(b_end - bcum), vc))
        if q is None:
            return S_next, None
        qc = inp[3]
        rel = bcum[:, :, :, None, :] - bcum[:, :, None, :, :]
        decay = jnp.exp(jnp.where(lower, rel, -jnp.inf))
        scores = jnp.einsum("bhrk,bhsk,bhrsk->bhrs", qc, kc, decay)
        o = (jnp.einsum("bhrk,bhkv->bhrv", qc * jnp.exp(bcum), S)
             + jnp.einsum("bhrs,bhsv->bhrv", scores, vc))
        return S_next, o

    xs = (chunks(k), chunks(v), chunks(log_f))
    if q is not None:
        xs = xs + (chunks(q),)
    S_fin, o = lax.scan(step, s0, xs)
    if q is not None:
        o = jnp.moveaxis(o, 0, 2).reshape(b_, h_, t_, dv).astype(v.dtype)
    return o, S_fin

def forget_gate(z, lb):
    f = lb + (1.0 - lb) * jax.nn.sigmoid(z.astype(jnp.float32))
    return jnp.log(f), 1.0 - f

def token_mixer(h_lat, h_ctx, w_in, w_out, lam, lambda_init, da_subln, lb, hg_norm, cos, sin, ctx_out):
    b_ = h_lat.shape[0]
    da_q, da_k, da_v, hg_ff, hg_fb, hg_i, hg_q, hg_g = jnp.split(h_lat @ w_in, SPLITS, axis=-1)
    c_da_k, c_da_v, c_ff, c_fb, c_i = jnp.split(h_ctx @ w_in[:, DA_WIDTH:CTX_KV_END], CTX_SPLITS, axis=-1)
    if ctx_out:
        c_da_q = h_ctx @ w_in[:, :DA_WIDTH]
        c_hg_q, c_hg_g = jnp.split(h_ctx @ w_in[:, CTX_KV_END:], 2, axis=-1)

    q = apply_axial_rope(qk_heads(da_q), cos, sin)
    k_ctx = qk_heads(c_da_k)
    k_all = jnp.concatenate([k_ctx, apply_axial_rope(qk_heads(da_k), cos, sin)], axis=3)
    v_ctx = to_heads(c_da_v, DA_HEADS, DA_V_DIM)
    v_all = jnp.concatenate([v_ctx, to_heads(da_v, DA_HEADS, DA_V_DIM)], axis=2)
    t_ = q.shape[3]
    n_blk = t_ // Q_BLOCK
    q_blocks = jnp.moveaxis(q.reshape(b_, DA_HEADS, 2, n_blk, Q_BLOCK, DA_HEAD_DIM), 3, 0)
    o_blocks = lax.map(lambda qb: diff_attend(qb, k_all, v_all, lam), q_blocks)
    o_da = jnp.moveaxis(o_blocks, 0, 2).reshape(b_, DA_HEADS, t_, DA_V_DIM)
    out_da = merge_heads(rmsnorm(o_da, da_subln) * (1.0 - lambda_init))

    v_lat = to_heads(hg_i, HG_HEADS, HG_HEAD_DIM)
    v_c = to_heads(c_i, HG_HEADS, HG_HEAD_DIM)
    q_lat = to_heads(hg_q, HG_HEADS, HG_HEAD_DIM)
    q_c = to_heads(c_hg_q, HG_HEADS, HG_HEAD_DIM) if ctx_out else None
    s0 = jnp.zeros((b_, HG_HEADS, HG_HEAD_DIM, HG_HEAD_DIM), jnp.float32)
    o_hg_lat = None
    o_hg_ctx = None
    for d, (z_lat, z_ctx) in enumerate(((hg_ff, c_ff), (hg_fb, c_fb))):
        flip = (lambda a: a) if d == 0 else (lambda a: jnp.flip(a, axis=2))
        lf_l, k_l = forget_gate(z_lat, lb[d])
        lf_c, k_c = forget_gate(z_ctx, lb[d])
        k_l, lf_l = to_heads(k_l, HG_HEADS, HG_HEAD_DIM), to_heads(lf_l, HG_HEADS, HG_HEAD_DIM)
        k_c, lf_c = to_heads(k_c, HG_HEADS, HG_HEAD_DIM), to_heads(lf_c, HG_HEADS, HG_HEAD_DIM)
        o_c, S_c = hgrn2_chunk_scan(flip(k_c), flip(v_c), flip(lf_c), s0,
                                    q=None if q_c is None else flip(q_c))
        o_l, _ = hgrn2_chunk_scan(flip(k_l), flip(v_lat), flip(lf_l), S_c, q=flip(q_lat))
        o_hg_lat = flip(o_l) if o_hg_lat is None else o_hg_lat + flip(o_l)
        if ctx_out:
            o_hg_ctx = flip(o_c) if o_hg_ctx is None else o_hg_ctx + flip(o_c)
    out_hg = merge_heads(rmsnorm(o_hg_lat, hg_norm)) * jax.nn.silu(hg_g)

    y_lat = jnp.concatenate([out_da, out_hg], axis=-1) @ w_out
    if not ctx_out:
        return y_lat, None
    o_c_da = diff_attend(qk_heads(c_da_q), k_ctx, v_ctx, lam)
    out_c_da = merge_heads(rmsnorm(o_c_da, da_subln) * (1.0 - lambda_init))
    out_c_hg = merge_heads(rmsnorm(o_hg_ctx, hg_norm)) * jax.nn.silu(c_hg_g)
    y_ctx = jnp.concatenate([out_c_da, out_c_hg], axis=-1) @ w_out
    return y_lat, y_ctx

def expert_choice_ffn(h, w_router, w_gate, w_up, w_down):
    b_, t_, d_ = h.shape
    cap = CAPACITY_FACTOR * t_ // N_EXPERTS
    aff = jax.nn.softmax(jnp.einsum("btd,de->bte", h, w_router).astype(jnp.float32), axis=-1)
    top_aff, top_idx = lax.top_k(jnp.swapaxes(aff, 1, 2), cap)
    xin = jax.vmap(lambda hb, ib: hb[ib])(h, top_idx)
    g = jnp.einsum("becd,edf->becf", xin, w_gate)
    u = jnp.einsum("becd,edf->becf", xin, w_up)
    y = jnp.einsum("becf,efd->becd", jax.nn.silu(g) * u, w_down) * top_aff[..., None].astype(h.dtype)
    return jax.vmap(lambda yb, ib: jnp.zeros((t_, d_), h.dtype).at[ib.reshape(-1)].add(yb.reshape(-1, d_)))(y, top_idx)

def first_inputs(seed: int = 0) -> dict:
    key = jax.random.key(seed)
    ks = jax.random.split(key, 24)
    D = D_MODEL

    def nrm(k, shape, scale):
        return jax.random.normal(k, shape, jnp.float32) * scale

    return {
        "x": nrm(ks[0], (BATCH, SEQ, D), 1.0),
        "c": nrm(ks[1], (BATCH, D), 1.0),
        "ctx": nrm(ks[2], (BATCH, CTX_LEN, D), 1.0),
        "c_ctx": nrm(ks[3], (D,), 1.0),
        "w_ada": nrm(ks[4], (DEPTH, D, 6 * D), 0.5 * D ** -0.5),
        "b_ada": nrm(ks[5], (DEPTH, 6 * D), 0.02),
        "norm_pre_mix": 1.0 + nrm(ks[6], (DEPTH, D), 0.05),
        "norm_post_mix": 1.0 + nrm(ks[7], (DEPTH, D), 0.05),
        "norm_pre_ffn": 1.0 + nrm(ks[8], (DEPTH, D), 0.05),
        "norm_post_ffn": 1.0 + nrm(ks[9], (DEPTH, D), 0.05),
        "w_in": nrm(ks[10], (DEPTH, D, IN_WIDTH), D ** -0.5),
        "da_lambda_q1": nrm(ks[11], (DEPTH, DA_HEAD_DIM), 0.1),
        "da_lambda_k1": nrm(ks[12], (DEPTH, DA_HEAD_DIM), 0.1),
        "da_lambda_q2": nrm(ks[13], (DEPTH, DA_HEAD_DIM), 0.1),
        "da_lambda_k2": nrm(ks[14], (DEPTH, DA_HEAD_DIM), 0.1),
        "da_subln": 1.0 + nrm(ks[15], (DEPTH, DA_V_DIM), 0.05),
        "hg_lower_bound": nrm(ks[16], (DEPTH + 1, 2, HG_WIDTH), 0.5),
        "hg_norm": 1.0 + nrm(ks[17], (DEPTH, HG_HEAD_DIM), 0.05),
        "w_out": nrm(ks[18], (DEPTH, MIX_WIDTH, D), MIX_WIDTH ** -0.5),
        "w_router": nrm(ks[19], (DEPTH, D, N_EXPERTS), D ** -0.5),
        "w_gate": nrm(ks[20], (DEPTH, N_EXPERTS, D, EXPERT_FF), D ** -0.5),
        "w_up": nrm(ks[21], (DEPTH, N_EXPERTS, D, EXPERT_FF), D ** -0.5),
        "w_down": nrm(ks[22], (DEPTH, N_EXPERTS, EXPERT_FF, D), EXPERT_FF ** -0.5),
    }

def first_block(x, c, ctx, c_ctx, w_ada, b_ada, norm_pre_mix, norm_post_mix, norm_pre_ffn, norm_post_ffn,
              w_in, da_lambda_q1, da_lambda_k1, da_lambda_q2, da_lambda_k2, da_subln, hg_lower_bound,
              hg_norm, w_out, w_router, w_gate, w_up, w_down):
    T = x.shape[1]
    ROWS = T // GRID_W
    cos, sin = axial_rope_tables(ROWS)
    lb_all = jnp.cumsum(jax.nn.softmax(hg_lower_bound.astype(jnp.float32), axis=0), axis=0)
    x_lat, x_ctx = x, ctx
    for l in range(DEPTH):
        last = l == DEPTH - 1
        lambda_init = 0.8 - 0.6 * math.exp(-0.3 * l)
        lam = (jnp.exp(jnp.sum(da_lambda_q1[l].astype(jnp.float32) * da_lambda_k1[l].astype(jnp.float32)))
               - jnp.exp(jnp.sum(da_lambda_q2[l].astype(jnp.float32) * da_lambda_k2[l].astype(jnp.float32)))
               + lambda_init)
        mod_lat = jax.nn.silu(c) @ w_ada[l] + b_ada[l]
        mod_ctx = jax.nn.silu(c_ctx) @ w_ada[l] + b_ada[l]
        sh1, sc1, gt1, sh2, sc2, gt2 = jnp.split(mod_lat[:, None, :], 6, axis=-1)
        csh1, csc1, cgt1, csh2, csc2, cgt2 = jnp.split(mod_ctx, 6, axis=-1)

        h_lat = modulate(rmsnorm(x_lat, norm_pre_mix[l]), sh1, sc1)
        h_ctx = modulate(rmsnorm(x_ctx, norm_pre_mix[l]), csh1, csc1)
        y_lat, y_ctx = token_mixer(h_lat, h_ctx, w_in[l], w_out[l], lam, lambda_init, da_subln[l],
                                   lb_all[l], hg_norm[l], cos, sin, not last)
        x_lat = x_lat + gt1 * rmsnorm(y_lat, norm_post_mix[l])
        h_lat = modulate(rmsnorm(x_lat, norm_pre_ffn[l]), sh2, sc2)
        f_lat = expert_choice_ffn(h_lat, w_router[l], w_gate[l], w_up[l], w_down[l])
        x_lat = x_lat + gt2 * rmsnorm(f_lat, norm_post_ffn[l])
        if not last:
            x_ctx = x_ctx + cgt1 * rmsnorm(y_ctx, norm_post_mix[l])
            h_ctx = modulate(rmsnorm(x_ctx, norm_pre_ffn[l]), csh2, csc2)
            f_ctx = expert_choice_ffn(h_ctx, w_router[l], w_gate[l], w_up[l], w_down[l])
            x_ctx = x_ctx + cgt2 * rmsnorm(f_ctx, norm_post_ffn[l])
    return x_lat


DEPTH_2 = 2

N_MIXERS = 2

MLA_HEADS = 8
QK_NOPE = 128
QK_ROPE = 64
V_DIM = 128
Q_LORA = 256
KV_LORA = 128
MLA_WIDTH = MLA_HEADS * V_DIM
MLA_IN_WIDTH = Q_LORA + KV_LORA + QK_ROPE + MLA_WIDTH
ROPE_AXIS_DIM = QK_ROPE // 2

FOURIER_WIDTH = D_MODEL
FOURIER_GROUPS = 8
FOURIER_GROUP_DIM = FOURIER_WIDTH // FOURIER_GROUPS

N_MLA_LAYERS = (DEPTH_2 + 1) // 2
N_FOURIER_LAYERS = DEPTH_2 // 2
ADA_STD = 0.5 * D_MODEL ** -0.5


def rms_norm(x, g):
    xf = x.astype(jnp.float32)
    y = xf * lax.rsqrt(jnp.mean(xf * xf, axis=-1, keepdims=True) + NORM_EPS)
    return (y * g.astype(jnp.float32)).astype(x.dtype)

def axial_rope_tables_2(row, col):
    inv_freq = 1.0 / (ROPE_THETA ** (jnp.arange(0, ROPE_AXIS_DIM, 2, dtype=jnp.float32) / ROPE_AXIS_DIM))
    ang_r = row.astype(jnp.float32)[:, None] * inv_freq[None, :]
    ang_c = col.astype(jnp.float32)[:, None] * inv_freq[None, :]
    return jnp.cos(ang_r), jnp.sin(ang_r), jnp.cos(ang_c), jnp.sin(ang_c)

def _rotate(t, cos, sin):
    t1, t2 = jnp.split(t, 2, axis=-1)
    return jnp.concatenate([t1 * cos - t2 * sin, t2 * cos + t1 * sin], axis=-1)

def apply_axial_rope_2(t, tables):
    cos_r, sin_r, cos_c, sin_c = [a.astype(t.dtype)[None, :, None, :] for a in tables]
    t_r, t_c = jnp.split(t, 2, axis=-1)
    return jnp.concatenate([_rotate(t_r, cos_r, sin_r), _rotate(t_c, cos_c, sin_c)], axis=-1)

def mla_query(c_q, g_qa, w_qup):
    b, t, _ = c_q.shape
    q = (rms_norm(c_q, g_qa) @ w_qup).reshape(b, t, MLA_HEADS, QK_NOPE + QK_ROPE)
    return q[..., :QK_NOPE], q[..., QK_NOPE:]

def mla_keyvalue(c_kv, g_kva, w_kvup):
    b, t, _ = c_kv.shape
    kv = (rms_norm(c_kv, g_kva) @ w_kvup).reshape(b, t, MLA_HEADS, QK_NOPE + V_DIM)
    return kv[..., :QK_NOPE], kv[..., QK_NOPE:]

def assemble_keys(k_nope, k_pe):
    return jnp.concatenate([k_nope, jnp.broadcast_to(k_pe, k_nope.shape[:-1] + (QK_ROPE,))], axis=-1)

def dense_attention(q, k, v):
    scale = 1.0 / math.sqrt(QK_NOPE + QK_ROPE)
    s = jnp.einsum('bqhd,bkhd->bhqk', q, k).astype(jnp.float32) * scale
    p = jax.nn.softmax(s, axis=-1).astype(v.dtype)
    return jnp.einsum('bhqk,bkhd->bqhd', p, v)

def latent_attention(q, k_lat, v_lat, k_ctx, v_ctx):
    b, t, h, dk = q.shape
    k_all = jnp.concatenate([k_ctx, k_lat], axis=1)
    v_all = jnp.concatenate([v_ctx, v_lat], axis=1)
    nb = t // Q_BLOCK
    qb = q.reshape(b, nb, Q_BLOCK, h, dk).transpose(1, 0, 2, 3, 4)
    o = lax.map(lambda qblk: dense_attention(qblk, k_all, v_all), qb)
    return o.transpose(1, 0, 2, 3, 4).reshape(b, t, h * V_DIM)

def fourier_mix(u, w_in, w_out):
    proj = u @ w_in
    z, gate = proj[..., :FOURIER_WIDTH], proj[..., FOURIER_WIDTH:]
    b, t, _ = z.shape
    zg = z.reshape(b, t, FOURIER_GROUPS, FOURIER_GROUP_DIM).astype(jnp.float32)
    y = jnp.fft.fftn(zg, axes=(1, 3), norm="ortho").real.astype(u.dtype).reshape(b, t, FOURIER_WIDTH)
    return (y * jax.nn.silu(gate)) @ w_out

def ada_params(cond_act, w, b):
    mod = cond_act @ w + b
    return jnp.split(mod, 3, axis=-1)

def second_inputs(seed: int = 0) -> dict:
    key = jax.random.key(seed)
    ks = jax.random.split(key, 16)
    n = jax.random.normal
    f32 = jnp.float32
    return {
        "x": n(ks[0], (BATCH, SEQ, D_MODEL), f32),
        "c": n(ks[1], (BATCH, D_MODEL), f32),
        "ctx": n(ks[2], (BATCH, CTX_LEN, D_MODEL), f32),
        "c_ctx": n(ks[3], (D_MODEL,), f32),
        "norm_g": 1.0 + 0.02 * n(ks[4], (DEPTH_2, D_MODEL), f32),
        "w_ada": ADA_STD * n(ks[5], (DEPTH_2, D_MODEL, 3 * D_MODEL), f32),
        "b_ada": 0.02 * n(ks[6], (DEPTH_2, 3 * D_MODEL), f32),
        "mla_w_in": D_MODEL ** -0.5 * n(ks[7], (N_MLA_LAYERS, D_MODEL, MLA_IN_WIDTH), f32),
        "mla_g_qa": 1.0 + 0.02 * n(ks[8], (N_MLA_LAYERS, Q_LORA), f32),
        "mla_w_qup": Q_LORA ** -0.5 * n(ks[9], (N_MLA_LAYERS, Q_LORA, MLA_HEADS * (QK_NOPE + QK_ROPE)), f32),
        "mla_g_kva": 1.0 + 0.02 * n(ks[10], (N_MLA_LAYERS, KV_LORA), f32),
        "mla_w_kvup": KV_LORA ** -0.5 * n(ks[11], (N_MLA_LAYERS, KV_LORA, MLA_HEADS * (QK_NOPE + V_DIM)), f32),
        "mla_w_out": MLA_WIDTH ** -0.5 * n(ks[12], (N_MLA_LAYERS, MLA_WIDTH, D_MODEL), f32),
        "fno_w_in": D_MODEL ** -0.5 * n(ks[13], (N_FOURIER_LAYERS, D_MODEL, 2 * FOURIER_WIDTH), f32),
        "fno_w_out": FOURIER_WIDTH ** -0.5 * n(ks[14], (N_FOURIER_LAYERS, FOURIER_WIDTH, D_MODEL), f32),
        "final_g": 1.0 + 0.02 * n(ks[15], (D_MODEL,), f32),
    }

def second_block(x, c, ctx, c_ctx, norm_g, w_ada, b_ada, mla_w_in, mla_g_qa, mla_w_qup, mla_g_kva,
              mla_w_kvup, mla_w_out, fno_w_in, fno_w_out, final_g):
    n_tok = x.shape[1]
    rows = n_tok // GRID_W
    row = jnp.repeat(jnp.arange(rows, dtype=jnp.int32), GRID_W)
    col = jnp.tile(jnp.arange(GRID_W, dtype=jnp.int32), rows)
    rope = axial_rope_tables_2(row, col)

    act_lat = jax.nn.silu(c)
    act_ctx = jax.nn.silu(c_ctx)
    h_lat, h_ctx = x, ctx
    kv_lo, kv_hi = Q_LORA, Q_LORA + KV_LORA
    pe_hi = kv_hi + QK_ROPE

    for i in range(DEPTH_2):
        mixer = i % N_MIXERS
        idx = i // N_MIXERS
        ctx_later = any(j % N_MIXERS == 0 for j in range(i + 1, DEPTH_2))

        sh_l, sc_l, gt_l = ada_params(act_lat, w_ada[i], b_ada[i])
        u_lat = rms_norm(h_lat, norm_g[i]) * (1.0 + sc_l[:, None, :]) + sh_l[:, None, :]
        sh_c, sc_c, gt_c = ada_params(act_ctx, w_ada[i], b_ada[i])

        if mixer == 0:
            w_in = mla_w_in[idx]
            u_ctx = rms_norm(h_ctx, norm_g[i]) * (1.0 + sc_c) + sh_c
            p_lat = u_lat @ w_in
            qn_l, qp_l = mla_query(p_lat[..., :kv_lo], mla_g_qa[idx], mla_w_qup[idx])
            kn_l, v_l = mla_keyvalue(p_lat[..., kv_lo:kv_hi], mla_g_kva[idx], mla_w_kvup[idx])
            kp_l = apply_axial_rope_2(p_lat[..., None, kv_hi:pe_hi], rope)
            q_l = jnp.concatenate([qn_l, apply_axial_rope_2(qp_l, rope)], axis=-1)
            k_l = assemble_keys(kn_l, kp_l)
            if ctx_later:
                p_ctx = u_ctx @ w_in
            else:
                p_ctx = u_ctx @ w_in[:, kv_lo:pe_hi]
                p_ctx = jnp.concatenate([jnp.zeros(p_ctx.shape[:-1] + (kv_lo,), p_ctx.dtype), p_ctx], axis=-1) if False else p_ctx
            off = 0 if not ctx_later else kv_lo
            kn_c, v_c = mla_keyvalue(p_ctx[..., off:off + KV_LORA], mla_g_kva[idx], mla_w_kvup[idx])
            k_c = assemble_keys(kn_c, p_ctx[..., None, off + KV_LORA:off + KV_LORA + QK_ROPE])

            o_lat = latent_attention(q_l, k_l, v_l, k_c, v_c)
            y_lat = (o_lat * jax.nn.silu(p_lat[..., pe_hi:])) @ mla_w_out[idx]
            if ctx_later:
                qn_c, qp_c = mla_query(p_ctx[..., :kv_lo], mla_g_qa[idx], mla_w_qup[idx])
                q_c = jnp.concatenate([qn_c, qp_c], axis=-1)
                b_, t_c = h_ctx.shape[0], h_ctx.shape[1]
                o_ctx = dense_attention(q_c, k_c, v_c).reshape(b_, t_c, MLA_WIDTH)
                y_ctx = (o_ctx * jax.nn.silu(p_ctx[..., pe_hi:])) @ mla_w_out[idx]
                h_ctx = h_ctx + gt_c * y_ctx
            h_lat = h_lat + gt_l[:, None, :] * y_lat
        else:
            y_lat = fourier_mix(u_lat, fno_w_in[idx], fno_w_out[idx])
            if ctx_later:
                u_ctx = rms_norm(h_ctx, norm_g[i]) * (1.0 + sc_c) + sh_c
                h_ctx = h_ctx + gt_c * fourier_mix(u_ctx, fno_w_in[idx], fno_w_out[idx])
            h_lat = h_lat + gt_l[:, None, :] * y_lat

    return rms_norm(h_lat, final_g)


def setup_inputs(seed=0):
    out = dict(first_inputs(seed))
    for name, value in second_inputs(seed + 1).items():
        if name != "x":
            out[name + "_2"] = value
    return out


def reference(
    x, c, ctx, c_ctx, w_ada, b_ada, norm_pre_mix, norm_post_mix, norm_pre_ffn, norm_post_ffn,
    w_in, da_lambda_q1, da_lambda_k1, da_lambda_q2, da_lambda_k2, da_subln, hg_lower_bound,
    hg_norm, w_out, w_router, w_gate, w_up, w_down, c_2, ctx_2, c_ctx_2, norm_g_2, w_ada_2,
    b_ada_2, mla_w_in_2, mla_g_qa_2, mla_w_qup_2, mla_g_kva_2, mla_w_kvup_2, mla_w_out_2,
    fno_w_in_2, fno_w_out_2, final_g_2,
):
    x = first_block(
        x, c, ctx, c_ctx, w_ada, b_ada, norm_pre_mix, norm_post_mix, norm_pre_ffn,
        norm_post_ffn, w_in, da_lambda_q1, da_lambda_k1, da_lambda_q2, da_lambda_k2, da_subln,
        hg_lower_bound, hg_norm, w_out, w_router, w_gate, w_up, w_down,
    )
    return second_block(
        x, c_2, ctx_2, c_ctx_2, norm_g_2, w_ada_2, b_ada_2, mla_w_in_2, mla_g_qa_2, mla_w_qup_2,
        mla_g_kva_2, mla_w_kvup_2, mla_w_out_2, fno_w_in_2, fno_w_out_2, final_g_2,
    )


_drawn_inputs = setup_inputs


def setup_inputs(seed=0):
    import zlib

    import numpy as np

    out = dict(_drawn_inputs(seed))
    spreads = {}
    factors = {'norm_post_ffn': 3.835,
     'da_lambda_k2': 3.493,
     'ctx_2': 5.718,
     'norm_g_2': 8.0,
     'b_ada_2': 4.955,
     'mla_g_qa_2': 8.0,
     'mla_w_qup_2': 2.975,
     'mla_g_kva_2': 8.0,
     'final_g_2': 2.882}
    for name, (base, spread) in spreads.items():
        noise = np.random.default_rng([zlib.crc32(name.encode()), seed]).standard_normal(out[name].shape)
        drawn = base * np.exp(spread * noise) if base else spread * noise
        out[name] = jnp.asarray(drawn.astype(out[name].dtype))
    for name, factor in factors.items():
        out[name] = (out[name] * factor).astype(out[name].dtype)
    return out
```

```python
from contextlib import ExitStack

import numpy as np
import concourse.bass as bass
from concourse import mybir

ALU = mybir.AluOpType
ACT = mybir.ActivationFunctionType
F32 = mybir.dt.float32
U8 = mybir.dt.uint8
AX = mybir.AxisListType.X

P = 128
D = 1024
J = D // P
T = 256
TB = T // P
TN = 512
HEADS = 4
DH = 64
E = 16
CAP = 2 * T // E
LAMBDA_INIT = 0.8 - 0.6 * float(np.exp(0.0))
EPS = 1e-6
LEVELS = [64, 32, 16, 8, 4, 2, 1]
MH = 8
NOPE, ROPE, QL, KVL = 128, 64, 256, 128
SLOTS = 6
LATE_SLOTS = 5
EARLY_SLOTS = 4
SLOT = J * TN


def f32_constants():
    s = np.arange(P)
    out, at = [], {}

    def put(name, a):
        a = np.asarray(a, np.float32).reshape(P, -1)
        at[name] = (sum(x.shape[1] for x in out), a.shape[1])
        out.append(a)

    put("ident", np.eye(P))
    put("after", s[:, None] > s[None, :])
    put("before", s[:, None] < s[None, :])
    put("ones", np.ones((P, P)))
    R = np.zeros((P, P))
    for b in range(0, P, 32):
        for i in range(16):
            R[b + 16 + i, b + i] = -1.0
            R[b + i, b + 16 + i] = 1.0
    put("rotate", R)
    half = DH // 2
    inv = (1.0 / (10000.0 ** (np.arange(0, half, 2, dtype=np.float32) / np.float32(half)))).astype(np.float32)
    r, c = np.meshgrid(np.arange(T // 64, dtype=np.float32), np.arange(64, dtype=np.float32), indexing="ij")
    ar = r.reshape(-1)[:, None] * inv
    ac = c.reshape(-1)[:, None] * inv
    ang = np.concatenate([ar, ar, ac, ac], -1).T.astype(np.float32)
    put("cos", np.tile(np.cos(ang), (2, 1)))
    put("sin", np.tile(np.sin(ang), (2, 1)))
    put("rank", np.tile(np.arange(1, CAP + 1), (P, 1)))
    return np.concatenate(out, 1), at


def fourier_constants():
    t = np.arange(T)
    a = 2 * np.pi * ((t[:, None] * t[None, :]) % T) / T
    cs = np.concatenate([np.cos(a), np.sin(a)], 1) / np.sqrt(T)
    c = np.arange(P)
    b = 2 * np.pi * ((c[:, None] * c[None, :]) % P) / P
    return np.concatenate([cs[:P], cs[P:], np.cos(b) / np.sqrt(P), -np.sin(b) / np.sqrt(P)], 1).astype(np.float32)


def level_masks():
    s = np.arange(P)
    out = []
    for L in LEVELS:
        same = (s[:, None] // (2 * L)) == (s[None, :] // (2 * L))
        sh, rh = (s[:, None] // L) % 2, (s[None, :] // L) % 2
        out += [same & (sh == 0) & (rh == 1), same & (sh == 1) & (rh == 0)]
    out.append(np.eye(P, dtype=bool))
    return np.concatenate(out, 1).astype(np.float32)


CONST, CONST_AT = f32_constants()
N_CONST = CONST.shape[1]
N_MASK = (2 * len(LEVELS) + 1) * P

ROWS = {}
_n = 0
for _name, _k in (("c", 8), ("c_ctx", 8), ("c_2", 8), ("c_ctx_2", 8), ("pre_mix", 8), ("pre_ffn", 8),
                  ("norm_g_2", 16), ("lower", 16), ("g_qa", 2), ("g_kva", 1)):
    ROWS[_name] = (_n, _k)
    _n += _k
N_ROWS = _n


class Steps:

    def __init__(self, eng, own, reached):
        self.eng, self.own, self.reached, self.last = eng, own, reached, None

    def did(self, ins, sem=None):
        s = sem or self.own
        self.reached[s.name] = self.reached.get(s.name, 0) + 1
        ins.then_inc(s, 1)
        self.last = (s, self.reached[s.name])

    def settle(self):
        self.eng.wait_ge(*self.last)


def block_program(nc, a, out):
    ctx = ExitStack()
    with ctx:
        sems = {}

        def sem(name):
            if name not in sems:
                sems[name] = ctx.enter_context(nc.semaphore(name))
            return sems[name]

        def sb(name, n, parts=P, dt=F32):
            return ctx.enter_context(nc.sbuf_tensor(name, [parts, n], dt))

        ring = sb("ring", SLOTS * SLOT)
        const = sb("const", N_CONST)
        masks = sb("masks", N_MASK, dt=U8)
        rows = sb("rows", P, N_ROWS)
        cols = sb("cols", N_ROWS)
        act32 = sb("act32", 2 * J * 32)
        modb = sb("modb", TN)
        modc = sb("modc", 6 * 2 * J)
        small = sb("small", 256)
        xres = sb("xres", TB * D)
        hT = sb("hT", J * 2 * T)
        pair = sb("pair", 2 * TB * D)
        ctxb, tmpb = pair[:, 0:TB * D], pair[:, TB * D:]
        qT = sb("qT", HEADS * T)
        kT = sb("kT", HEADS * 2 * T)
        vda = sb("vda", 2 * TB * TN)
        gates = sb("gates", 2 * 1024 + 2 * 1040)
        qh = sb("qh", HEADS * T)
        ilat = sb("ilat", TB * TN)
        smat = sb("smat", HEADS * T)
        state = sb("state", 2 * TN)
        state1 = sb("state1", 2 * TN)
        lamrow = smat[:, 0:4 * DH]
        subln = sb("subln", P)
        hgn = sb("hgn", P)
        junk = sb("junk", D, dt=mybir.dt.bfloat16)
        lbrow = (state, state1)

        def C(name):
            o, n = CONST_AT[name]
            return const[:, o:o + n]

        ident = C("ident")
        bank = [ctx.enter_context(nc.psum_tensor(f"bank{b}", [P, TN], F32)) for b in range(8)]
        filled = [sem(f"filled{b}") for b in range(8)]
        freed = [sem(f"freed{b}") for b in range(8)]
        landed = [sem(f"landed{s}") for s in range(SLOTS)]
        reached = {}
        turns, used = {}, [0] * 8

        def claim(name, b):
            turns[name] = (b, used[b])
            used[b] += 1

        def pe_take(pe, name):
            b, n = turns[name]
            if n:
                pe.wait_ge(freed[b], n)
            return bank[b]

        def wait_filled(eng, name):
            b, n = turns[name]
            eng.wait_ge(filled[b], n + 1)
            return bank[b]

        def wait_copied(eng, name):
            b, n = turns[name]
            eng.wait_ge(freed[b], n + 1)

        def fills(ins, name):
            ins.then_inc(filled[turns[name][0]], 1)

        def frees(steps, ins, name):
            b, n = turns[name]
            ins.then_inc(freed[b], 1)
            steps.last = (freed[b], n + 1)

        def wtile(w, n0, n=TN):
            return w[:, n0:n0 + n].rearrange("(j p) n -> p j n", p=P)

        w_in = a["w_in"][0]
        stream = []

        def tile(name, src):
            stream.append((name, src))

        for t in range(4):
            tile(("ada", 0, t), wtile(a["w_ada"][0], t * TN))
        for t in (3, 4, 6, 5, 1, 0, 2, 7):
            tile(("in", t), wtile(w_in, t * TN))
        for g in (1, 2):
            for t in range(4):
                tile(("ada", g, t), wtile(a["w_ada"][0], (4 * g + t) * TN))
        for g in range(3):
            for t in range(4):
                l, o = divmod((4 * g + t) * TN, 3 * D)
                tile(("ada2", g, t), wtile(a["w_ada_2"][l], o))
        tile(("kvctx",), wtile(a["mla_w_in_2"][0], QL, KVL + ROPE))
        for n in range(2):
            tile(("out", n), wtile(a["w_out"][0], n * TN))
        n_early = len(stream)
        slot_of, turn_of = {}, {}
        slot_uses = [0] * SLOTS
        late = [(("min", 0), wtile(a["mla_w_in_2"][0], 0, 448)),
                (("qup",), a["mla_w_qup_2"][0].rearrange("(j p) n -> p j n", p=P)),
                (("kvup",), a["mla_w_kvup_2"][0].rearrange("(j p) n -> p j n", p=P)),
                (("min", 1), wtile(a["mla_w_in_2"][0], 448)),
                (("min", 2), wtile(a["mla_w_in_2"][0], 960)),
                (("mout", 0), wtile(a["mla_w_out_2"][0], 0)),
                (("mout", 1), wtile(a["mla_w_out_2"][0], TN)),
                (("fin", 0), wtile(a["fno_w_in_2"][0], 0)),
                (("fin", 1), wtile(a["fno_w_in_2"][0], TN)),
                (("fin", 2), wtile(a["fno_w_in_2"][0], 2 * TN)),
                (("fin", 3), wtile(a["fno_w_in_2"][0], 3 * TN)),
                (("fout", 0), wtile(a["fno_w_out_2"][0], 0)),
                (("fout", 1), wtile(a["fno_w_out_2"][0], TN))]

        def place(name, s):
            slot_of[name], turn_of[name] = s, slot_uses[s]
            slot_uses[s] += 1

        for i, (name, _) in enumerate(stream):
            place(name, i % EARLY_SLOTS)
        expert_turn0 = list(slot_uses)
        for s in range(SLOTS):
            slot_uses[s] += E
        for i, (name, _) in enumerate(late):
            place(name, i % LATE_SLOTS)

        def last_reader(name):
            kind = name[0]
            if kind == "ada":
                return ("mod", name[1])
            if kind == "ada2":
                return ("mod2", name[1])
            if kind == "in":
                return {3: ("zc", 0, TB - 1), 4: ("zc", 1, TB - 1), 6: ("hq", 1), 5: ("i", 2 * TB - 1),
                        1: ("k", HEADS - 1), 0: ("q", 1), 2: ("v", 2 * TB - 1), 7: ("g", TB - 1)}[name[1]]
            return {"out": ("y", TB - 1, name[-1]), "kvctx": ("kvc", TB - 1), "qup": ("qr", MH // 2 - 1),
                    "kvup": ("v2", 2 * TB - 1, 1), "mout": ("y2", TB - 1, name[-1]),
                    "fout": ("y3", TB - 1, name[-1]),
                    "min": {0: ("pa", TB - 1), 1: ("g2", 1), 2: ("g2", 3)}.get(name[-1]),
                    "fin": {0: ("fz", TB - 1, 0), 1: ("fz", TB - 1, 1), 2: ("fg", 1), 3: ("fg", 3)}.get(name[-1])}[kind]

        def slot_view(s, j, n):
            return ring[:, s * SLOT:s * SLOT + j * n].rearrange("p (j n) -> p j n", j=j)

        def wait_tile(pe, name, j=J, n=TN):
            s = slot_of[name]
            pe.wait_ge(landed[s], 16 * (turn_of[name] + 1))
            return slot_view(s, j, n)

        scr = ring[:, EARLY_SLOTS * SLOT:SLOTS * SLOT]
        kd = [scr[:, d * 1024:(d + 1) * 1024] for d in range(2)]
        ictx = scr[:, 2048:3072]
        ebuf = [scr[:, 3072 + i * 1024:4096 + i * 1024] for i in range(2)]
        xbuf = [scr[:, 5120 + i * 1024:6144 + i * 1024] for i in range(3)]
        QB_, QF_ = kd
        KFB = ictx
        XFB = ebuf[0]

        hT3 = hT[:, :].rearrange("p (j t) -> p j t", j=J)
        xr3 = xres[:, :].rearrange("p (b d) -> p b d", b=TB)
        cx3 = ctxb[:, :].rearrange("p (b d) -> p b d", b=TB)
        tm3 = tmpb[:, :].rearrange("p (b d) -> p b d", b=TB)
        lfc = [ctxb[:, d * 1024:(d + 1) * 1024] for d in range(2)]
        kc = [tmpb[:, d * 1024:(d + 1) * 1024] for d in range(2)]
        gb = xbuf[0]
        q3 = qT[:, :].rearrange("p (h t) -> p h t", h=HEADS)
        k3 = kT[:, :].rearrange("p (h t) -> p h t", h=HEADS)
        v3 = vda[:, :].rearrange("p (b n) -> p b n", b=2 * TB)
        kg = [gates[:, d * 1024:(d + 1) * 1024] for d in range(2)]
        Bc = [gates[:, 2048 + d * 1040:2048 + (d + 1) * 1040].rearrange("p (h t) -> p h t", t=130) for d in range(2)]
        colof = lambda n: cols[:, ROWS[n][0]:ROWS[n][0] + ROWS[n][1]]
        act_cols = [act32[:, l * 256:(l + 1) * 256].rearrange("p (j m) -> p j m", j=J) for l in range(2)]
        ssq = small[:, 0:8]
        rr = small[:, 8:16]
        lbc = small[:, 16:24]
        omlb = small[:, 24:32]
        lamc = small[:, 32:33]
        dec = small[:, 40:48]
        mx = small[:, 48:56]
        rs = small[:, 56:64]
        cf = small[:, 64:80]
        lnb = small[:, 80:88]
        ssum = small[:, 88:90]
        epsc = small[:, 90:91]
        ecol = small[:, 96:128]
        lbt = small[:, 128:152]
        mc = modc[:, :].rearrange("p (s k j) -> p s k j", k=2, j=J)
        MIX, MIXC, FFN, MLA, MLAC, FNO = range(6)

        claim("rows", 0)
        for s in range(2):
            for b in range(TB):
                for g in range(2):
                    claim(("xT", s, b, g), 2 + (2 * b + g) % 2)
        claim(("mod", 0), 0)
        claim(("modT", 0), 1)
        pb = [0]

        def pclaim(name):
            claim(name, pb[0] % 4)
            pb[0] += 1

        def claim_gate(d):
            for hp in range(2):
                pclaim(("z", d, hp))
            for b in range(TB):
                pclaim(("zc", d, b))

        claim_gate(0)
        claim_gate(1)
        for hp in range(2):
            pclaim(("hq", hp))
        for d in range(2):
            for b in range(TB):
                pclaim(("dsum", d, b))
        for b in range(2 * TB):
            pclaim(("i", b))
        for d in range(2):
            pclaim(("S", d))
        lb_turn = [0]

        def claim_level(i, d):
            for g in range(2):
                claim(("lv", i, d, g), 4 + lb_turn[0] % 4)
                lb_turn[0] += 1

        for i in range(0, 2):
            for d in range(2):
                claim_level(i, d)
        for h in range(HEADS):
            pclaim(("k", h))
        for i in range(2, 4):
            for d in range(2):
                claim_level(i, d)
        for hp in range(2):
            pclaim(("q", hp))
        for i in range(4, 7):
            for d in range(2):
                claim_level(i, d)
        claim_level(7, 0)
        for b in range(2 * TB):
            pclaim(("v", b))
        claim(("cross", 0), 4 + lb_turn[0] % 4)
        claim(("cross", 1), 4 + (lb_turn[0] + 1) % 4)
        lb_turn[0] += 2
        for b in range(TB):
            claim(("oh", b), 4 + lb_turn[0] % 4)
            lb_turn[0] += 1
        for b in range(TB):
            pclaim(("g", b))
        for s in range(2):
            for n in range(2):
                pclaim(("rot", s, n))

        nq = 0
        for b in range(TB):
            for h in range(HEADS):
                for i in range(2):
                    claim(("s", b, h, i), nq % 4)
                    nq += 1
        nt = 0
        for b in range(TB):
            for h in range(HEADS):
                claim(("aT", b, h), 4 + nt % 2)
                nt += 1
            claim(("o", b), 6 + b)
        for g in (1, 2):
            claim(("mod", g), 0)
            claim(("modT", g), 1)
            for t in ((0, 1) if g == 1 else (2, 3)):
                claim(("gt", g, t), 2 + t % 2)
        for g in range(3):
            claim(("mod2", g), 0)
            claim(("modT2", g), 1)
            for t in {0: (), 1: (0, 1), 2: (2, 3)}[g]:
                claim(("gt2", g, t), 2 + t % 2)
        for b in range(TB):
            for g in range(2):
                claim(("c2T", b, g), 4 + (2 * b + g) % 4)
        for b in range(TB):
            claim(("kvc", b), 4 + b)
        claim(("kvcT",), 6)
        claim(("kpcT",), 7)
        for b in range(TB):
            for g in range(2):
                claim(("mixT", b, g), 4 + (2 * b + g) % 4)
        for n in range(2):
            for b in range(TB):
                claim(("y", b, n), 2 * b + n)
        for b in range(TB):
            for g in range(2):
                claim(("x1T", b, g), 4 + (2 * b + g) % 4)
        for b in range(TB):
            claim(("logit", b), b)
        claim(("affT",), 2)
        claim(("posT",), 3)
        for j in range(J):
            claim(("xin", j), j % 4)
        for e in range(0, E, 2):
            claim(("ST", e), (e // 2) % 4)
        exp_base = list(used)
        for b in range(4):
            used[b] += E
        for b in range(TB):
            for n in range(2):
                claim(("f", b, n), 4 + 2 * b + n)

        def late_claims():
            for b in range(TB):
                for g in range(2):
                    claim(("x2T", b, g), (2 * b + g) % 4)
            for b in range(TB):
                claim(("pa", b), 4 + b)
            claim(("cqT",), 6)
            claim(("ckT",), 7)
            for h in range(MH // 2):
                claim(("qn", h), h % 4)
            for h in range(MH // 2):
                claim(("qr", h), h % 4)
            for h in range(MH // 2):
                claim(("qrot", h), 4 + h % 4)
            claim(("krot",), 0)
            n = 1
            for h in range(MH):
                claim(("kn", h), n % 4)
                n += 1
            for b in range(2 * TB):
                for g in range(2):
                    claim(("v2", b, g), n % 4)
                    n += 1
            for m in range(MH // 2):
                claim(("g2", m), 4 + m % 4)
            k = 0
            for h in range(MH):
                for b in range(TB):
                    claim(("s2", h, b), k % 3)
                    k += 1
            k = 0
            for h in range(MH):
                for b in range(TB):
                    claim(("pT", h, b), 3 + k % 3)
                    k += 1
                claim(("o2", h), 6 + h % 2)
            for b in range(TB):
                for n in range(2):
                    claim(("y2", b, n), 2 * b + n)
            for b in range(TB):
                for g in range(2):
                    claim(("x3T", b, g), 4 + (2 * b + g) % 4)
            for n in range(2):
                for b in range(TB):
                    claim(("fz", b, n), 2 * b + n)
            for m in range(MH // 2):
                claim(("fg", m), 4 + m)
            for g in range(8):
                claim(("fa", g), g % 4)
            for m in range(4):
                claim(("fb", m), 4 + m)
            for b in range(TB):
                for n in range(2):
                    claim(("y3", b, n), 2 * b + n)

        late_claims()

        qz = [qh, smat]
        pbuf = [gates[:, i * 512:(i + 1) * 512] for i in range(4)]
        aTb = [gates[:, 2048 + i * 512:2560 + i * 512] for i in range(2)]
        oda = gates[:, 3072:4096].rearrange("p (b n) -> p b n", b=TB)
        mix = tmpb[:, :].rearrange("p (b d) -> p b d", b=TB)
        mixT = kT[:, :].rearrange("p (j t) -> p j t", j=J)
        G = [hT[:, i * D:(i + 1) * D] for i in range(4)]
        c2 = ctxb[:, :].rearrange("p (b d) -> p b d", b=TB)
        uT = vda[:, :].rearrange("p (j t) -> p j t", j=J)
        kvn = state[:, 0:256].rearrange("p (b n) -> p b n", b=TB)
        kvn2 = state[:, 512:768].rearrange("p (b n) -> p b n", b=TB)
        rtmp = gates[:, 3072:4096]
        xn = tmpb[:, :].rearrange("p (b d) -> p b d", b=TB)
        h2T = kT[:, :].rearrange("p (j t) -> p j t", j=J)
        router = qh[:, 0:J * E].rearrange("p (j e) -> p j e", j=J)
        logit = smat[:, 0:TB * E].rearrange("p (b e) -> p b e", b=TB)
        aff = smat[:, 64:64 + TB * E].rearrange("p (b e) -> p b e", b=TB)
        pos = smat[:, 128:128 + TB * E].rearrange("p (b e) -> p b e", b=TB)
        affT, work = smat[0:E, 160:416], smat[0:E, 416:672]
        top8 = smat[0:E, 672:680]
        onehot = vda[:, 0:TB * E * CAP].rearrange("p (b e c) -> p b e c", b=TB, e=E)
        onehot2 = vda[:, 0:TB * E * CAP].rearrange("p (b n) -> p b n", b=TB)
        weighted = vda[:, 1024:1024 + TB * E * CAP].rearrange("p (b e c) -> p b e c", b=TB, e=E)
        xin_all = gates[:, 0:4096].rearrange("p (j n) -> p j n", j=J)
        s_all = pair[:, :]
        sall3 = s_all[:, :].rearrange("p (e t) -> p e t", e=E)
        xin_cur = ilat[:, 0:256].rearrange("p (j c) -> p j c", j=J)
        hmT = ilat[:, 256:512].rearrange("p (j n) -> p j n", j=4)
        s_cur = ilat[:, 512:768]
        hidden_rows = state[:, 512:1024]
        eg, hm = state[0:64, 0:512], hidden_rows[0:64]
        yb = [state1[:, i * 512:(i + 1) * 512] for i in range(2)]
        zeros = qh[:, 256:256 + P + TN]
        cqn = state[:, 0:512].rearrange("p (b n) -> p b n", b=TB)
        cqT = state[:, 512:1024].rearrange("p (c t) -> p c t", c=2)
        kvl = state1[:, 0:256].rearrange("p (b n) -> p b n", b=TB)
        kpl = state1[:, 256:512].rearrange("p (b n) -> p b n", b=TB)
        u2T = kT[:, :].rearrange("p (j t) -> p j t", j=J)
        qraw = smat
        fgrow = state[:, :]
        ckv_all = qT[:, 512:1024]
        kp_all = qT[:, 0:512]
        ckv_ctx, kp_ctx = ckv_all[:, T:2 * T], kp_all[:, T:2 * T]
        rt = state1[:, 512:1024]
        knT = ring[:, (SLOTS - 1) * SLOT:].rearrange("p (h t) -> p h t", h=MH)
        v2 = gates[:, 0:4096].rearrange("p (b n) -> p b n", b=2 * TB)
        qnT = ctxb[:, :].rearrange("p (h t) -> p h t", h=MH)
        qrz = vda[:, :].rearrange("p (h t) -> p h t", h=MH)
        gT = tmpb[:, :].rearrange("p (h t) -> p h t", h=MH)
        oT = kT[:, :].rearrange("p (h t) -> p h t", h=MH)
        p2 = [smat[:, i * 512:(i + 1) * 512] for i in range(2)]
        pTs = [x[:, :].rearrange("p (k t) -> p k t", k=4) for x in (ilat, qh)]
        z3 = ctxb[:, :].rearrange("p (b d) -> p b d", b=TB)
        faT = [vda[:, i * 512:(i + 1) * 512] for i in range(4)]
        gT3 = gates[:, 0:2048].rearrange("p (h t) -> p h t", h=MH)
        oT3 = gates[:, 2048:4096].rearrange("p (h t) -> p h t", h=MH)
        fft = hT[:, 0:1280]

        block = ctx.enter_context(nc.Block())

        def mod_bias(eng, l, g, name):
            flat = a["b_ada"] if l == 0 else a["b_ada_2"].rearrange("l n -> (l n)").rearrange("(a n) -> a n", a=1)
            for t in range(4):
                o = (4 * g + t) * TN
                eng.dma_start(modb[32 * t:32 * t + 32, :], flat[0, o:o + TN].partition_broadcast(32))\
                   .then_inc(sem(name), 16)

        def expert_src(w, e, n):
            return w[bass.ds(e, 1), :, n * TN:(n + 1) * TN].rearrange("e (j p) n -> p (e j) n", p=P)

        expert_tiles = [(a["w_gate"][0], 0), (a["w_gate"][0], 1), (a["w_up"][0], 0), (a["w_up"][0], 1),
                        (a["w_down"][0], 0), (a["w_down"][0], 1)]
        expert_bank = [0, 0, 0, 0, 2, 3]

        @block.sync
        def _(sp):
            sp.dma_start(rows[:, :], a["rows"]).then_inc(sem("rows_in"), 16)
            for i, (name, src) in enumerate(stream):
                if i >= EARLY_SLOTS:
                    wait_filled(sp, last_reader(stream[i - EARLY_SLOTS][0]))
                s = slot_of[name]
                sp.dma_start(slot_view(s, src.shape[1], src.shape[2]), src).then_inc(landed[s], 16)
            for s in (4, 5, 0, 1, 2, 3):
                if s == EARLY_SLOTS:
                    sp.wait_ge(sem("scratch_done"), 1)
                if s < EARLY_SLOTS:
                    wait_filled(sp, last_reader([n for n, _ in stream if slot_of[n] == s][-1]))
                w, n = expert_tiles[s]
                sp.dma_start(slot_view(s, J, TN), expert_src(w, 0, n)).then_inc(landed[s], 16)
            with sp.Fori(1, E) as e:
                for s, (w, n) in enumerate(expert_tiles):
                    b = expert_bank[s]
                    sp.wait_ge(filled[b], e + exp_base[b])
                    sp.dma_start(slot_view(s, J, TN), expert_src(w, e, n)).then_inc(landed[s], 16)
            for i, (name, src) in enumerate(late):
                s = slot_of[name]
                if i < LATE_SLOTS:
                    sp.wait_ge(filled[expert_bank[s]], E + exp_base[expert_bank[s]])
                else:
                    wait_filled(sp, last_reader(late[i - LATE_SLOTS][0]))
                sp.dma_start(slot_view(s, src.shape[1], src.shape[2]), src).then_inc(landed[s], 16)
            for b in range(TB):
                sp.wait_ge(sem("result"), b + 1)
                sp.dma_start(out[0].rearrange("(b p) d -> p b d", p=P)[:, b, :], xr3[:, b, :])\
                  .then_inc(sem("stored"), 16)
            sp.wait_ge(sem("stored"), 16 * TB)

        @block.gpsimd
        def _(pool):
            pool.dma_start(const[:, :], a["const"]).then_inc(sem("const_in"), 16)
            pool.dma_start(xr3, a["x"][0].rearrange("(b p) d -> p b d", p=P)).then_inc(sem("x_in"), 16)
            pool.dma_start(cx3, a["ctx"][0].rearrange("(b p) d -> p b d", p=P)).then_inc(sem("ctx_in"), 16)
            mod_bias(pool, 0, 0, "bias0")
            for l in range(2):
                pool.dma_start(lbrow[l][:, :], a["hg_lower_bound"].rearrange("l d n -> l (d n)")[l]
                               .partition_broadcast(P)).then_inc(sem("side_in"), 16)
            for i, n in enumerate(("da_lambda_q1", "da_lambda_k1", "da_lambda_q2", "da_lambda_k2")):
                pool.dma_start(lamrow[:, i * DH:(i + 1) * DH], a[n][0].partition_broadcast(P))\
                    .then_inc(sem("side_in"), 16)
            pool.dma_start(subln[:, :], a["da_subln"][0].partition_broadcast(P)).then_inc(sem("side_in"), 16)
            pool.dma_start(hgn[:, :], a["hg_norm"][0].partition_broadcast(P)).then_inc(sem("side_in"), 16)
            pool.dma_start(scr[:, 5120:5120 + N_MASK], a["mask"]).then_inc(sem("mask_in"), 16)
            wait_filled(pool, ("g", TB - 1))
            pool.dma_start(G[0], a["norm_post_mix"][0].partition_broadcast(P)).then_inc(sem("post_in"), 16)
            pool.dma_start(G[1], a["norm_post_ffn"][0].partition_broadcast(P)).then_inc(sem("post_in"), 16)
            wait_filled(pool, ("oh", TB - 1))
            pool.dma_start(c2, a["ctx_2"][0].rearrange("(b p) d -> p b d", p=P)).then_inc(sem("ctx2_in"), 16)
            wait_filled(pool, ("modT", 0))
            mod_bias(pool, 0, 1, "bias1")
            wait_filled(pool, ("modT", 1))
            wait_filled(pool, ("gt", 1, 1))
            mod_bias(pool, 0, 2, "bias2")
            wait_filled(pool, ("modT", 2))
            wait_filled(pool, ("gt", 2, 3))
            mod_bias(pool, 1, 0, "bias3")
            wait_filled(pool, ("modT2", 0))
            mod_bias(pool, 1, 1, "bias4")
            wait_filled(pool, ("modT2", 1))
            wait_filled(pool, ("gt2", 1, 1))
            mod_bias(pool, 1, 2, "bias5")
            wait_filled(pool, ("s", TB - 1, HEADS - 1, 1))
            pool.dma_start(router, a["w_router"][0].rearrange("(j p) e -> p j e", p=P)).then_inc(sem("router_in"), 16)
            pool.memset(zeros, 0.0).then_inc(sem("zeros_set"), 1)
            wait_copied(pool, ("xin", J - 1))
            wait_copied(pool, ("xin", J - 2))
            wait_copied(pool, ("ST", E - 2))
            with pool.Fori(0, E) as e:
                pool.wait_ge(filled[0], e + exp_base[0])
                pool.tensor_copy(xin_cur, xin_all[:, :, bass.ds(e * CAP, CAP)]).then_inc(sem("tokens"), 1)
                pool.wait_ge(sem("scattered"), e + 1)
                pool.tensor_copy(s_cur, s_all[:, bass.ds(e * T, T)]).then_inc(sem("scatter_matrix"), 1)
            pool.wait_ge(sem("x_updated"), 2 * TB)
            pool.dma_start(fft, a["fft"]).then_inc(sem("fft_in"), 16)
            wait_filled(pool, ("qr", MH // 2 - 1))
            pool.dma_start(fgrow, a["final_g_2"].partition_broadcast(P)).then_inc(sem("fg_in"), 16)

        @block.tensor
        def _(pe):
            def sum_of(o, terms, start=True, stop=True):
                for i, (l, r) in enumerate(terms):
                    ins = pe.matmul(o, l, r, start=start and i == 0, stop=stop and i == len(terms) - 1)
                return ins

            def turn_chunks(name, src, g):
                o = pe_take(pe, name)
                for jj in range(4):
                    j = 4 * g + jj
                    ins = pe.transpose(o[:, jj * P:(jj + 1) * P], src[:, j * P:(j + 1) * P], ident)
                fills(ins, name)

            def modulation(l, g, tag, tagT):
                kind = ("ada", "ada2")[l]
                w = [wait_tile(pe, (kind, g, t)) for t in range(4)]
                o = pe_take(pe, (tag, g))
                for j in range(J):
                    for t in range(4):
                        ins = pe.matmul(o[32 * t:32 * t + 32, :], act_cols[l][:, j, :], w[t][:, j, :],
                                        start=j == 0, stop=j == J - 1)
                fills(ins, (tag, g))

            def mod_columns(g, tag, tagT, picks, tagG):
                wait_copied(pe, (tag, g))
                o = pe_take(pe, (tagT, g))
                for jj in range(4):
                    ins = pe.transpose(o[:, jj * P:(jj + 1) * P], modb[:, jj * P:(jj + 1) * P], ident)
                fills(ins, (tagT, g))
                for t in picks:
                    name = (tagG, g, t)
                    o = pe_take(pe, name)
                    row = ident[:, 32 * t:32 * t + 1].broadcast_to([P, P])
                    fills(pe.matmul(o[:, :], row, modb[:, :], start=True, stop=True), name)

            pe.wait_ge(sem("const_in"), 16)
            pe.wait_ge(sem("rows_in"), 16)
            o = pe_take(pe, "rows")
            fills(pe.transpose(o[:, 0:N_ROWS], rows[:, :], ident[0:N_ROWS, 0:N_ROWS]), "rows")
            for s, src in enumerate((tm3, cx3)):
                for b in range(TB):
                    pe.wait_ge(sem("normed"), 2 * s + b + 1)
                    for g in range(2):
                        turn_chunks(("xT", s, b, g), src[:, b, :], g)
            pe.wait_ge(sem("silu_c"), 1)
            modulation(0, 0, "mod", "modT")
            mod_columns(0, "mod", "modT", (), "gt")

            pe.wait_ge(sem("hT_ready"), 1)
            def heads_out(name, w, hs, rhs, n):
                o = pe_take(pe, name)
                for i, h in enumerate(hs):
                    ins = sum_of(o[:, i * n:(i + 1) * n], [(w[:, j, h * P:(h + 1) * P], rhs[j]) for j in range(J)])
                fills(ins, name)

            def tokens_out(name, w, x, b, n=TN, n0=0):
                o = pe_take(pe, name)
                fills(sum_of(o[:, 0:n], [(x[:, j, b * P:(b + 1) * P], w[:, j, n0:n0 + n]) for j in range(J)]), name)

            lat = [hT3[:, j, 0:T] for j in range(J)]
            for d in range(2):
                w = wait_tile(pe, ("in", 3 + d))
                for hp in range(2):
                    heads_out(("z", d, hp), w, (2 * hp, 2 * hp + 1), lat, T)
                for b in range(TB):
                    tokens_out(("zc", d, b), w, hT3, TB + b)
            w = wait_tile(pe, ("in", 6))
            for hp in range(2):
                heads_out(("hq", hp), w, (2 * hp, 2 * hp + 1), lat, T)
            for d in range(2):
                pe.wait_ge(sem("lfc_ready"), d + 1)
                tri = C(("after", "before")[d])
                for b in range(TB):
                    o = pe_take(pe, ("dsum", d, b))
                    terms = [(tri, lfc[d][:, b * TN:(b + 1) * TN])]
                    if b == d:
                        terms.append((C("ones"), lfc[d][:, (1 - b) * TN:(2 - b) * TN]))
                    fills(sum_of(o[:, :], terms), ("dsum", d, b))
            w = wait_tile(pe, ("in", 5))
            for b in range(2 * TB):
                tokens_out(("i", b), w, hT3, b)
            for b in range(2 * TB):
                wait_copied(pe, ("i", b))
            for d in range(2):
                pe.wait_ge(sem("kd_ready"), d + 1)
                o = pe_take(pe, ("S", d))
                for h in range(HEADS):
                    ins = sum_of(o[:, h * P:(h + 1) * P],
                                 [(kd[d][:, b * TN + h * P:b * TN + (h + 1) * P],
                                   ictx[:, b * TN + h * P:b * TN + (h + 1) * P]) for b in range(TB)])
                fills(ins, ("S", d))

            def level(i):
                for d in range(2 if i < len(LEVELS) else 1):
                    pe.wait_ge(sem("x_ready"), 2 * i + d + 1)
                    x = xbuf[(2 * i + d) % 3]
                    for g in range(2):
                        o = pe_take(pe, ("lv", i, d, g))
                        for k in range(4):
                            c = (4 * g + k) * P
                            r = x if i < len(LEVELS) else qh
                            ins = pe.matmul(o[:, k * P:(k + 1) * P], x[:, c:c + P], r[:, c:c + P],
                                            start=True, stop=True)
                        fills(ins, ("lv", i, d, g))

            for i in range(0, 2):
                level(i)
            w = wait_tile(pe, ("in", 1))
            for h in range(HEADS):
                heads_out(("k", h), w, (h,), [hT3[:, j, :] for j in range(J)], 2 * T)
            for i in range(2, 4):
                level(i)
            w = wait_tile(pe, ("in", 0))
            for hp in range(2):
                heads_out(("q", hp), w, (2 * hp, 2 * hp + 1), lat, T)
            for i in range(4, 8):
                level(i)
            w = wait_tile(pe, ("in", 2))
            for b in range(2 * TB):
                tokens_out(("v", b), w, hT3, b)
            pe.wait_ge(sem("cross_ready"), 1)
            for d in range(2):
                o = pe_take(pe, ("cross", d))
                q_ = (QF_, QB_)[d]
                for h in range(HEADS):
                    r0 = (2 * h + 1 - d) * P
                    ins = pe.matmul(o[:, h * P:(h + 1) * P], KFB[:, d * TN + h * P:d * TN + (h + 1) * P],
                                    q_[:, r0:r0 + P], start=True, stop=True)
                fills(ins, ("cross", d))
            wait_copied(pe, ("cross", 0))
            wait_copied(pe, ("cross", 1))
            wait_copied(pe, ("S", 0))
            wait_copied(pe, ("S", 1))
            pe.wait_ge(sem("state1_ready"), 1)
            wait_copied(pe, ("lv", 7, 0, 1))
            wait_copied(pe, ("lv", 7, 0, 0))
            for b in range(TB):
                o = pe_take(pe, ("oh", b))
                for h in range(HEADS):
                    c = (2 * h + b) * P
                    hs = slice(h * P, (h + 1) * P)
                    sf = state[:, h * P:(h + 1) * P] if b == 0 else state1[:, h * P:(h + 1) * P]
                    sbk = (state1 if b == 0 else state)[:, TN + h * P:TN + (h + 1) * P]
                    ins = sum_of(o[:, hs], [
                        (smat[:, c:c + P], ilat[:, b * TN + h * P:b * TN + (h + 1) * P]),
                        (XFB[:, (1 - b) * TN + h * P:(1 - b) * TN + (h + 1) * P],
                         ilat[:, (1 - b) * TN + h * P:(1 - b) * TN + (h + 1) * P]),
                        (QF_[:, c:c + P], sf),
                        (QB_[:, c:c + P], sbk)])
                fills(ins, ("oh", b))
            w = wait_tile(pe, ("in", 7))
            for b in range(TB):
                tokens_out(("g", b), w, hT3, b)

            for s, (x, last) in enumerate(((q3, ("q",)), (k3, ("k",)))):
                for n in range(2):
                    if s == 0:
                        wait_copied(pe, ("q", n))
                    else:
                        wait_copied(pe, ("k", 2 * n))
                        wait_copied(pe, ("k", 2 * n + 1))
                    o = pe_take(pe, ("rot", s, n))
                    for i in range(2):
                        ins = pe.matmul(o[:, i * T:(i + 1) * T], C("rotate"), x[:, 2 * n + i, 0:T],
                                        start=True, stop=True)
                    fills(ins, ("rot", s, n))
            pe.wait_ge(sem("roped"), 1)

            def da_scores(b, h):
                for i in range(2):
                    o = pe_take(pe, ("s", b, h, i))
                    fills(pe.matmul(o[:, :], qz[i][:, h * T + b * P:h * T + (b + 1) * P], k3[:, h, :],
                                    start=True, stop=True), ("s", b, h, i))

            da = [(b, h) for b in range(TB) for h in range(HEADS)]
            for b in range(2 * TB):
                wait_copied(pe, ("v", b))
            da_scores(*da[0])
            for n, (b, h) in enumerate(da):
                if n + 1 < len(da):
                    da_scores(*da[n + 1])
                pe.wait_ge(sem("a_ready"), n + 1)
                o = pe_take(pe, ("aT", b, h))
                for k in range(4):
                    ins = pe.transpose(o[:, k * P:(k + 1) * P], pbuf[2 * (n % 2)][:, k * P:(k + 1) * P], ident)
                fills(ins, ("aT", b, h))
                wait_copied(pe, ("aT", b, h))
                o = pe_take(pe, ("o", b)) if h == 0 else bank[turns[("o", b)][0]]
                ins = sum_of(o[:, h * P:(h + 1) * P],
                             [(aTb[n % 2][:, k * P:(k + 1) * P], v3[:, k, h * P:(h + 1) * P]) for k in range(4)])
                if h == HEADS - 1:
                    fills(ins, ("o", b))
            for g in (1, 2):
                modulation(0, g, "mod", "modT")
                mod_columns(g, "mod", "modT", (0, 1) if g == 1 else (2, 3), "gt")
            for g in range(3):
                modulation(1, g, "mod2", "modT2")
                mod_columns(g, "mod2", "modT2", {0: (), 1: (0, 1), 2: (2, 3)}[g], "gt2")

            for b in range(TB):
                pe.wait_ge(sem("c2_normed"), b + 1)
                for g in range(2):
                    turn_chunks(("c2T", b, g), c2[:, b, :], g)
            w = wait_tile(pe, ("kvctx",), J, KVL + ROPE)
            pe.wait_ge(sem("c2_ready"), 1)
            for b in range(TB):
                tokens_out(("kvc", b), w, uT, b, KVL + ROPE)
            pe.wait_ge(sem("kvc_normed"), 1)
            o = pe_take(pe, ("kvcT",))
            for b in range(TB):
                ins = pe.transpose(o[:, b * P:(b + 1) * P], kvn[:, b, 0:KVL], ident)
            fills(ins, ("kvcT",))
            o = pe_take(pe, ("kpcT",))
            for b in range(TB):
                ins = pe.transpose(o[:, b * P:(b + 1) * P], kvn2[:, b, :], ident)
            fills(ins, ("kpcT",))

            for b in range(TB):
                pe.wait_ge(sem("mix_ready"), b + 1)
                for g in range(2):
                    turn_chunks(("mixT", b, g), mix[:, b, :], g)
            for b in range(TB):
                for g in range(2):
                    wait_copied(pe, ("mixT", b, g))
            for n in range(2):
                w = wait_tile(pe, ("out", n))
                for b in range(TB):
                    tokens_out(("y", b, n), w, mixT, b)

            for b in range(TB):
                pe.wait_ge(sem("x1_normed"), b + 1)
                for g in range(2):
                    turn_chunks(("x1T", b, g), xn[:, b, :], g)
            pe.wait_ge(sem("h2_ready"), 1)
            pe.wait_ge(sem("router_in"), 16)
            for b in range(TB):
                o = pe_take(pe, ("logit", b))
                fills(sum_of(o[:, 0:E], [(h2T[:, j, b * P:(b + 1) * P], router[:, j, :]) for j in range(J)]),
                      ("logit", b))
            pe.wait_ge(sem("aff_ready"), 1)
            o = pe_take(pe, ("affT",))
            for b in range(TB):
                ins = pe.transpose(o[0:E, b * P:(b + 1) * P], aff[:, b, :], ident)
            fills(ins, ("affT",))
            pe.wait_ge(sem("rank_ready"), 1)
            o = pe_take(pe, ("posT",))
            for b in range(TB):
                ins = pe.transpose(o[:, b * E:(b + 1) * E], work[:, b * P:(b + 1) * P], ident[0:E, 0:E])
            fills(ins, ("posT",))
            pe.wait_ge(sem("onehot_ready"), 1)
            for j in range(J):
                o = pe_take(pe, ("xin", j))
                fills(sum_of(o[:, :], [(xn[:, b, j * P:(j + 1) * P], onehot2[:, b, :]) for b in range(TB)]),
                      ("xin", j))
            pe.wait_ge(sem("weighted_ready"), 1)
            for e in range(0, E, 2):
                o = pe_take(pe, ("ST", e))
                for i in range(2):
                    for b in range(TB):
                        for q in range(4):
                            ins = pe.matmul(o[32 * q:32 * q + 32, (2 * i + b) * P:(2 * i + b + 1) * P],
                                            weighted[:, b, e + i, :], ident, start=True, stop=True)
                fills(ins, ("ST", e))

            pe.wait_ge(sem("zeros_set"), 1)
            for k in range(4):
                pe_take(pe, ("f", k // 2, k % 2))
                ins = pe.matmul(bank[4 + k][:, :], zeros[:, 0:P], zeros[:, P:P + TN], start=True, stop=False)
            ins.then_inc(sem("scattered"), 1)

            def expert(e, last):
                pe.wait_ge(sem("tokens"), e + 1)
                for s in range(4):
                    pe.wait_ge(landed[s], (e + (expert_turn0[s] + 1)) * 16)
                pe.wait_ge(freed[0], e + exp_base[0])
                w = [slot_view(s, J, TN) for s in range(SLOTS)]
                for j in range(J):
                    for t in range(4):
                        ins = pe.matmul(bank[0][32 * t:32 * t + 32, :], xin_cur[:, j, :], w[t][:, j, :],
                                        start=j == 0, stop=j == J - 1)
                ins.then_inc(filled[0], 1)
                pe.wait_ge(freed[0], e + (exp_base[0] + 1))
                pe.wait_ge(freed[1], e + exp_base[1])
                for k in range(4):
                    ins = pe.transpose(bank[1][:, k * P:(k + 1) * P], hidden_rows[:, k * P:(k + 1) * P], ident)
                ins.then_inc(filled[1], 1)
                pe.wait_ge(freed[1], e + (exp_base[1] + 1))
                for n in range(2):
                    pe.wait_ge(landed[4 + n], (e + (expert_turn0[4 + n] + 1)) * 16)
                    pe.wait_ge(freed[2 + n], e + exp_base[2 + n])
                    for c in range(2):
                        for q in range(4):
                            k = 2 * q + c
                            ins = pe.matmul(bank[2 + n][32 * q:32 * q + 32, :],
                                            hmT[:, k % 4, 32 * (k // 4):32 * (k // 4) + 32], w[4 + n][:, k, :],
                                            start=c == 0, stop=c == 1)
                    ins.then_inc(filled[2 + n], 1)
                pe.wait_ge(sem("scatter_matrix"), e + 1)
                for n in range(2):
                    pe.wait_ge(freed[2 + n], e + (exp_base[2 + n] + 1))
                for n in range(2):
                    for b in range(TB):
                        ins = pe.matmul(bank[4 + 2 * b + n][:, :], s_cur[:, b * P:(b + 1) * P], yb[n],
                                        start=False, stop=last)
                        if last:
                            fills(ins, ("f", b, n))
                if not last:
                    ins.then_inc(sem("scattered"), 1)

            with pe.Fori(0, E - 1) as e:
                expert(e, False)
            expert(E - 1, True)

            for b in range(TB):
                pe.wait_ge(sem("x2_normed"), b + 1)
                for g in range(2):
                    turn_chunks(("x2T", b, g), xn[:, b, :], g)
            w = wait_tile(pe, ("min", 0), J, 448)
            pe.wait_ge(sem("u2_ready"), 1)
            for b in range(TB):
                tokens_out(("pa", b), w, u2T, b, 448)
            pe.wait_ge(sem("lat_normed"), 1)
            o = pe_take(pe, ("cqT",))
            for c in range(2):
                for b in range(TB):
                    ins = pe.transpose(o[:, c * T + b * P:c * T + (b + 1) * P], cqn[:, b, c * P:(c + 1) * P], ident)
            fills(ins, ("cqT",))
            o = pe_take(pe, ("ckT",))
            for b in range(TB):
                pe.transpose(o[:, b * P:(b + 1) * P], kvl[:, b, 0:KVL], ident)
            for b in range(TB):
                ins = pe.transpose(o[:, T + b * P:T + (b + 1) * P], kpl[:, b, :], ident)
            fills(ins, ("ckT",))
            wq = wait_tile(pe, ("qup",), 2, MH * (NOPE + ROPE))
            wkv = wait_tile(pe, ("kvup",), 1, MH * (NOPE + KVL))
            pe.wait_ge(sem("latT_ready"), 1)
            HW = NOPE + ROPE
            for m in range(MH // 2):
                o = pe_take(pe, ("qn", m))
                for i in range(2):
                    h = 2 * m + i
                    ins = sum_of(o[:, i * T:(i + 1) * T],
                                 [(wq[:, c, h * HW:h * HW + NOPE], cqT[:, c, :]) for c in range(2)])
                fills(ins, ("qn", m))
            wqh = wq.rearrange("p c (h w) -> p c h w", w=HW)
            for m in range(MH // 2):
                o = pe_take(pe, ("qr", m))
                for i in range(2):
                    ins = sum_of(o[64 * i:64 * i + 64, 0:T],
                                 [(wqh[:, c, 2 * m + i, NOPE:HW], cqT[:, c, :]) for c in range(2)])
                fills(ins, ("qr", m))
            for m in range(MH // 2):
                wait_copied(pe, ("qr", m))
                o = pe_take(pe, ("qrot", m))
                fills(pe.matmul(o[:, 0:T], C("rotate"), qraw[:, m * T:(m + 1) * T], start=True, stop=True),
                      ("qrot", m))
            o = pe_take(pe, ("krot",))
            fills(pe.matmul(o[:, 0:T], C("rotate"), kp_all[:, 0:T], start=True, stop=True), ("krot",))
            for h in range(MH):
                o = pe_take(pe, ("kn", h))
                fills(pe.matmul(o[:, :], wkv[:, 0, h * 2 * P:h * 2 * P + P], ckv_all, start=True, stop=True),
                      ("kn", h))
            wvh = wkv.rearrange("p j (h w) -> p (j h) w", w=2 * P)
            for b in range(2 * TB):
                for g in range(2):
                    o = pe_take(pe, ("v2", b, g))
                    fills(pe.matmul(o[:, :], ckv_all[:, b * P:(b + 1) * P], wvh[:, 4 * g:4 * g + 4, P:2 * P],
                                    start=True, stop=True), ("v2", b, g))
            lat2 = [u2T[:, j, :] for j in range(J)]
            for m in range(MH // 2):
                w = wait_tile(pe, ("min", 1 + m // 2))
                heads_out(("g2", m), w, (2 * (m % 2), 2 * (m % 2) + 1), lat2, T)
            pe.wait_ge(sem("qk2_ready"), 1)
            for m in range(MH // 2):
                wait_copied(pe, ("qn", m))

            def mla_scores(h, b):
                if b == 0:
                    wait_copied(pe, ("kn", h))
                o = pe_take(pe, ("s2", h, b))
                fills(sum_of(o[:, :], [(qnT[:, h, b * P:(b + 1) * P], knT[:, h, :]),
                                       (qrz[:, h, b * P:(b + 1) * P], kp_all)]), ("s2", h, b))

            ml = [(h, b) for h in range(MH) for b in range(TB)]
            mla_scores(*ml[0])
            for b in range(2 * TB):
                for g in range(2):
                    wait_copied(pe, ("v2", b, g))
            for n, (h, b) in enumerate(ml):
                if n + 1 < len(ml):
                    mla_scores(*ml[n + 1])
                pe.wait_ge(sem("p2_ready"), n + 1)
                o = pe_take(pe, ("pT", h, b))
                for k in range(4):
                    ins = pe.transpose(o[:, k * P:(k + 1) * P], p2[n % 2][:, k * P:(k + 1) * P], ident)
                fills(ins, ("pT", h, b))
                if b == TB - 1:
                    wait_copied(pe, ("pT", h, 0))
                    wait_copied(pe, ("pT", h, 1))
                    o = pe_take(pe, ("o2", h))
                    fills(sum_of(o[:, 0:T], [(v2[:, k, h * P:(h + 1) * P], pTs[h % 2][:, k, :]) for k in range(4)]),
                          ("o2", h))
            for h in range(MH):
                wait_copied(pe, ("o2", h))
            for n in range(2):
                w = wait_tile(pe, ("mout", n))
                for b in range(TB):
                    tokens_out(("y2", b, n), w, oT, b)

            for b in range(TB):
                pe.wait_ge(sem("x3_normed"), b + 1)
                for g in range(2):
                    turn_chunks(("x3T", b, g), xn[:, b, :], g)
            pe.wait_ge(sem("u3_ready"), 1)
            for n in range(2):
                w = wait_tile(pe, ("fin", n))
                for b in range(TB):
                    tokens_out(("fz", b, n), w, u2T, b)
            for m in range(MH // 2):
                w = wait_tile(pe, ("fin", 2 + m // 2))
                heads_out(("fg", m), w, (2 * (m % 2), 2 * (m % 2) + 1), lat2, T)
            for b in range(TB):
                for n in range(2):
                    wait_copied(pe, ("fz", b, n))
            pe.wait_ge(sem("fft_in"), 16)
            for g in range(8):
                o = pe_take(pe, ("fa", g))
                fills(sum_of(o[:, :], [(z3[:, b, g * P:(g + 1) * P], fft[:, b * TN:(b + 1) * TN])
                                       for b in range(TB)]), ("fa", g))
                if g % 2:
                    m = g // 2
                    wait_copied(pe, ("fa", g - 1))
                    wait_copied(pe, ("fa", g))
                    o = pe_take(pe, ("fb", m))
                    for i in range(2):
                        x = faT[(g - 1 + i) % 4]
                        ins = sum_of(o[:, i * T:(i + 1) * T], [(fft[:, 2 * TN:2 * TN + P], x[:, 0:T]),
                                                               (fft[:, 2 * TN + P:2 * TN + 2 * P], x[:, T:2 * T])])
                    fills(ins, ("fb", m))
            for m in range(4):
                wait_copied(pe, ("fb", m))
            for n in range(2):
                w = wait_tile(pe, ("fout", n))
                for b in range(TB):
                    tokens_out(("y3", b, n), w, oT3, b)

        @block.scalar
        def _(act):
            st = Steps(act, sem("act_step"), reached)

            def root_inverse(c0, n, width, signal, pairs=False):
                st.settle()
                if pairs:
                    for i in range(n):
                        st.did(act.activation(ssq[:, c0 + i:c0 + i + 1], ssq[:, c0 + 2 * i:c0 + 2 * i + 1],
                                              ACT.Identity, bias=ssq[:, c0 + 2 * i + 1:c0 + 2 * i + 2]))
                        st.settle()
                st.did(act.activation(lnb[:, c0:c0 + n], ssq[:, c0:c0 + n], ACT.Ln, bias=epsc, scale=1.0 / width))
                st.settle()
                st.did(act.activation(rr[:, c0:c0 + n], lnb[:, c0:c0 + n], ACT.Exp, scale=-0.5), sem(signal))

            def square(src, c, n=None):
                n = n or src.shape[1]
                st.did(act.activation(junk[:, 0:n], src, ACT.Square, accum_out=ssq[:, c:c + 1]))
                st.settle()

            act.wait_ge(sem("eps_set"), 1)
            wait_copied(act, "rows")
            st.did(act.activation(ecol[:, 0:32], cols[:, 0:32], ACT.Exp, scale=-1.0), sem("exp_c"))
            st.settle()
            for s, (x, name) in enumerate(((xr3, "x_in"), (cx3, "ctx_in"))):
                act.wait_ge(sem(name), 16)
                for b in range(TB):
                    square(x[:, b, :], 2 * s + b)
                root_inverse(2 * s, 2, D, "rstd_in")
            act.wait_ge(sem("lb_shift"), 1)
            st.did(act.activation(lbt[:, 0:16], lbt[:, 0:16], ACT.Exp), sem("lb_exp"))
            act.wait_ge(sem("lbrow_shift"), 1)
            for l in range(2):
                st.did(act.activation(lbrow[l][:, :], lbrow[l][:, :], ACT.Exp), sem("lbrow_exp"))
            act.wait_ge(sem("lam_dot"), 1)
            st.did(act.activation(cf[:, 0:2], cf[:, 0:2], ACT.Exp), sem("lam_exp"))
            for s in range(2):
                for b in range(TB):
                    o = wait_filled(act, ("xT", s, b, 0))
                    frees(st, act.activation(hT3[:, 0:4, s * T + b * P:s * T + (b + 1) * P],
                                             o[:, :].rearrange("p (j t) -> p j t", j=4), ACT.Copy), ("xT", s, b, 0))
            act.wait_ge(sem("mc_ready"), 1)
            wait_copied(act, ("xT", 1, 1, 1))
            st.settle()
            for j in range(J):
                ins = act.activation(hT3[:, j, T:2 * T], hT3[:, j, T:2 * T], ACT.Identity,
                                     bias=mc[:, MIXC, 0, j:j + 1], scale=mc[:, MIXC, 1, j:j + 1])
                st.did(ins, sem("hTc_ready")) if j == J - 1 else st.did(ins)

            for d in range(2):
                for hp in range(2):
                    o = wait_filled(act, ("z", d, hp))
                    frees(st, act.activation(kg[d][:, hp * TN:(hp + 1) * TN], o[:, :], ACT.Exp, scale=-1.0),
                          ("z", d, hp))
                for b in range(TB):
                    o = wait_filled(act, ("zc", d, b))
                    frees(st, act.activation(kc[d][:, b * TN:(b + 1) * TN], o[:, :], ACT.Exp, scale=-1.0),
                          ("zc", d, b))
                act.wait_ge(sem("f_ready"), d + 1)
                st.did(act.activation(ebuf[d], kg[d], ACT.Ln), sem("lf_ready"))
                act.wait_ge(sem("fc_ready"), d + 1)
                st.did(act.activation(lfc[d], kc[d], ACT.Ln), sem("lfc_ready"))
            for hp in range(2):
                o = wait_filled(act, ("hq", hp))
                frees(st, act.activation(qh[:, hp * TN:(hp + 1) * TN], o[:, :], ACT.Copy), ("hq", hp))
            for d in range(2):
                for b in range(TB):
                    o = wait_filled(act, ("dsum", d, b))
                    frees(st, act.activation(kd[d][:, b * TN:(b + 1) * TN], o[:, :], ACT.Exp), ("dsum", d, b))
            for b in range(2 * TB):
                o = wait_filled(act, ("i", b))
                dst = (ilat if b < TB else ictx)[:, (b % TB) * TN:(b % TB + 1) * TN]
                frees(st, act.activation(dst, o[:, :], ACT.Copy), ("i", b))
            for d in range(2):
                o = wait_filled(act, ("S", d))
                frees(st, act.activation(state[:, d * TN:(d + 1) * TN], o[:, :], ACT.Copy), ("S", d))

            def decays(lo, hi):
                for k in range(lo, hi):
                    act.wait_ge(sem("distance"), k + 1)
                    st.did(act.activation(ebuf[k % 2], ebuf[k % 2], ACT.Exp), sem("decay"))

            decays(0, 4)
            for h in range(HEADS):
                o = wait_filled(act, ("k", h))
                frees(st, act.activation(k3[:, h, :], o[:, :], ACT.Copy), ("k", h))
            decays(4, 8)
            for hp in range(2):
                o = wait_filled(act, ("q", hp))
                frees(st, act.activation(qT[:, hp * TN:(hp + 1) * TN], o[:, :], ACT.Copy), ("q", hp))
            decays(8, 14)
            st.did(act.activation(QF_.rearrange("p (h t) -> p h t", t=P), Bc[0][:, :, 1:P + 1], ACT.Exp))
            kb3 = Bc[1].rearrange("p (h b) t -> p h b t", b=TB)
            kf3 = Bc[0].rearrange("p (h b) t -> p h b t", b=TB)
            st.did(act.activation(KFB[:, TN:2 * TN].rearrange("p (h t) -> p h t", t=P), kb3[:, :, 1, 0:P], ACT.Exp))
            st.did(act.activation(dec[:, 0:4], kf3[:, :, 0, P:P + 1].rearrange("p h t -> p (h t)"), ACT.Exp))
            st.did(act.activation(dec[:, 4:8], kb3[:, :, 1, P:P + 1].rearrange("p h t -> p (h t)"), ACT.Exp),
                   sem("end_decay"))
            act.wait_ge(sem("end_distance"), 1)
            st.did(act.activation(KFB[:, 0:TN], KFB[:, 0:TN], ACT.Exp))
            st.did(act.activation(QB_, QB_, ACT.Exp), sem("end_decay"))
            for b in range(2 * TB):
                o = wait_filled(act, ("v", b))
                frees(st, act.activation(v3[:, b, :], o[:, :], ACT.Copy), ("v", b))
            for d in range(2):
                o = wait_filled(act, ("cross", d))
                frees(st, act.activation(XFB[:, d * TN:(d + 1) * TN], o[:, :], ACT.Copy), ("cross", d))
            for b in range(TB):
                o = wait_filled(act, ("oh", b))
                for h in range(HEADS):
                    square(o[:, h * P:(h + 1) * P], 4 * b + h)
            root_inverse(0, 8, P, "rstd_oh")
            st.settle()
            for b in range(TB):
                o = wait_filled(act, ("g", b))
                st.did(act.activation(gb[:, b * TN:(b + 1) * TN], o[:, :], ACT.Exp, scale=-1.0), sem("gb_exp"))

            da = [(b, h) for b in range(TB) for h in range(HEADS)]

            def da_exp(n):
                b, h = da[n]
                if n >= 2:
                    wait_filled(act, ("aT",) + da[n - 2])
                for i in range(2):
                    act.wait_ge(sem("da_max"), 2 * n + i + 1)
                    o = bank[turns[("s", b, h, i)][0]]
                    c = (2 * n + i) % 4
                    frees(st, act.activation(pbuf[c], o[:, :], ACT.Exp, bias=mx[:, c:c + 1], scale=DH ** -0.5,
                                             accum_out=rs[:, c:c + 1]), ("s", b, h, i))

            da_exp(0)
            for n, (b, h) in enumerate(da):
                if n + 1 < len(da):
                    da_exp(n + 1)
                o = wait_filled(act, ("aT", b, h))
                frees(st, act.activation(aTb[n % 2], o[:, :], ACT.Copy), ("aT", b, h))
                if h == HEADS - 1:
                    if b == 0:
                        act.wait_ge(sem("oh_normed"), TB)
                    o = wait_filled(act, ("o", b))
                    for i in range(HEADS):
                        square(o[:, i * P:(i + 1) * P], 4 * b + i)
                    root_inverse(4 * b, 4, P, "rstd_o")
                    st.settle()
            act.wait_ge(sem("ctx2_in"), 16)
            act.wait_ge(sem("mix_ready"), TB)
            for b in range(TB):
                square(c2[:, b, :], b)
            root_inverse(0, 2, D, "rstd_c2")
            st.settle()
            for b in range(TB):
                for g in range(2):
                    o = wait_filled(act, ("c2T", b, g))
                    frees(st, act.activation(uT[:, 4 * g:4 * g + 4, b * P:(b + 1) * P],
                                             o[:, :].rearrange("p (j t) -> p j t", j=4), ACT.Copy), ("c2T", b, g))
            for b in range(TB):
                o = wait_filled(act, ("kvc", b))
                square(o[:, 0:KVL], b)
            root_inverse(0, 2, KVL, "rstd_kvc")
            st.settle()
            for b in range(TB):
                for g in range(2):
                    o = wait_filled(act, ("mixT", b, g))
                    frees(st, act.activation(mixT[:, 4 * g:4 * g + 4, b * P:(b + 1) * P],
                                             o[:, :].rearrange("p (j t) -> p j t", j=4), ACT.Copy), ("mixT", b, g))

            def branch_norm(tag, signal, before):
                if before is not None:
                    act.wait_ge(*before)
                for b in range(TB):
                    for n in range(2):
                        o = wait_filled(act, (tag, b, n))
                        square(o[:, :], 2 * b + n)
                st.settle()
                for b in range(TB):
                    st.did(act.activation(ssum[:, b:b + 1], ssq[:, 2 * b:2 * b + 1], ACT.Identity,
                                          bias=ssq[:, 2 * b + 1:2 * b + 2]))
                st.settle()
                st.did(act.activation(lnb[:, 0:2], ssum[:, 0:2], ACT.Ln, bias=epsc, scale=1.0 / D))
                st.settle()
                st.did(act.activation(rr[:, 0:2], lnb[:, 0:2], ACT.Exp, scale=-0.5), sem(signal))
                st.settle()

            def residual_norm(k):
                for b in range(TB):
                    act.wait_ge(sem("x_updated"), TB * k + b + 1)
                    square(xr3[:, b, :], 4 + b)
                    root_inverse(4 + b, 1, D, "rstd_x")
                    st.settle()

            def turned_out(tag, dst):
                for b in range(TB):
                    for g in range(2):
                        o = wait_filled(act, (tag, b, g))
                        frees(st, act.activation(dst[:, 4 * g:4 * g + 4, b * P:(b + 1) * P],
                                                 o[:, :].rearrange("p (j t) -> p j t", j=4), ACT.Copy), (tag, b, g))

            branch_norm("y", "rstd_y", None)
            residual_norm(0)
            turned_out("x1T", h2T)
            for b in range(TB):
                act.wait_ge(sem("logit_max"), b + 1)
                frees(st, act.activation(aff[:, b, :], bank[turns[("logit", b)][0]][:, 0:E], ACT.Exp,
                                         bias=mx[:, b:b + 1], accum_out=rs[:, b:b + 1]), ("logit", b))
            for j in range(1, J, 2):
                o = wait_filled(act, ("xin", j))
                frees(st, act.activation(xin_all[:, j, :], o[:, :], ACT.Identity, bias=mc[:, FFN, 0, j:j + 1],
                                         scale=mc[:, FFN, 1, j:j + 1]), ("xin", j))
            for e in range(0, E, 2):
                o = wait_filled(act, ("ST", e))
                frees(st, act.activation(s_all[:, e * T:(e + 2) * T], o[:, :], ACT.Copy), ("ST", e))
            with act.Fori(0, E) as e:
                act.wait_ge(filled[0], e + (exp_base[0] + 1))
                act.activation(eg, bank[0][0:64, :], ACT.Exp, scale=-1.0).then_inc(sem("gate_exp"), 1)
                act.wait_ge(filled[1], e + (exp_base[1] + 1))
                act.activation(hmT, bank[1][:, :].rearrange("p (j n) -> p j n", j=4)[:, :, 0:64], ACT.Copy)\
                   .then_inc(freed[1], 1)
                act.wait_ge(filled[2], e + (exp_base[2] + 1))
                act.activation(yb[0], bank[2][:, :], ACT.Copy).then_inc(freed[2], 1)

            branch_norm("f", "rstd_y", None)
            residual_norm(1)
            turned_out("x2T", u2T)
            for b in range(TB):
                o = wait_filled(act, ("pa", b))
                square(o[:, 0:QL], b)
                square(o[:, QL:QL + KVL], 2 + b)
            root_inverse(0, 2, QL, "rstd_lat")
            root_inverse(2, 2, KVL, "rstd_lat")
            st.settle()
            for m in range(MH // 2):
                o = wait_filled(act, ("qn", m))
                frees(st, act.activation(ctxb[:, m * TN:(m + 1) * TN], o[:, :], ACT.Copy), ("qn", m))
            for m in range(MH // 2):
                o = wait_filled(act, ("qr", m))
                frees(st, act.activation(qraw[:, m * T:(m + 1) * T], o[:, 0:T], ACT.Copy), ("qr", m))
            for h in range(MH):
                o = wait_filled(act, ("kn", h))
                frees(st, act.activation(knT[:, h, :], o[:, :], ACT.Copy), ("kn", h))
            for b in range(2 * TB):
                for g in range(2):
                    o = wait_filled(act, ("v2", b, g))
                    if g == 0:
                        frees(st, act.activation(v2[:, b, 0:TN], o[:, :], ACT.Copy), ("v2", b, g))
            for m in range(MH // 2):
                o = wait_filled(act, ("g2", m))
                st.did(act.activation(tmpb[:, m * TN:(m + 1) * TN], o[:, :], ACT.Exp, scale=-1.0), sem("g2_exp"))
            ml = [(h, b) for h in range(MH) for b in range(TB)]

            def mla_exp(n):
                if n >= 2:
                    wait_filled(act, ("pT",) + ml[n - 2])
                act.wait_ge(sem("mla_max"), n + 1)
                frees(st, act.activation(p2[n % 2], bank[turns[("s2",) + ml[n]][0]][:, :], ACT.Exp,
                                         bias=mx[:, n % 2:n % 2 + 1], scale=(NOPE + ROPE) ** -0.5,
                                         accum_out=rs[:, n % 2:n % 2 + 1]), ("s2",) + ml[n])

            mla_exp(0)
            for n, (h, b) in enumerate(ml):
                if n + 1 < len(ml):
                    mla_exp(n + 1)
                o = wait_filled(act, ("pT", h, b))
                frees(st, act.activation(pTs[h % 2][:, :, b * P:(b + 1) * P],
                                         o[:, :].rearrange("p (k t) -> p k t", k=4), ACT.Copy), ("pT", h, b))
            residual_norm(2)
            turned_out("x3T", u2T)
            for b in range(TB):
                o = wait_filled(act, ("fz", b, 0))
                frees(st, act.activation(z3[:, b, 0:TN], o[:, :], ACT.Copy), ("fz", b, 0))
            for m in range(MH // 2):
                o = wait_filled(act, ("fg", m))
                st.did(act.activation(gates[:, m * TN:(m + 1) * TN], o[:, :], ACT.Exp, scale=-1.0), sem("fg_exp"))
            for g in range(8):
                o = wait_filled(act, ("fa", g))
                frees(st, act.activation(faT[g % 4], o[:, :], ACT.Copy), ("fa", g))
            residual_norm(3)

        @block.vector
        def _(dve):
            st = Steps(dve, sem("dve_step"), reached)

            def step(ins, signal=None):
                st.did(ins, sem(signal) if signal else None)

            def sigmoid_in_place(x, steps=2):
                step(dve.tensor_scalar(x, x, 1.0, None, ALU.add))
                st.settle()
                step(dve.reciprocal(x, x))
                st.settle()

            st_eps = dve.memset(epsc, EPS)
            step(st_eps, "eps_set")
            step(dve.memset(act32[:, :], 0.0))
            for d in range(2):
                step(dve.memset(Bc[d][:, :, 0:1], 0.0))
            o = wait_filled(dve, "rows")
            frees(st, dve.tensor_copy(cols[:, :], o[:, 0:N_ROWS]), "rows")
            st.settle()
            dve.wait_ge(sem("exp_c"), 1)
            sigmoid_in_place(ecol[:, 0:32])
            for l in range(2):
                for i in range(2):
                    c0 = (2 * l + i) * J
                    ins = dve.tensor_tensor(act_cols[l][:, :, i:i + 1].rearrange("p j m -> p (j m)"),
                                            cols[:, c0:c0 + J], ecol[:, c0:c0 + J], ALU.mult)
                    step(ins, "silu_c") if (l, i) == (1, 1) else step(ins)
            for s in range(2):
                dve.wait_ge(sem("rstd_in"), s + 1)
                for b in range(TB):
                    c = 2 * s + b
                    step(dve.tensor_scalar((tm3, cx3)[s][:, b, :], (xr3, cx3)[s][:, b, :], rr[:, c:c + 1], None,
                                           ALU.mult), "normed")
            dve.wait_ge(sem("mask_in"), 16)
            step(dve.tensor_copy(masks[:, :], scr[:, 5120:5120 + N_MASK]))
            lo = colof("lower")
            step(dve.tensor_tensor(lbt[:, 16:24], lo[:, 0:8], lo[:, 8:16], ALU.max))
            st.settle()
            step(dve.tensor_tensor(lbt[:, 0:8], lo[:, 0:8], lbt[:, 16:24], ALU.subtract))
            step(dve.tensor_tensor(lbt[:, 8:16], lo[:, 8:16], lbt[:, 16:24], ALU.subtract), "lb_shift")
            dve.wait_ge(sem("side_in"), 16 * 8)
            mrow = gates[:, 0:1024]
            step(dve.tensor_tensor(mrow, lbrow[0][:, :], lbrow[1][:, :], ALU.max))
            st.settle()
            for l in range(2):
                step(dve.tensor_tensor(lbrow[l][:, :], lbrow[l][:, :], mrow, ALU.subtract),
                     "lbrow_shift" if l else None)
            for i in range(2):
                step(dve.tensor_tensor(lamrow[:, 2 * i * DH:(2 * i + 1) * DH], lamrow[:, 2 * i * DH:(2 * i + 1) * DH],
                                       lamrow[:, (2 * i + 1) * DH:(2 * i + 2) * DH], ALU.mult))
            st.settle()
            for i in range(2):
                step(dve.tensor_reduce(cf[:, i:i + 1], lamrow[:, 2 * i * DH:(2 * i + 1) * DH], AX, ALU.add),
                     "lam_dot" if i else None)
            dve.wait_ge(sem("lb_exp"), 1)
            step(dve.tensor_tensor(lbt[:, 16:24], lbt[:, 0:8], lbt[:, 8:16], ALU.add))
            st.settle()
            step(dve.reciprocal(lbt[:, 16:24], lbt[:, 16:24]))
            st.settle()
            step(dve.tensor_tensor(lbc, lbt[:, 0:8], lbt[:, 16:24], ALU.mult))
            st.settle()
            step(dve.tensor_scalar(omlb, lbc, -1.0, 1.0, ALU.mult, ALU.add))
            dve.wait_ge(sem("lbrow_exp"), 2)
            step(dve.tensor_tensor(mrow, lbrow[0][:, :], lbrow[1][:, :], ALU.add))
            st.settle()
            step(dve.reciprocal(mrow, mrow))
            st.settle()
            step(dve.tensor_tensor(lbrow[0][:, :], lbrow[0][:, :], mrow, ALU.mult))
            st.settle()
            step(dve.tensor_scalar(lbrow[1][:, :], lbrow[0][:, :], -1.0, 1.0, ALU.mult, ALU.add))
            dve.wait_ge(sem("lam_exp"), 1)
            step(dve.tensor_tensor(cf[:, 2:3], cf[:, 0:1], cf[:, 1:2], ALU.subtract))
            st.settle()
            step(dve.tensor_scalar(lamc, cf[:, 2:3], -1.0, -LAMBDA_INIT, ALU.mult, ALU.add))
            step(dve.tensor_scalar(subln[:, :], subln[:, :], 1.0 - LAMBDA_INIT, None, ALU.mult))
            for s in range(2):
                for b in range(TB):
                    o = wait_filled(dve, ("xT", s, b, 1))
                    frees(st, dve.tensor_copy(hT3[:, 4:8, s * T + b * P:s * T + (b + 1) * P],
                                              o[:, :].rearrange("p (j t) -> p j t", j=4)), ("xT", s, b, 1))

            def mod_rows(tag, g, bias):
                dve.wait_ge(sem(bias), 64)
                o = wait_filled(dve, (tag, g))
                frees(st, dve.tensor_tensor(modb[:, :], o[:, :], modb[:, :], ALU.add), (tag, g))

            def mod_cols(tag, g, picks):
                o = wait_filled(dve, (tag, g))
                v = o[:, :].rearrange("p (j t m) -> p t j m", j=4, t=4)
                for i, (s, k, t, n, r) in enumerate(picks):
                    ins = dve.tensor_copy(modc[:, (2 * s + k) * J:(2 * s + k) * J + 4 * n].rearrange(
                        "p (t j) -> p t j", j=4), v[:, t:t + n, :, r])
                    if i == len(picks) - 1:
                        frees(st, ins, (tag, g))
                    else:
                        step(ins)
                if not picks:
                    frees(st, dve.memset(epsc, EPS), (tag, g))
                st.settle()

            def fold(s, norm, signal):
                step(dve.scalar_tensor_tensor(mc[:, s, 1, :], mc[:, s, 1, :], 1.0, norm, ALU.add, ALU.mult), signal)
                st.settle()

            mod_rows("mod", 0, "bias0")
            mod_cols("modT", 0, [(MIX, 0, 0, 4, 0), (MIXC, 0, 0, 4, 1)])
            fold(MIX, colof("pre_mix"), None)
            fold(MIXC, colof("pre_mix"), "mc_ready")
            wait_copied(dve, ("xT", 0, 1, 0))
            for j in range(J):
                step(dve.tensor_scalar(hT3[:, j, 0:T], hT3[:, j, 0:T], mc[:, MIX, 1, j:j + 1], mc[:, MIX, 0, j:j + 1],
                                       ALU.mult, ALU.add))
            dve.wait_ge(sem("hTc_ready"), 1)
            step(dve.memset(cf[:, 8:9], 0.0), "hT_ready")

            for d in range(2):
                wait_copied(dve, ("z", d, 0))
                wait_copied(dve, ("z", d, 1))
                sigmoid_in_place(kg[d])
                for h in range(HEADS):
                    c = 4 * d + h
                    step(dve.tensor_scalar(kg[d][:, h * T:(h + 1) * T], kg[d][:, h * T:(h + 1) * T],
                                           omlb[:, c:c + 1], lbc[:, c:c + 1], ALU.mult, ALU.add),
                         "f_ready" if h == HEADS - 1 else None)
                wait_copied(dve, ("zc", d, 0))
                wait_copied(dve, ("zc", d, 1))
                sigmoid_in_place(kc[d])
                kc3 = kc[d].rearrange("p (b n) -> p b n", b=TB)
                for l in (1, 0):
                    r = lbrow[l][:, d * TN:(d + 1) * TN].rearrange("p (a n) -> p a n", a=1).broadcast_to([P, TB, TN])
                    step(dve.tensor_tensor(kc3, kc3, r, ALU.mult if l else ALU.add), None if l else "fc_ready")
                    st.settle()
                dve.wait_ge(sem("lf_ready"), d + 1)
                step(dve.tensor_scalar(kg[d], kg[d], -1.0, 1.0, ALU.mult, ALU.add))
                for hb in range(2 * HEADS):
                    step(dve.tensor_tensor_scan(Bc[d][:, hb, 1:P + 1], C("ones"), ebuf[d][:, hb * P:(hb + 1) * P],
                                                0.0, ALU.mult, ALU.add))
                dve.wait_ge(sem("lfc_ready"), d + 1)
                step(dve.tensor_scalar(kc[d], kc[d], -1.0, 1.0, ALU.mult, ALU.add))
            st.settle()
            for d in range(2):
                wait_copied(dve, ("dsum", d, 0))
                wait_copied(dve, ("dsum", d, 1))
                step(dve.tensor_tensor(kd[d], kd[d], kc[d], ALU.mult), "kd_ready")

            def halves(ap, L):
                return ap.rearrange("p (n x l) -> p n x l", x=2, l=L)

            def distance(k):
                i, d = divmod(k, 2)
                L = LEVELS[i]
                nb = P // (2 * L)
                e = ebuf[k % 2].rearrange("p (h n x l) -> p h n x l", h=2 * HEADS, x=2, l=L)
                shift = Bc[d][:, :, 1 - d:P + 1 - d].rearrange("p h (n x l) -> p h n x l", x=2, l=L)
                mid = Bc[d][:, :, 0:P].rearrange("p h (n x l) -> p h n x l", x=2, l=L)[:, :, :, 1, 0:1]\
                    .broadcast_to([P, 2 * HEADS, nb, L])
                step(dve.tensor_tensor(e[:, :, :, 0, :], mid, shift[:, :, :, 0, :], ALU.subtract))
                step(dve.tensor_tensor(e[:, :, :, 1, :], shift[:, :, :, 1, :], mid, ALU.subtract), "distance")

            def decayed(k):
                i, d = divmod(k, 2)
                L = LEVELS[i]
                dve.wait_ge(sem("decay"), k + 1)
                if k >= 3:
                    wait_filled(dve, ("lv", (k - 3) // 2, (k - 3) % 2, 1))
                x, e = halves(xbuf[k % 3], L), halves(ebuf[k % 2], L)
                kk, qq = halves(kg[d], L), halves(qh[:, :], L)
                first, second = (kk, qq) if d == 0 else (qq, kk)
                step(dve.tensor_tensor(x[:, :, 0, :], e[:, :, 0, :], first[:, :, 0, :], ALU.mult))
                step(dve.tensor_tensor(x[:, :, 1, :], e[:, :, 1, :], second[:, :, 1, :], ALU.mult), "x_ready")
                st.settle()

            def take(i, d, m):
                for g in range(2):
                    o = wait_filled(dve, ("lv", i, d, g))
                    st.settle()
                    mk = masks[:, m * P:(m + 1) * P].rearrange("p (a n) -> p a n", a=1).broadcast_to([P, 4, P])
                    frees(st, dve.copy_predicated(smat[:, g * TN:(g + 1) * TN].rearrange("p (a n) -> p a n", a=4),
                                                  mk, o[:, :].rearrange("p (a n) -> p a n", a=4)), ("lv", i, d, g))

            wait_copied(dve, ("hq", 1))
            step(dve.memset(smat[:, :], 0.0))
            n_lv = 2 * len(LEVELS)
            distance(0)
            for k in range(n_lv):
                if k + 1 < n_lv:
                    distance(k + 1)
                decayed(k)
                if k:
                    take(*divmod(k - 1, 2), k - 1)
            wait_filled(dve, ("lv", (n_lv - 3) // 2, (n_lv - 3) % 2, 1))
            step(dve.tensor_tensor(xbuf[n_lv % 3], kg[0], kg[1], ALU.add), "x_ready")
            take(*divmod(n_lv - 1, 2), n_lv - 1)
            take(len(LEVELS), 0, n_lv)
            kf3 = Bc[0].rearrange("p (h b) t -> p h b t", b=TB)
            step(dve.tensor_tensor(KFB[:, 0:TN].rearrange("p (h t) -> p h t", t=P),
                                   kf3[:, :, 0, P:P + 1].broadcast_to([P, HEADS, P]), kf3[:, :, 0, 1:P + 1],
                                   ALU.subtract))
            step(dve.tensor_tensor(QB_.rearrange("p (h t) -> p h t", t=P),
                                   Bc[1][:, :, P:P + 1].broadcast_to([P, 2 * HEADS, P]), Bc[1][:, :, 0:P],
                                   ALU.subtract), "end_distance")
            kgb = [kg[d].rearrange("p (h b t) -> p h b t", b=TB, t=P) for d in range(2)]
            kfb = KFB.rearrange("p (d h t) -> p d h t", d=2, t=P)
            dve.wait_ge(sem("end_decay"), 2)
            step(dve.tensor_tensor(QF_, QF_, qh[:, :], ALU.mult))
            step(dve.tensor_tensor(kfb[:, 1], kfb[:, 1], kgb[1][:, :, 1, :], ALU.mult))
            step(dve.tensor_tensor(kfb[:, 0], kfb[:, 0], kgb[0][:, :, 0, :], ALU.mult))
            step(dve.tensor_tensor(QB_, QB_, qh[:, :], ALU.mult), "cross_ready")
            for d in range(2):
                wait_copied(dve, ("S", d))
                step(dve.tensor_tensor(state1[:, d * TN:(d + 1) * TN].rearrange("p (h t) -> p h t", t=P),
                                       state[:, d * TN:(d + 1) * TN].rearrange("p (h t) -> p h t", t=P),
                                       dec[:, 4 * d:4 * d + 4].rearrange("p (h t) -> p h t", t=1)
                                       .broadcast_to([P, HEADS, P]), ALU.mult), "state1_ready" if d else None)
            dve.wait_ge(sem("rstd_oh"), 1)
            for b in range(TB):
                o = wait_filled(dve, ("oh", b))
                for h in range(HEADS):
                    ins = dve.scalar_tensor_tensor(mix[:, b, TN + h * P:TN + (h + 1) * P], o[:, h * P:(h + 1) * P],
                                                   rr[:, 4 * b + h:4 * b + h + 1], hgn[:, :], ALU.mult, ALU.mult)
                    frees(st, ins, ("oh", b)) if h == HEADS - 1 else step(ins)
            for b in range(TB):
                dve.wait_ge(sem("gb_exp"), b + 1)
                g_ = gb[:, b * TN:(b + 1) * TN]
                sigmoid_in_place(g_)
                o = bank[turns[("g", b)][0]]
                frees(st, dve.tensor_tensor(g_, g_, o[:, :], ALU.mult), ("g", b))
                st.settle()
                step(dve.tensor_tensor(mix[:, b, TN:2 * TN], mix[:, b, TN:2 * TN], g_, ALU.mult), "oh_normed")
            step(dve.memset(cf[:, 8:9], 0.0), "scratch_done")

            step(dve.memset(qh[64:P, :], 0.0))
            step(dve.memset(smat[0:64, :], 0.0))
            cosb = C("cos").rearrange("p (a t) -> p a t", a=1).broadcast_to([P, HEADS, T])
            sin2 = C("sin").rearrange("p (a t) -> p a t", a=1).broadcast_to([P, 2, T])
            for s, (x, tag) in enumerate(((q3, "q"), (k3, "k"))):
                for n in range(2):
                    o = wait_filled(dve, ("rot", s, n))
                    frees(st, dve.tensor_tensor(rtmp[:, n * TN:(n + 1) * TN].rearrange("p (a t) -> p a t", a=2),
                                                o[:, :].rearrange("p (a t) -> p a t", a=2), sin2, ALU.mult),
                          ("rot", s, n))
                step(dve.tensor_tensor(x[:, :, 0:T], x[:, :, 0:T], cosb, ALU.mult))
                st.settle()
                r3 = rtmp.rearrange("p (a t) -> p a t", a=HEADS)
                if s == 0:
                    for i in range(2):
                        ps = slice(64 * i, 64 * i + 64)
                        step(dve.tensor_tensor(qz[i][ps, :].rearrange("p (a t) -> p a t", a=HEADS),
                                               x[ps, :, 0:T], r3[ps], ALU.add))
                    st.settle()
                else:
                    step(dve.tensor_tensor(x[:, :, 0:T], x[:, :, 0:T], r3, ALU.add), "roped")
            da = [(b, h) for b in range(TB) for h in range(HEADS)]

            def da_max(n):
                for i in range(2):
                    o = wait_filled(dve, ("s",) + da[n] + (i,))
                    c = (2 * n + i) % 4
                    step(dve.tensor_reduce(mx[:, 4 + c:5 + c], o[:, :], AX, ALU.max))
                    st.settle()
                    step(dve.tensor_scalar(mx[:, c:c + 1], mx[:, 4 + c:5 + c], -DH ** -0.5, None, ALU.mult), "da_max")

            da_max(0)
            for n, (b, h) in enumerate(da):
                if n + 1 < len(da):
                    da_max(n + 1)
                wait_copied(dve, ("s", b, h, 0))
                wait_copied(dve, ("s", b, h, 1))
                c = (2 * n) % 4
                step(dve.reciprocal(cf[:, c:c + 2], rs[:, c:c + 2]))
                st.settle()
                step(dve.tensor_tensor(cf[:, 4 + c:5 + c], cf[:, c + 1:c + 2], lamc, ALU.mult))
                st.settle()
                step(dve.tensor_scalar(pbuf[c + 1], pbuf[c + 1], cf[:, 4 + c:5 + c], None, ALU.mult))
                st.settle()
                step(dve.scalar_tensor_tensor(pbuf[c], pbuf[c], cf[:, c:c + 1], pbuf[c + 1], ALU.mult, ALU.add),
                     "a_ready")
                if h == HEADS - 1:
                    dve.wait_ge(sem("rstd_o"), b + 1)
                    o = bank[turns[("o", b)][0]]
                    for i in range(HEADS):
                        ins = dve.scalar_tensor_tensor(mix[:, b, i * P:(i + 1) * P], o[:, i * P:(i + 1) * P],
                                                       rr[:, 4 * b + i:4 * b + i + 1], subln[:, :], ALU.mult, ALU.mult)
                        frees(st, ins, ("o", b)) if i == HEADS - 1 else step(ins)
                    st.settle()
                    step(dve.memset(cf[:, 8:9], 0.0), "mix_ready")

            dve.wait_ge(sem("post_in"), 32)

            def gate_rows(tagG, g, t, i, n):
                o = wait_filled(dve, (tagG, g, t))
                dst = G[i][:, n * TN:(n + 1) * TN]
                ins = dve.tensor_tensor(dst, o[:, :], dst, ALU.mult) if i < 2 else dve.tensor_copy(dst, o[:, :])
                frees(st, ins, (tagG, g, t))

            mod_rows("mod", 1, "bias1")
            mod_cols("modT", 1, [(FFN, 0, 2, 2, 0)])
            for t in range(2):
                gate_rows("gt", 1, t, 0, t)
            mod_rows("mod", 2, "bias2")
            mod_cols("modT", 2, [(FFN, 1, 0, 2, 0)])
            for t in range(2):
                gate_rows("gt", 2, 2 + t, 1, t)
            fold(FFN, colof("pre_ffn"), None)
            ng = colof("norm_g_2")
            mod_rows("mod2", 0, "bias3")
            mod_cols("modT2", 0, [(MLA, 0, 0, 4, 0), (MLAC, 0, 0, 4, 1)])
            fold(MLA, ng[:, 0:J], None)
            fold(MLAC, ng[:, 0:J], None)
            mod_rows("mod2", 1, "bias4")
            mod_cols("modT2", 1, [(FNO, 0, 2, 2, 0)])
            for t in range(2):
                gate_rows("gt2", 1, t, 2, t)
            mod_rows("mod2", 2, "bias5")
            mod_cols("modT2", 2, [(FNO, 1, 0, 2, 0)])
            for t in range(2):
                gate_rows("gt2", 2, 2 + t, 3, t)
            fold(FNO, ng[:, J:2 * J], "folded")

            def affine(x, s, signal, n=T):
                for j in range(J):
                    step(dve.tensor_scalar(x[:, j, :], x[:, j, :], mc[:, s, 1, j:j + 1], mc[:, s, 0, j:j + 1],
                                           ALU.mult, ALU.add), signal if j == J - 1 else None)

            dve.wait_ge(sem("rstd_c2"), 1)
            for b in range(TB):
                step(dve.tensor_scalar(c2[:, b, :], c2[:, b, :], rr[:, b:b + 1], None, ALU.mult), "c2_normed")
            wait_copied(dve, ("c2T", 1, 0))
            wait_copied(dve, ("c2T", 1, 1))
            affine(uT, MLAC, "c2_ready")
            dve.wait_ge(sem("rstd_kvc"), 1)
            for b in range(TB):
                o = bank[turns[("kvc", b)][0]]
                step(dve.tensor_scalar(kvn[:, b, :], o[:, 0:KVL], rr[:, b:b + 1], None, ALU.mult))
                frees(st, dve.tensor_copy(kvn2[:, b, :].rearrange("p (a n) -> p a n", a=2),
                                          o[:, KVL:KVL + ROPE].rearrange("p (a n) -> p a n", a=1)
                                          .broadcast_to([P, 2, ROPE])), ("kvc", b))
            st.settle()
            step(dve.memset(cf[:, 8:9], 0.0), "kvc_normed")
            o = wait_filled(dve, ("kvcT",))
            frees(st, dve.tensor_scalar(ckv_ctx, o[:, 0:T], colof("g_kva"), None, ALU.mult), ("kvcT",))
            o = wait_filled(dve, ("kpcT",))
            frees(st, dve.tensor_copy(kp_ctx, o[:, 0:T]), ("kpcT",))

            step(dve.memset(hidden_rows[64:P], 0.0))

            def add_branch(tag, i, k, norm):
                if norm:
                    dve.wait_ge(sem("rstd_y"), norm)
                for b in range(TB):
                    for n in range(2):
                        o = wait_filled(dve, (tag, b, n))
                        cs = slice(n * TN, (n + 1) * TN)
                        if norm:
                            ins = dve.scalar_tensor_tensor(xn[:, b, cs], o[:, :], rr[:, b:b + 1], G[i][:, cs],
                                                           ALU.mult, ALU.mult)
                        else:
                            ins = dve.tensor_tensor(xn[:, b, cs], o[:, :], G[i][:, cs], ALU.mult)
                        frees(st, ins, (tag, b, n))
                    st.settle()
                    step(dve.tensor_tensor(xr3[:, b, :], xr3[:, b, :], xn[:, b, :], ALU.add), "x_updated")

            def normalise(k, signal):
                for b in range(TB):
                    dve.wait_ge(sem("rstd_x"), TB * k + b + 1)
                    step(dve.tensor_scalar(xn[:, b, :], xr3[:, b, :], rr[:, 4 + b:5 + b], None, ALU.mult), signal)

            def turned_in(tag, x, s, signal):
                for b in range(TB):
                    for g in range(2):
                        wait_copied(dve, (tag, b, g))
                affine(x, s, signal)

            add_branch("y", 0, 0, 1)
            normalise(0, "x1_normed")
            turned_in("x1T", h2T, FFN, "h2_ready")
            for b in range(TB):
                o = wait_filled(dve, ("logit", b))
                step(dve.tensor_reduce(mx[:, 4 + b:5 + b], o[:, 0:E], AX, ALU.max))
                st.settle()
                step(dve.tensor_scalar(mx[:, b:b + 1], mx[:, 4 + b:5 + b], -1.0, None, ALU.mult), "logit_max")
            for b in range(TB):
                wait_copied(dve, ("logit", b))
            step(dve.reciprocal(cf[:, 0:2], rs[:, 0:2]))
            st.settle()
            for b in range(TB):
                step(dve.tensor_scalar(aff[:, b, :], aff[:, b, :], cf[:, b:b + 1], None, ALU.mult),
                     "aff_ready" if b else None)
            o = wait_filled(dve, ("affT",))
            frees(st, dve.tensor_copy(affT, o[0:E, 0:T]), ("affT",))
            st.settle()
            for r in range(CAP // 8):
                src = affT if r == 0 else work
                step(dve.max(top8, src))
                st.settle()
                step(dve.match_replace(work, top8, src, -1.0))
                st.settle()
            step(dve.tensor_scalar(affT, work, 0.0, None, ALU.is_lt))
            st.settle()
            step(dve.tensor_tensor_scan(work, affT, affT, 0.0, ALU.add, ALU.max))
            st.settle()
            step(dve.tensor_tensor(work, work, affT, ALU.mult), "rank_ready")
            o = wait_filled(dve, ("posT",))
            frees(st, dve.tensor_copy(smat[:, 128:128 + TB * E], o[:, 0:TB * E]), ("posT",))
            st.settle()
            rank = C("rank").rearrange("p (a c) -> p a c", a=1).broadcast_to([P, E, CAP])
            wide = lambda x: x.rearrange("p (e c) -> p e c", c=1).broadcast_to([P, E, CAP])
            for b in range(TB):
                step(dve.tensor_tensor(onehot[:, b], wide(pos[:, b, :]), rank, ALU.is_equal),
                     "onehot_ready" if b else None)
            st.settle()
            for b in range(TB):
                step(dve.tensor_tensor(weighted[:, b], onehot[:, b], wide(aff[:, b, :]), ALU.mult),
                     "weighted_ready" if b else None)
            for j in range(0, J, 2):
                o = wait_filled(dve, ("xin", j))
                frees(st, dve.tensor_scalar(xin_all[:, j, :], o[:, :], mc[:, FFN, 1, j:j + 1],
                                            mc[:, FFN, 0, j:j + 1], ALU.mult, ALU.add), ("xin", j))
            hidden = sem("hidden_step")
            with dve.Fori(0, E) as e:
                dve.wait_ge(sem("gate_exp"), e + 1)
                dve.tensor_scalar(eg, eg, 1.0, None, ALU.add).then_inc(hidden, 1)
                dve.wait_ge(hidden, e * 3 + 1)
                dve.reciprocal(eg, eg).then_inc(hidden, 1)
                dve.wait_ge(hidden, e * 3 + 2)
                dve.tensor_tensor(eg, eg, bank[0][0:64, :], ALU.mult).then_inc(hidden, 1)
                dve.wait_ge(hidden, e * 3 + 3)
                dve.tensor_tensor(hm, eg, bank[0][64:P, :], ALU.mult).then_inc(freed[0], 1)
                dve.wait_ge(filled[3], e + (exp_base[3] + 1))
                dve.tensor_copy(yb[1], bank[3][:, :]).then_inc(freed[3], 1)

            add_branch("f", 1, 1, 2)
            normalise(1, "x2_normed")
            turned_in("x2T", u2T, MLA, "u2_ready")
            dve.wait_ge(sem("rstd_lat"), 2)
            for b in range(TB):
                o = bank[turns[("pa", b)][0]]
                step(dve.tensor_scalar(cqn[:, b, :], o[:, 0:QL], rr[:, b:b + 1], None, ALU.mult))
                step(dve.tensor_scalar(kvl[:, b, :], o[:, QL:QL + KVL], rr[:, 2 + b:3 + b], None, ALU.mult))
                frees(st, dve.tensor_copy(kpl[:, b, :].rearrange("p (a n) -> p a n", a=2),
                                          o[:, QL + KVL:448].rearrange("p (a n) -> p a n", a=1)
                                          .broadcast_to([P, 2, ROPE])), ("pa", b))
            st.settle()
            step(dve.memset(cf[:, 8:9], 0.0), "lat_normed")
            o = wait_filled(dve, ("cqT",))
            for c in range(2):
                ins = dve.tensor_scalar(cqT[:, c, :], o[:, c * T:(c + 1) * T], colof("g_qa")[:, c:c + 1], None, ALU.mult)
                frees(st, ins, ("cqT",)) if c else step(ins)
            o = wait_filled(dve, ("ckT",))
            step(dve.tensor_scalar(ckv_all[:, 0:T], o[:, 0:T], colof("g_kva"), None, ALU.mult))
            frees(st, dve.tensor_copy(kp_all[:, 0:T], o[:, T:2 * T]), ("ckT",))
            st.settle()
            step(dve.memset(vda[:, :], 0.0), "latT_ready")
            st.settle()
            cs_, sn = C("cos"), C("sin")
            for m in range(MH // 2):
                o = wait_filled(dve, ("qrot", m))
                t_ = rt[:, (m % 2) * T:(m % 2 + 1) * T]
                frees(st, dve.tensor_tensor(t_, o[:, 0:T], sn, ALU.mult), ("qrot", m))
                q_ = qraw[:, m * T:(m + 1) * T]
                step(dve.tensor_tensor(q_, q_, cs_, ALU.mult))
                st.settle()
                for i in range(2):
                    ps = slice(64 * i, 64 * i + 64)
                    step(dve.tensor_tensor(qrz[ps, 2 * m + i, :], q_[ps], t_[ps], ALU.add))
            o = wait_filled(dve, ("krot",))
            st.settle()
            frees(st, dve.tensor_tensor(rt[:, 0:T], o[:, 0:T], sn, ALU.mult), ("krot",))
            step(dve.tensor_tensor(kp_all[:, 0:T], kp_all[:, 0:T], cs_, ALU.mult))
            st.settle()
            step(dve.tensor_tensor(kp_all[:, 0:T], kp_all[:, 0:T], rt[:, 0:T], ALU.add), "qk2_ready")
            for b in range(2 * TB):
                o = wait_filled(dve, ("v2", b, 1))
                frees(st, dve.tensor_copy(v2[:, b, TN:2 * TN], o[:, :]), ("v2", b, 1))

            def silu_bank(x, name):
                sigmoid_in_place(x)
                o = bank[turns[name][0]]
                frees(st, dve.tensor_tensor(x, x, o[:, :], ALU.mult), name)

            for m in range(MH // 2):
                dve.wait_ge(sem("g2_exp"), m + 1)
                silu_bank(tmpb[:, m * TN:(m + 1) * TN], ("g2", m))
            ml = [(h, b) for h in range(MH) for b in range(TB)]

            def mla_max(n):
                o = wait_filled(dve, ("s2",) + ml[n])
                c = n % 2
                step(dve.tensor_reduce(mx[:, 4 + c:5 + c], o[:, :], AX, ALU.max))
                st.settle()
                step(dve.tensor_scalar(mx[:, c:c + 1], mx[:, 4 + c:5 + c], -(NOPE + ROPE) ** -0.5, None, ALU.mult),
                     "mla_max")

            mla_max(0)
            for n, (h, b) in enumerate(ml):
                if n + 1 < len(ml):
                    mla_max(n + 1)
                wait_copied(dve, ("s2", h, b))
                c = n % 2
                step(dve.reciprocal(cf[:, c:c + 1], rs[:, c:c + 1]))
                st.settle()
                step(dve.tensor_scalar(p2[c], p2[c], cf[:, c:c + 1], None, ALU.mult), "p2_ready")
                if b == TB - 1 and h:
                    o = wait_filled(dve, ("o2", h - 1))
                    frees(st, dve.tensor_tensor(oT[:, h - 1, :], o[:, 0:T], gT[:, h - 1, :], ALU.mult),
                          ("o2", h - 1))
            o = wait_filled(dve, ("o2", MH - 1))
            frees(st, dve.tensor_tensor(oT[:, MH - 1, :], o[:, 0:T], gT[:, MH - 1, :], ALU.mult), ("o2", MH - 1))
            st.settle()
            add_branch("y2", 2, 2, 0)
            normalise(2, "x3_normed")
            turned_in("x3T", u2T, FNO, "u3_ready")
            for b in range(TB):
                o = wait_filled(dve, ("fz", b, 1))
                frees(st, dve.tensor_copy(z3[:, b, TN:2 * TN], o[:, :]), ("fz", b, 1))
            for m in range(MH // 2):
                dve.wait_ge(sem("fg_exp"), m + 1)
                silu_bank(gates[:, m * TN:(m + 1) * TN], ("fg", m))
            st.settle()
            for m in range(4):
                o = wait_filled(dve, ("fb", m))
                frees(st, dve.tensor_tensor(gates[:, 2048 + m * TN:2048 + (m + 1) * TN], o[:, :],
                                            gates[:, m * TN:(m + 1) * TN], ALU.mult), ("fb", m))
            add_branch("y3", 3, 3, 0)
            dve.wait_ge(sem("fg_in"), 16)
            for b in range(TB):
                dve.wait_ge(sem("rstd_x"), TB * 3 + b + 1)
                step(dve.scalar_tensor_tensor(xr3[:, b, :], xr3[:, b, :], rr[:, 4 + b:5 + b], fgrow,
                                              ALU.mult, ALU.mult), "result")


_ROW_SOURCES = {"c": "c", "c_ctx": "c_ctx", "c_2": "c_2", "c_ctx_2": "c_ctx_2", "pre_mix": "norm_pre_mix",
                "pre_ffn": "norm_pre_ffn", "norm_g_2": "norm_g_2", "lower": "hg_lower_bound",
                "g_qa": "mla_g_qa_2", "g_kva": "mla_g_kva_2"}
_DIRECT = ["x", "ctx", "w_ada", "b_ada", "norm_post_mix", "norm_post_ffn", "w_in", "da_lambda_q1", "da_lambda_k1",
           "da_lambda_q2", "da_lambda_k2", "da_subln", "hg_lower_bound", "hg_norm", "w_out", "w_router", "w_gate",
           "w_up", "w_down", "ctx_2", "w_ada_2", "b_ada_2", "mla_w_in_2", "mla_w_qup_2", "mla_w_kvup_2",
           "mla_w_out_2", "fno_w_in_2", "fno_w_out_2", "final_g_2"]


def build(nc, arrays):
    a = {}
    for name, x in arrays.items():
        a[name] = nc.dram_tensor(name + "_dram", x.shape, mybir.dt.from_np(x.dtype), kind="ExternalInput").ap()
    out = nc.dram_tensor("out_dram", (1, T, D), F32, kind="ExternalOutput").ap()
    block_program(nc, a, out)


def laid_out(inputs):
    arrays = {n: np.ascontiguousarray(inputs[n]) for n in _DIRECT}
    arrays["rows"] = np.concatenate([np.asarray(inputs[_ROW_SOURCES[n]]).reshape(-1, P) for n in ROWS])
    arrays["const"], arrays["mask"], arrays["fft"] = CONST, level_masks(), fourier_constants()
    return arrays


def kernel(**inputs):
    import concourse.bacc as bacc
    from concourse.bass_utils import run_bass_kernel_spmd

    arrays = laid_out(inputs)
    nc = bacc.Bacc("TRN2", target_bir_lowering=False, num_devices=1)
    build(nc, arrays)
    r = run_bass_kernel_spmd(nc, [{n + "_dram": x for n, x in arrays.items()}], core_ids=[0])
    return r.results[0]["out_dram"]
```

```python
from contextlib import ExitStack

import numpy as np
import concourse.bass as bass
from concourse import mybir

ALU = mybir.AluOpType
ACT = mybir.ActivationFunctionType
F32 = mybir.dt.float32
U8 = mybir.dt.uint8
AX = mybir.AxisListType.X

P = 128
D = 1024
J = D // P
T = 256
TB = T // P
TN = 512
HEADS = 4
DH = 64
E = 16
CAP = 2 * T // E
LAMBDA_INIT = 0.8 - 0.6 * float(np.exp(0.0))
EPS = 1e-6
LEVELS = [64, 32, 16, 8, 4, 2, 1]
MH = 8
NOPE, ROPE, QL, KVL = 128, 64, 256, 128
SLOTS = 6
LATE_SLOTS = 5
EARLY_SLOTS = 4
SLOT = J * TN


def f32_constants():
    s = np.arange(P)
    out, at = [], {}

    def put(name, a):
        a = np.asarray(a, np.float32).reshape(P, -1)
        at[name] = (sum(x.shape[1] for x in out), a.shape[1])
        out.append(a)

    put("ident", np.eye(P))
    put("after", s[:, None] > s[None, :])
    put("before", s[:, None] < s[None, :])
    put("ones", np.ones((P, P)))
    R = np.zeros((P, P))
    for b in range(0, P, 32):
        for i in range(16):
            R[b + 16 + i, b + i] = -1.0
            R[b + i, b + 16 + i] = 1.0
    put("rotate", R)
    half = DH // 2
    inv = (1.0 / (10000.0 ** (np.arange(0, half, 2, dtype=np.float32) / np.float32(half)))).astype(np.float32)
    r, c = np.meshgrid(np.arange(T // 64, dtype=np.float32), np.arange(64, dtype=np.float32), indexing="ij")
    ar = r.reshape(-1)[:, None] * inv
    ac = c.reshape(-1)[:, None] * inv
    ang = np.concatenate([ar, ar, ac, ac], -1).T.astype(np.float32)
    put("cos", np.tile(np.cos(ang), (2, 1)))
    put("sin", np.tile(np.sin(ang), (2, 1)))
    put("sum_columns", (s % 32)[:, None] == np.arange(2)[None, :])
    put("rank", np.tile(np.arange(1, CAP + 1), (P, 1)))
    return np.concatenate(out, 1), at


def fourier_constants():
    t = np.arange(T)
    a = 2 * np.pi * ((t[:, None] * t[None, :]) % T) / T
    cs = np.concatenate([np.cos(a), np.sin(a)], 1) / np.sqrt(T)
    c = np.arange(P)
    b = 2 * np.pi * ((c[:, None] * c[None, :]) % P) / P
    return np.concatenate([cs[:P], cs[P:], np.cos(b) / np.sqrt(P), -np.sin(b) / np.sqrt(P)], 1).astype(np.float32)


def level_masks():
    s = np.arange(P)
    out = []
    for L in LEVELS:
        same = (s[:, None] // (2 * L)) == (s[None, :] // (2 * L))
        sh, rh = (s[:, None] // L) % 2, (s[None, :] // L) % 2
        out += [same & (sh == 0) & (rh == 1), same & (sh == 1) & (rh == 0)]
    out.append(np.eye(P, dtype=bool))
    return np.concatenate(out, 1).astype(np.float32)


CONST, CONST_AT = f32_constants()
N_CONST = CONST.shape[1]
N_MASK = (2 * len(LEVELS) + 1) * P

ROWS = {}
_n = 0
for _name, _k in (("c", 8), ("c_ctx", 8), ("c_2", 8), ("c_ctx_2", 8), ("pre_mix", 8), ("pre_ffn", 8),
                  ("norm_g_2", 16), ("lower", 16), ("g_qa", 2), ("g_kva", 1)):
    ROWS[_name] = (_n, _k)
    _n += _k
N_ROWS = _n
N_BIAS = 2 * 6 * J

FIRST_MODS = [0, 1, 2, 3]
COLUMN_MODS = [6, 7, 8, 9, 12, 13, 14, 15, 18, 19, 20, 21]
GATE_MODS = [4, 5, 10, 11, 16, 17, 22, 23]


class Steps:

    def __init__(self, eng, own, reached):
        self.eng, self.own, self.reached, self.last = eng, own, reached, None

    def did(self, ins, sem=None):
        s = sem or self.own
        self.reached[s.name] = self.reached.get(s.name, 0) + 1
        ins.then_inc(s, 1)
        self.last = (s, self.reached[s.name])

    def settle(self):
        self.eng.wait_ge(*self.last)


def block_program(nc, a, out):
    ctx = ExitStack()
    with ctx:
        sems = {}

        def sem(name):
            if name not in sems:
                sems[name] = ctx.enter_context(nc.semaphore(name))
            return sems[name]

        def sb(name, n, parts=P, dt=F32):
            return ctx.enter_context(nc.sbuf_tensor(name, [parts, n], dt))

        ring = sb("ring", SLOTS * SLOT)
        const = sb("const", N_CONST)
        masks = sb("masks", N_MASK, dt=U8)
        cols = sb("cols", N_ROWS)
        act32 = sb("act32", 2 * J * 32)
        modr1 = sb("modr1", TN)
        modc = sb("modc", 6 * 2 * J)
        small = sb("small", 256)
        xres = sb("xres", TB * D)
        hT = sb("hT", J * 2 * T)
        pair = sb("pair", 2 * TB * D)
        ctxb, tmpb = pair[:, 0:TB * D], pair[:, TB * D:]
        qT = sb("qT", HEADS * T)
        kT = sb("kT", HEADS * 2 * T)
        vda = sb("vda", 2 * TB * TN)
        gates = sb("gates", 2 * 1024 + 2 * 1040)
        qh = sb("qh", HEADS * T)
        ilat = sb("ilat", TB * TN)
        smat = sb("smat", HEADS * T)
        state = sb("state", 2 * TN)
        state1 = sb("state1", 2 * TN)
        lamrow = smat[:, 0:4 * DH]
        subln = sb("subln", P)
        hgn = sb("hgn", P)
        junk = sb("junk", D, dt=mybir.dt.bfloat16)
        lbrow = (state, state1)

        def C(name):
            o, n = CONST_AT[name]
            return const[:, o:o + n]

        ident = C("ident")
        bank = [ctx.enter_context(nc.psum_tensor(f"bank{b}", [P, TN], F32)) for b in range(8)]
        filled = [sem(f"filled{b}") for b in range(8)]
        freed = [sem(f"freed{b}") for b in range(8)]
        landed = [sem(f"landed{s}") for s in range(SLOTS)]
        reached = {}
        turns, used = {}, [0] * 8

        def claim(name, b):
            turns[name] = (b, used[b])
            used[b] += 1

        def pe_take(pe, name):
            b, n = turns[name]
            if n:
                pe.wait_ge(freed[b], n)
            return bank[b]

        def wait_filled(eng, name):
            b, n = turns[name]
            eng.wait_ge(filled[b], n + 1)
            return bank[b]

        def wait_copied(eng, name):
            b, n = turns[name]
            eng.wait_ge(freed[b], n + 1)

        def fills(ins, name):
            ins.then_inc(filled[turns[name][0]], 1)

        def frees(steps, ins, name):
            b, n = turns[name]
            ins.then_inc(freed[b], 1)
            steps.last = (freed[b], n + 1)

        def wtile(w, n0, n=TN):
            return w[:, n0:n0 + n].rearrange("(j p) n -> p j n", p=P)

        w_in = a["w_in"][0]
        stream = []

        def tile(name, src):
            stream.append((name, src))

        def mod_tile(i):
            l, o = divmod((i - 12) * TN, 3 * D)
            tile(("ada", i), wtile(a["w_ada"][0], i * TN) if i < 12 else wtile(a["w_ada_2"][l], o))

        for i in FIRST_MODS:
            mod_tile(i)
        order = iter(COLUMN_MODS)
        for t in (3, None, 4, None, 6, None, 5, None, None, 1, None, None, 0, None, None, None, None, 2, None, 7):
            if t is None:
                mod_tile(next(order))
            else:
                tile(("in", t), wtile(w_in, t * TN))
        for n, i in enumerate(GATE_MODS):
            if n == 4:
                tile(("kvctx",), wtile(a["mla_w_in_2"][0], QL, KVL + ROPE))
            mod_tile(i)
        for n in range(2):
            tile(("out", n), wtile(a["w_out"][0], n * TN))
        n_early = len(stream)
        slot_of, turn_of = {}, {}
        slot_uses = [0] * SLOTS
        late = [(("min", 0), wtile(a["mla_w_in_2"][0], 0, 448)),
                (("min", 1), wtile(a["mla_w_in_2"][0], 448)),
                (("min", 2), wtile(a["mla_w_in_2"][0], 960)),
                (("qup",), a["mla_w_qup_2"][0].rearrange("(j p) n -> p j n", p=P)),
                (("kvup",), a["mla_w_kvup_2"][0].rearrange("(j p) n -> p j n", p=P)),
                (("mout", 0), wtile(a["mla_w_out_2"][0], 0)),
                (("mout", 1), wtile(a["mla_w_out_2"][0], TN)),
                (("fin", 0), wtile(a["fno_w_in_2"][0], 0)),
                (("fin", 1), wtile(a["fno_w_in_2"][0], TN)),
                (("fin", 2), wtile(a["fno_w_in_2"][0], 2 * TN)),
                (("fin", 3), wtile(a["fno_w_in_2"][0], 3 * TN)),
                (("fout", 0), wtile(a["fno_w_out_2"][0], 0)),
                (("fout", 1), wtile(a["fno_w_out_2"][0], TN))]

        mod_seq = FIRST_MODS + COLUMN_MODS + GATE_MODS
        mod_turn = {i: k for k, i in enumerate(mod_seq)}

        def place(name, s):
            slot_of[name], turn_of[name] = s, slot_uses[s]
            slot_uses[s] += 1

        for i, (name, _) in enumerate(stream):
            place(name, i % EARLY_SLOTS)
        expert_turn0 = list(slot_uses)
        for s in range(SLOTS):
            slot_uses[s] += E
        for i, (name, _) in enumerate(late):
            place(name, i % LATE_SLOTS)

        def last_reader(name):
            kind = name[0]
            if kind == "ada":
                return ("mod", name[1])
            if kind == "in":
                return {3: ("zc", 0, TB - 1), 4: ("zc", 1, TB - 1), 6: ("hq", 1), 5: ("i", 2 * TB - 1),
                        1: ("k", HEADS - 1), 0: ("q", 1), 2: ("v", 2 * TB - 1), 7: ("g", TB - 1)}[name[1]]
            return {"out": ("y", TB - 1, name[-1]), "kvctx": ("kvc", TB - 1), "qup": ("qr", MH // 2 - 1),
                    "kvup": ("v2", 2 * TB - 1, 1), "mout": ("y2", TB - 1, name[-1]),
                    "fout": ("y3", TB - 1, name[-1]),
                    "min": {0: ("pa", TB - 1), 1: ("g2", 1), 2: ("g2", 3)}.get(name[-1]),
                    "fin": {0: ("fz", TB - 1, 0), 1: ("fz", TB - 1, 1), 2: ("fg", 1), 3: ("fg", 3)}.get(name[-1])}[kind]

        def slot_view(s, j, n):
            return ring[:, s * SLOT:s * SLOT + j * n].rearrange("p (j n) -> p j n", j=j)

        def wait_tile(pe, name, j=J, n=TN):
            s = slot_of[name]
            pe.wait_ge(landed[s], 16 * (turn_of[name] + 1))
            return slot_view(s, j, n)

        rows, bias_rows = gates[0:N_ROWS, P:2 * P], gates[0:N_BIAS, 0:P]
        scr = ring[:, EARLY_SLOTS * SLOT:SLOTS * SLOT]
        kd = [scr[:, d * 1024:(d + 1) * 1024] for d in range(2)]
        ictx = scr[:, 2048:3072]
        ebuf = [scr[:, 3072 + i * 1024:4096 + i * 1024] for i in range(2)]
        xbuf = [scr[:, 5120 + i * 1024:6144 + i * 1024] for i in range(3)]
        QB_, QF_ = kd
        KFB = ictx
        XFB = ebuf[0]

        hT3 = hT[:, :].rearrange("p (j t) -> p j t", j=J)
        xr3 = xres[:, :].rearrange("p (b d) -> p b d", b=TB)
        cx3 = ctxb[:, :].rearrange("p (b d) -> p b d", b=TB)
        tm3 = tmpb[:, :].rearrange("p (b d) -> p b d", b=TB)
        lfc = [ctxb[:, d * 1024:(d + 1) * 1024] for d in range(2)]
        kc = [tmpb[:, d * 1024:(d + 1) * 1024] for d in range(2)]
        gb, zb = xbuf[0], ebuf[1]
        q3 = qT[:, :].rearrange("p (h t) -> p h t", h=HEADS)
        k3 = kT[:, :].rearrange("p (h t) -> p h t", h=HEADS)
        v3 = vda[:, :].rearrange("p (b n) -> p b n", b=2 * TB)
        kg = [gates[:, d * 1024:(d + 1) * 1024] for d in range(2)]
        Bc = [gates[:, 2048 + d * 1040:2048 + (d + 1) * 1040].rearrange("p (h t) -> p h t", t=130) for d in range(2)]
        colof = lambda n: cols[:, ROWS[n][0]:ROWS[n][0] + ROWS[n][1]]
        act_cols = [act32[:, l * 256:(l + 1) * 256].rearrange("p (j m) -> p j m", j=J) for l in range(2)]
        ssq = small[:, 0:8]
        rr = small[:, 8:16]
        lbc = small[:, 16:24]
        omlb = small[:, 24:32]
        lamc = small[:, 32:33]
        dec = small[:, 40:48]
        mx = small[:, 48:56]
        rs = small[:, 56:64]
        cf = small[:, 64:80]
        lnb = small[:, 80:88]
        ssum = small[:, 88:90]
        epsc = small[:, 90:91]
        biasc = small[:, 152:152 + N_BIAS]
        ecol = small[:, 96:128]
        lbt = small[:, 128:152]
        mc = modc[:, :].rearrange("p (s k j) -> p s k j", k=2, j=J)
        MIX, MIXC, FFN, MLA, MLAC, FNO = range(6)

        claim("rows", 0)
        claim("bias_rows", 1)
        for b in range(TB):
            for g in range(2):
                claim(("xT", 0, b, g), 2 + g)
        for i in FIRST_MODS:
            claim(("mod", i), i)
            claim(("modT", i), 4 + i)
        pb = [0]

        def pclaim(name):
            claim(name, pb[0] % 4)
            pb[0] += 1

        def claim_gate(d):
            for hp in range(2):
                pclaim(("z", d, hp))
            if d == 0:
                for b in range(TB):
                    for g in range(2):
                        claim(("xT", 1, b, g), 2 + g)
            for b in range(TB):
                pclaim(("zc", d, b))

        def claim_mod(k):
            if k:
                pclaim(("modT", COLUMN_MODS[k - 1]))
            if k < len(COLUMN_MODS):
                pclaim(("mod", COLUMN_MODS[k]))

        claim_gate(0)
        claim_mod(0)
        claim_gate(1)
        claim_mod(1)
        for hp in range(2):
            pclaim(("hq", hp))
        claim_mod(2)
        for d in range(2):
            for b in range(TB):
                pclaim(("dsum", d, b))
        for b in range(2 * TB):
            pclaim(("i", b))
        claim_mod(3)
        for d in range(2):
            pclaim(("S", d))
        lb_turn = [0]

        def claim_level(i, d):
            for g in range(2):
                claim(("lv", i, d, g), 4 + lb_turn[0] % 4)
                lb_turn[0] += 1

        def claim_levels(i):
            for d in range(2 if i < len(LEVELS) else 1):
                claim_level(i, d)

        claim_levels(0)
        claim_mod(4)
        claim_levels(1)
        pclaim(("k", 0))
        pclaim(("k", 1))
        claim_mod(5)
        pclaim(("k", 2))
        pclaim(("k", 3))
        claim_levels(2)
        claim_mod(6)
        claim_levels(3)
        pclaim(("q", 0))
        claim_mod(7)
        pclaim(("q", 1))
        claim_levels(4)
        claim_mod(8)
        claim_levels(5)
        claim_mod(9)
        claim_levels(6)
        claim_mod(10)
        claim_levels(7)
        pclaim(("v", 0))
        pclaim(("v", 1))
        claim_mod(11)
        pclaim(("v", 2))
        pclaim(("v", 3))
        claim(("cross", 0), 4 + lb_turn[0] % 4)
        claim(("cross", 1), 4 + (lb_turn[0] + 1) % 4)
        lb_turn[0] += 2
        for b in range(TB):
            claim(("oh", b), 4 + lb_turn[0] % 4)
            lb_turn[0] += 1
        claim_mod(12)
        for s in range(2):
            for n in range(2):
                pclaim(("rot", s, n))
        for b in range(TB):
            pclaim(("g", b))

        context_work = [(), (("c2T", 0, 0),), (("c2T", 0, 1),), (("c2T", 1, 0),), (("c2T", 1, 1),),
                        (("kvc", 0),), (("kvc", 1),), (("kvcT",), ("kpcT",))]
        nq = 0
        for b in range(TB):
            for h in range(HEADS):
                for i in range(2):
                    claim(("s", b, h, i), nq % 4)
                    nq += 1
        for b in range(TB):
            if b:
                claim(("o", b), 7)
            for h in range(HEADS):
                n = b * HEADS + h
                claim(("aT", b, h), 4)
                if n == 0:
                    claim(("o", 0), 6)
                for name in context_work[n]:
                    claim(name, 4 if name == ("kpcT",) else 5)
                claim(("mod", GATE_MODS[n]), 7 - b)
                claim(("gt", GATE_MODS[n]), 7 - b)
        for b in range(TB):
            for g in range(2):
                claim(("mixT", b, g), 4 + (2 * b + g) % 4)
        for n in range(2):
            for b in range(TB):
                claim(("y", b, n), 2 * b + n)
        for b in range(TB):
            for g in range(2):
                claim(("x1T", b, g), 4 + (2 * b + g) % 4)
        for b in range(TB):
            claim(("logit", b), b)
        claim(("affT",), 2)
        claim(("posT",), 3)
        for j in range(J):
            claim(("xin", j), j % 4)
        for e in range(0, E, 2):
            claim(("ST", e), (e // 2) % 4)
        exp_base = list(used)
        for b in range(4):
            used[b] += E
        for b in range(TB):
            for n in range(2):
                claim(("f", b, n), 4 + 2 * b + n)

        def late_claims():
            for b in range(TB):
                for g in range(2):
                    claim(("x2T", b, g), (2 * b + g) % 4)
            for b in range(TB):
                claim(("pa", b), 4 + b)
            for m in range(MH // 2):
                claim(("g2", m), m)
            claim(("cqT",), 6)
            claim(("ckT",), 7)
            for h in range(MH // 2):
                claim(("qn", h), 4 + h % 4)
            for h in range(MH // 2):
                claim(("qr", h), 4 + h % 4)
            for h in range(MH // 2):
                claim(("qrot", h), h % 4)
            claim(("krot",), 0)
            n = 1
            for h in range(MH):
                claim(("kn", h), n % 4)
                n += 1
            for b in range(2 * TB):
                for g in range(2):
                    claim(("v2", b, g), n % 4)
                    n += 1
            k = 0
            for h in range(MH):
                for b in range(TB):
                    claim(("s2", h, b), k % 3)
                    k += 1
            k = 0
            for h in range(MH):
                for b in range(TB):
                    claim(("pT", h, b), 3 + k % 3)
                    k += 1
                claim(("o2", h), 6 + h % 2)
            for b in range(TB):
                for n in range(2):
                    claim(("y2", b, n), 2 * b + n)
            for b in range(TB):
                for g in range(2):
                    claim(("x3T", b, g), 4 + (2 * b + g) % 4)
            for n in range(2):
                for b in range(TB):
                    claim(("fz", b, n), 2 * b + n)
            for m in range(MH // 2):
                claim(("fg", m), 4 + m)
            for g in range(8):
                claim(("fa", g), g % 4)
            for m in range(4):
                claim(("fb", m), 4 + m)
            for b in range(TB):
                for n in range(2):
                    claim(("y3", b, n), 2 * b + n)

        late_claims()

        qz = [qh, smat]
        pbuf = [gates[:, i * 512:(i + 1) * 512] for i in range(4)]
        aTb = [gates[:, 2048 + i * 512:2560 + i * 512] for i in range(2)]
        oda = gates[:, 3072:4096].rearrange("p (b n) -> p b n", b=TB)
        mix = tmpb[:, :].rearrange("p (b d) -> p b d", b=TB)
        mixT = kT[:, :].rearrange("p (j t) -> p j t", j=J)
        G = [hT[:, i * D:(i + 1) * D] for i in range(4)]
        post_norm = (state, state1)
        c2 = ctxb[:, :].rearrange("p (b d) -> p b d", b=TB)
        uT = scr[:, 6144:8192].rearrange("p (j t) -> p j t", j=J)
        kvn = qT[:, 0:256].rearrange("p (b n) -> p b n", b=TB)
        kvn2 = qT[:, 512:768].rearrange("p (b n) -> p b n", b=TB)
        rtmp = gates[:, 3072:4096]
        xn = tmpb[:, :].rearrange("p (b d) -> p b d", b=TB)
        h2T = kT[:, :].rearrange("p (j t) -> p j t", j=J)
        router = qh[:, 0:J * E].rearrange("p (j e) -> p j e", j=J)
        logit = smat[:, 0:TB * E].rearrange("p (b e) -> p b e", b=TB)
        aff = smat[:, 64:64 + TB * E].rearrange("p (b e) -> p b e", b=TB)
        pos = smat[:, 128:128 + TB * E].rearrange("p (b e) -> p b e", b=TB)
        affT, work = smat[0:E, 160:416], smat[0:E, 416:672]
        top8 = smat[0:E, 672:680]
        onehot = vda[:, 0:TB * E * CAP].rearrange("p (b e c) -> p b e c", b=TB, e=E)
        onehot2 = vda[:, 0:TB * E * CAP].rearrange("p (b n) -> p b n", b=TB)
        weighted_parts = [(0, kT[:, 0:2048]), (8, vda[:, 1024:2048]), (12, ilat[:, :])]

        def weighted_of(part):
            e0, x = part
            return e0, x.rearrange("p (b e q c) -> p b e q c", b=TB, q=4, c=CAP)
        xin_all = gates[:, 0:4096].rearrange("p (j n) -> p j n", j=J)
        s_all = pair[:, :]
        sall3 = s_all[:, :].rearrange("p (e t) -> p e t", e=E)
        xin_cur = ilat[:, 0:256].rearrange("p (j c) -> p j c", j=J)
        hmT = ilat[:, 256:512].rearrange("p (j n) -> p j n", j=4)
        s_cur = ilat[:, 512:768]
        hidden_rows = state[:, 512:1024]
        eg, hm = state[0:64, 0:512], hidden_rows[0:64]
        yb = [state1[:, i * 512:(i + 1) * 512] for i in range(2)]
        zeros = qh[:, 256:256 + P + TN]
        cqn = state[:, 0:512].rearrange("p (b n) -> p b n", b=TB)
        cqT = state[:, 512:1024].rearrange("p (c t) -> p c t", c=2)
        kvl = state1[:, 0:256].rearrange("p (b n) -> p b n", b=TB)
        kpl = state1[:, 256:512].rearrange("p (b n) -> p b n", b=TB)
        u2T = kT[:, :].rearrange("p (j t) -> p j t", j=J)
        qraw = smat
        fgrow = state[:, :]
        ckv_all = qT[:, 512:1024]
        kp_all = qT[:, 0:512]
        ckv_ctx, kp_ctx = ckv_all[:, T:2 * T], kp_all[:, T:2 * T]
        rt = state1[:, 512:1024]
        knT = ring[:, (SLOTS - 1) * SLOT:].rearrange("p (h t) -> p h t", h=MH)
        v2 = gates[:, 0:4096].rearrange("p (b n) -> p b n", b=2 * TB)
        qnT = ctxb[:, :].rearrange("p (h t) -> p h t", h=MH)
        qrz = vda[:, :].rearrange("p (h t) -> p h t", h=MH)
        gT = tmpb[:, :].rearrange("p (h t) -> p h t", h=MH)
        oT = kT[:, :].rearrange("p (h t) -> p h t", h=MH)
        p2 = [smat[:, i * 512:(i + 1) * 512] for i in range(2)]
        pTs = [x[:, :].rearrange("p (k t) -> p k t", k=4) for x in (ilat, qh)]
        z3 = ctxb[:, :].rearrange("p (b d) -> p b d", b=TB)
        faT = [vda[:, i * 512:(i + 1) * 512] for i in range(4)]
        gT3 = gates[:, 0:2048].rearrange("p (h t) -> p h t", h=MH)
        oT3 = gates[:, 2048:4096].rearrange("p (h t) -> p h t", h=MH)
        fft = hT[:, 0:1280]

        def modr_of(i):
            if mod_turn[i] % 2:
                return modr1[:, :]
            return gates[:, 3072:3584] if i in GATE_MODS else vda[:, 3 * TN:4 * TN]

        block = ctx.enter_context(nc.Block())

        def expert_src(w, e, n):
            return w[bass.ds(e, 1), :, n * TN:(n + 1) * TN].rearrange("e (j p) n -> p (e j) n", p=P)

        expert_tiles = [(a["w_gate"][0], 0), (a["w_gate"][0], 1), (a["w_up"][0], 0), (a["w_up"][0], 1),
                        (a["w_down"][0], 0), (a["w_down"][0], 1)]
        expert_bank = [0, 0, 0, 0, 2, 3]

        @block.sync
        def _(sp):
            sp.dma_start(rows, a["rows"]).then_inc(sem("rows_in"), 16)
            sp.dma_start(xr3, a["x"][0].rearrange("(b p) d -> p b d", p=P)).then_inc(sem("x_in"), 16)
            sp.dma_start(bias_rows, a["bias_rows"]).then_inc(sem("rows_in"), 16)
            for i, (name, src) in enumerate(stream):
                if i >= EARLY_SLOTS:
                    wait_filled(sp, last_reader(stream[i - EARLY_SLOTS][0]))
                s = slot_of[name]
                sp.dma_start(slot_view(s, src.shape[1], src.shape[2]), src).then_inc(landed[s], 16)
            for s in (4, 5, 0, 1, 2, 3):
                if s == EARLY_SLOTS:
                    sp.wait_ge(sem("scratch_done"), 1)
                if s == EARLY_SLOTS + 1:
                    wait_filled(sp, ("kvc", TB - 1))
                if s < EARLY_SLOTS:
                    wait_filled(sp, last_reader([n for n, _ in stream if slot_of[n] == s][-1]))
                w, n = expert_tiles[s]
                sp.dma_start(slot_view(s, J, TN), expert_src(w, 0, n)).then_inc(landed[s], 16)
            with sp.Fori(1, E) as e:
                for s, (w, n) in enumerate(expert_tiles):
                    b = expert_bank[s]
                    sp.wait_ge(filled[b], e + exp_base[b])
                    sp.dma_start(slot_view(s, J, TN), expert_src(w, e, n)).then_inc(landed[s], 16)
            for i, (name, src) in enumerate(late):
                s = slot_of[name]
                if i < LATE_SLOTS:
                    sp.wait_ge(filled[expert_bank[s]], E + exp_base[expert_bank[s]])
                else:
                    wait_filled(sp, last_reader(late[i - LATE_SLOTS][0]))
                sp.dma_start(slot_view(s, src.shape[1], src.shape[2]), src).then_inc(landed[s], 16)
            for b in range(TB):
                sp.wait_ge(sem("result"), b + 1)
                sp.dma_start(out[0].rearrange("(b p) d -> p b d", p=P)[:, b, :], xr3[:, b, :])\
                  .then_inc(sem("stored"), 16)
            sp.wait_ge(sem("stored"), 16 * TB)

        @block.gpsimd
        def _(pool):
            pool.dma_start(const[:, :], a["const"]).then_inc(sem("const_in"), 16)
            pool.wait_ge(landed[FIRST_MODS[-1]], 16)
            pool.dma_start(cx3, a["ctx"][0].rearrange("(b p) d -> p b d", p=P)).then_inc(sem("ctx_in"), 16)
            for l in range(2):
                pool.dma_start(lbrow[l][:, :], a["hg_lower_bound"].rearrange("l d n -> l (d n)")[l]
                               .partition_broadcast(P)).then_inc(sem("side_in"), 16)
            for i, n in enumerate(("da_lambda_q1", "da_lambda_k1", "da_lambda_q2", "da_lambda_k2")):
                pool.dma_start(lamrow[:, i * DH:(i + 1) * DH], a[n][0].partition_broadcast(P))\
                    .then_inc(sem("side_in"), 16)
            pool.dma_start(subln[:, :], a["da_subln"][0].partition_broadcast(P)).then_inc(sem("side_in"), 16)
            pool.dma_start(hgn[:, :], a["hg_norm"][0].partition_broadcast(P)).then_inc(sem("side_in"), 16)
            pool.dma_start(scr[:, 5120:5120 + N_MASK], a["mask"]).then_inc(sem("mask_in"), 16)
            wait_filled(pool, ("oh", TB - 1))
            for i, n in enumerate(("norm_post_mix", "norm_post_ffn")):
                pool.dma_start(post_norm[i][:, :], a[n][0].partition_broadcast(P)).then_inc(sem("post_in"), 16)
            pool.dma_start(c2, a["ctx_2"][0].rearrange("(b p) d -> p b d", p=P)).then_inc(sem("ctx2_in"), 16)
            wait_filled(pool, ("g", TB - 1))
            for i, row in enumerate((a["b_ada"][0, 2 * D:3 * D], a["b_ada"][0, 5 * D:6 * D],
                                     a["b_ada_2"][0, 2 * D:3 * D], a["b_ada_2"][1, 2 * D:3 * D])):
                pool.dma_start(G[i], row.partition_broadcast(P)).then_inc(sem("post_in"), 16)
            wait_filled(pool, ("s", TB - 1, HEADS - 1, 1))
            pool.dma_start(router, a["w_router"][0].rearrange("(j p) e -> p j e", p=P)).then_inc(sem("router_in"), 16)
            pool.memset(zeros, 0.0).then_inc(sem("zeros_set"), 1)
            wait_copied(pool, ("xin", J - 1))
            wait_copied(pool, ("xin", J - 2))
            wait_copied(pool, ("ST", E - 2))
            with pool.Fori(0, E) as e:
                pool.wait_ge(filled[0], e + exp_base[0])
                pool.tensor_copy(xin_cur, xin_all[:, :, bass.ds(e * CAP, CAP)]).then_inc(sem("tokens"), 1)
                pool.wait_ge(sem("scattered"), e + 1)
                pool.tensor_copy(s_cur, s_all[:, bass.ds(e * T, T)]).then_inc(sem("scatter_matrix"), 1)
            pool.wait_ge(sem("x_updated"), 2 * TB)
            pool.dma_start(fft, a["fft"]).then_inc(sem("fft_in"), 16)
            wait_filled(pool, ("qr", MH // 2 - 1))
            pool.dma_start(fgrow, a["final_g_2"].partition_broadcast(P)).then_inc(sem("fg_in"), 16)

        @block.tensor
        def _(pe):
            def sum_of(o, terms, start=True, stop=True):
                for i, (l, r) in enumerate(terms):
                    ins = pe.matmul(o, l, r, start=start and i == 0, stop=stop and i == len(terms) - 1)
                return ins

            def turn_chunks(name, src, g):
                o = pe_take(pe, name)
                for jj in range(4):
                    j = 4 * g + jj
                    ins = pe.transpose(o[:, jj * P:(jj + 1) * P], src[:, j * P:(j + 1) * P], ident)
                fills(ins, name)

            def mod_product(i):
                w = wait_tile(pe, ("ada", i))
                o = pe_take(pe, ("mod", i))
                for jj in range(2):
                    for q in range(4):
                        j = 2 * q + jj
                        ins = pe.matmul(o[32 * q:32 * q + 32, :], act_cols[i // 12][:, j, :], w[:, j, :],
                                        start=jj == 0, stop=jj == 1)
                fills(ins, ("mod", i))

            def mod_columns(i):
                wait_copied(pe, ("mod", i))
                o = pe_take(pe, ("modT", i))
                x = modr_of(i)
                for jj in range(4):
                    ins = pe.matmul(o[:, 2 * jj:2 * jj + 2], x[:, jj * P:(jj + 1) * P], C("sum_columns"),
                                    start=True, stop=True)
                fills(ins, ("modT", i))

            def mod_gate(i):
                wait_copied(pe, ("mod", i))
                o = pe_take(pe, ("gt", i))
                fills(pe.matmul(o[:, :], C("sum_columns")[:, 0:1].broadcast_to([P, P]), modr_of(i),
                                start=True, stop=True), ("gt", i))

            def mod_step(k):
                if k:
                    mod_columns(COLUMN_MODS[k - 1])
                if k < len(COLUMN_MODS):
                    mod_product(COLUMN_MODS[k])

            pe.wait_ge(sem("const_in"), 16)
            pe.wait_ge(sem("rows_in"), 32)
            o = pe_take(pe, "rows")
            fills(pe.transpose(o[:, 0:N_ROWS], rows, ident[0:N_ROWS, 0:N_ROWS]), "rows")
            o = pe_take(pe, "bias_rows")
            fills(pe.transpose(o[:, 0:N_BIAS], bias_rows, ident[0:N_BIAS, 0:N_BIAS]), "bias_rows")
            def turn_input(s):
                for b in range(TB):
                    pe.wait_ge(sem("normed"), 2 * s + b + 1)
                    for g in range(2):
                        turn_chunks(("xT", s, b, g), (tm3, cx3)[s][:, b, :], g)

            turn_input(0)
            pe.wait_ge(sem("silu_c"), 1)
            for i in FIRST_MODS:
                mod_product(i)
                if i:
                    mod_columns(i - 1)
            mod_columns(FIRST_MODS[-1])

            pe.wait_ge(sem("hT_ready"), 1)
            def heads_out(name, w, hs, rhs, n):
                o = pe_take(pe, name)
                for i, h in enumerate(hs):
                    ins = sum_of(o[:, i * n:(i + 1) * n], [(w[:, j, h * P:(h + 1) * P], rhs[j]) for j in range(J)])
                fills(ins, name)

            def tokens_out(name, w, x, b, n=TN, n0=0):
                o = pe_take(pe, name)
                fills(sum_of(o[:, 0:n], [(x[:, j, b * P:(b + 1) * P], w[:, j, n0:n0 + n]) for j in range(J)]), name)

            lat = [hT3[:, j, 0:T] for j in range(J)]
            for d in range(2):
                w = wait_tile(pe, ("in", 3 + d))
                for hp in range(2):
                    heads_out(("z", d, hp), w, (2 * hp, 2 * hp + 1), lat, T)
                if d == 0:
                    turn_input(1)
                    for b in range(TB):
                        for g in range(2):
                            wait_copied(pe, ("xT", 1, b, g))
                for b in range(TB):
                    tokens_out(("zc", d, b), w, hT3, TB + b)
                mod_step(d)
            w = wait_tile(pe, ("in", 6))
            for hp in range(2):
                heads_out(("hq", hp), w, (2 * hp, 2 * hp + 1), lat, T)
            mod_step(2)
            for d in range(2):
                pe.wait_ge(sem("lfc_ready"), d + 1)
                tri = C(("after", "before")[d])
                for b in range(TB):
                    o = pe_take(pe, ("dsum", d, b))
                    terms = [(tri, lfc[d][:, b * TN:(b + 1) * TN])]
                    if b == d:
                        terms.append((C("ones"), lfc[d][:, (1 - b) * TN:(2 - b) * TN]))
                    fills(sum_of(o[:, :], terms), ("dsum", d, b))
            w = wait_tile(pe, ("in", 5))
            for b in range(2 * TB):
                tokens_out(("i", b), w, hT3, b)
            mod_step(3)
            for b in range(2 * TB):
                wait_copied(pe, ("i", b))
            for d in range(2):
                pe.wait_ge(sem("kd_ready"), d + 1)
                o = pe_take(pe, ("S", d))
                for h in range(HEADS):
                    ins = sum_of(o[:, h * P:(h + 1) * P],
                                 [(kd[d][:, b * TN + h * P:b * TN + (h + 1) * P],
                                   ictx[:, b * TN + h * P:b * TN + (h + 1) * P]) for b in range(TB)])
                fills(ins, ("S", d))

            def level(i):
                for d in range(2 if i < len(LEVELS) else 1):
                    pe.wait_ge(sem("x_ready"), 2 * i + d + 1)
                    x = xbuf[(2 * i + d) % 3]
                    for g in range(2):
                        o = pe_take(pe, ("lv", i, d, g))
                        for k in range(4):
                            c = (4 * g + k) * P
                            r = x if i < len(LEVELS) else qh
                            ins = pe.matmul(o[:, k * P:(k + 1) * P], x[:, c:c + P], r[:, c:c + P],
                                            start=True, stop=True)
                        fills(ins, ("lv", i, d, g))

            level(0)
            mod_step(4)
            level(1)
            w = wait_tile(pe, ("in", 1))
            for h in range(HEADS):
                heads_out(("k", h), w, (h,), [hT3[:, j, :] for j in range(J)], 2 * T)
                if h == 1:
                    mod_step(5)
            level(2)
            mod_step(6)
            level(3)
            w = wait_tile(pe, ("in", 0))
            heads_out(("q", 0), w, (0, 1), lat, T)
            mod_step(7)
            heads_out(("q", 1), w, (2, 3), lat, T)
            level(4)
            mod_step(8)
            level(5)
            mod_step(9)
            level(6)
            mod_step(10)
            level(7)
            w = wait_tile(pe, ("in", 2))
            for b in range(2 * TB):
                tokens_out(("v", b), w, hT3, b)
                if b == 1:
                    mod_step(11)
            pe.wait_ge(sem("cross_ready"), 1)
            for d in range(2):
                o = pe_take(pe, ("cross", d))
                q_ = (QF_, QB_)[d]
                for h in range(HEADS):
                    r0 = (2 * h + 1 - d) * P
                    ins = pe.matmul(o[:, h * P:(h + 1) * P], KFB[:, d * TN + h * P:d * TN + (h + 1) * P],
                                    q_[:, r0:r0 + P], start=True, stop=True)
                fills(ins, ("cross", d))
            wait_copied(pe, ("cross", 0))
            wait_copied(pe, ("cross", 1))
            wait_copied(pe, ("S", 0))
            wait_copied(pe, ("S", 1))
            pe.wait_ge(sem("state1_ready"), 1)
            wait_copied(pe, ("lv", 7, 0, 1))
            wait_copied(pe, ("lv", 7, 0, 0))
            for b in range(TB):
                o = pe_take(pe, ("oh", b))
                for h in range(HEADS):
                    c = (2 * h + b) * P
                    hs = slice(h * P, (h + 1) * P)
                    sf = state[:, h * P:(h + 1) * P] if b == 0 else state1[:, h * P:(h + 1) * P]
                    sbk = (state1 if b == 0 else state)[:, TN + h * P:TN + (h + 1) * P]
                    ins = sum_of(o[:, hs], [
                        (smat[:, c:c + P], ilat[:, b * TN + h * P:b * TN + (h + 1) * P]),
                        (XFB[:, (1 - b) * TN + h * P:(1 - b) * TN + (h + 1) * P],
                         ilat[:, (1 - b) * TN + h * P:(1 - b) * TN + (h + 1) * P]),
                        (QF_[:, c:c + P], sf),
                        (QB_[:, c:c + P], sbk)])
                fills(ins, ("oh", b))
            mod_step(12)
            for s, (x, last) in enumerate(((q3, ("q",)), (k3, ("k",)))):
                for n in range(2):
                    if s == 0:
                        wait_copied(pe, ("q", n))
                    else:
                        wait_copied(pe, ("k", 2 * n))
                        wait_copied(pe, ("k", 2 * n + 1))
                    o = pe_take(pe, ("rot", s, n))
                    for i in range(2):
                        ins = pe.matmul(o[:, i * T:(i + 1) * T], C("rotate"), x[:, 2 * n + i, 0:T],
                                        start=True, stop=True)
                    fills(ins, ("rot", s, n))
            w = wait_tile(pe, ("in", 7))
            for b in range(TB):
                tokens_out(("g", b), w, hT3, b)

            pe.wait_ge(sem("roped"), 1)

            def da_scores(b, h):
                for i in range(2):
                    o = pe_take(pe, ("s", b, h, i))
                    fills(pe.matmul(o[:, :], qz[i][:, h * T + b * P:h * T + (b + 1) * P], k3[:, h, :],
                                    start=True, stop=True), ("s", b, h, i))

            def context_product(kind, b=None, g=None):
                if kind == "c2T":
                    pe.wait_ge(sem("c2_normed"), b + 1)
                    turn_chunks(("c2T", b, g), c2[:, b, :], g)
                elif kind == "kvc":
                    w = wait_tile(pe, ("kvctx",), J, KVL + ROPE)
                    for g in range(2):
                        wait_copied(pe, ("c2T", b, g))
                    tokens_out(("kvc", b), w, uT, b, KVL + ROPE)
                else:
                    pe.wait_ge(sem("kvc_normed"), TB)
                    o = pe_take(pe, (kind,))
                    for b in range(TB):
                        src = kvn[:, b, 0:KVL] if kind == "kvcT" else kvn2[:, b, :]
                        ins = pe.transpose(o[:, b * P:(b + 1) * P], src, ident)
                    fills(ins, (kind,))

            da = [(b, h) for b in range(TB) for h in range(HEADS)]
            for b in range(2 * TB):
                wait_copied(pe, ("v", b))
            da_scores(*da[0])
            da_scores(*da[1])
            for n, (b, h) in enumerate(da):
                pe.wait_ge(sem("a_ready"), n + 1)
                o = pe_take(pe, ("aT", b, h))
                for k in range(4):
                    ins = pe.transpose(o[:, k * P:(k + 1) * P], pbuf[2 * (n % 2)][:, k * P:(k + 1) * P], ident)
                fills(ins, ("aT", b, h))
                if n + 2 < len(da):
                    da_scores(*da[n + 2])
                if n:
                    mod_gate(GATE_MODS[n - 1])
                wait_copied(pe, ("aT", b, h))
                o = pe_take(pe, ("o", b)) if h == 0 else bank[turns[("o", b)][0]]
                ins = sum_of(o[:, h * P:(h + 1) * P],
                             [(aTb[n % 2][:, k * P:(k + 1) * P], v3[:, k, h * P:(h + 1) * P]) for k in range(4)])
                if h == HEADS - 1:
                    fills(ins, ("o", b))
                for name in context_work[n]:
                    context_product(*name)
                mod_product(GATE_MODS[n])
            mod_gate(GATE_MODS[-1])

            for b in range(TB):
                pe.wait_ge(sem("mix_ready"), b + 1)
                for g in range(2):
                    turn_chunks(("mixT", b, g), mix[:, b, :], g)
            for b in range(TB):
                for g in range(2):
                    wait_copied(pe, ("mixT", b, g))
            for b in range(TB):
                for n in range(2):
                    tokens_out(("y", b, n), wait_tile(pe, ("out", n)), mixT, b)

            for b in range(TB):
                pe.wait_ge(sem("x1_normed"), b + 1)
                for g in range(2):
                    turn_chunks(("x1T", b, g), xn[:, b, :], g)
            for b in range(TB):
                for g in range(2):
                    wait_copied(pe, ("x1T", b, g))
            pe.wait_ge(sem("router_in"), 16)
            for b in range(TB):
                o = pe_take(pe, ("logit", b))
                fills(sum_of(o[:, 0:E], [(h2T[:, j, b * P:(b + 1) * P], router[:, j, :]) for j in range(J)]),
                      ("logit", b))
            pe.wait_ge(sem("aff_ready"), 1)
            o = pe_take(pe, ("affT",))
            for b in range(TB):
                ins = pe.transpose(o[0:E, b * P:(b + 1) * P], aff[:, b, :], ident)
            fills(ins, ("affT",))
            pe.wait_ge(sem("rank_ready"), 1)
            o = pe_take(pe, ("posT",))
            for b in range(TB):
                ins = pe.transpose(o[:, b * E:(b + 1) * E], work[:, b * P:(b + 1) * P], ident[0:E, 0:E])
            fills(ins, ("posT",))
            pe.wait_ge(sem("onehot_ready"), 1)
            for j in range(J):
                o = pe_take(pe, ("xin", j))
                fills(sum_of(o[:, :], [(xn[:, b, j * P:(j + 1) * P], onehot2[:, b, :]) for b in range(TB)]),
                      ("xin", j))
            for e in range(0, E, 2):
                k = 0 if e < 8 else 1 if e < 12 else 2
                e0, x = weighted_of(weighted_parts[k])
                pe.wait_ge(sem("weighted_ready"), k + 1)
                o = pe_take(pe, ("ST", e))
                for i in range(2):
                    for b in range(TB):
                        ins = pe.transpose(o[:, (2 * i + b) * P:(2 * i + b + 1) * P],
                                           x[:, b, e + i - e0].rearrange("p q c -> p (q c)"), ident)
                fills(ins, ("ST", e))

            pe.wait_ge(sem("zeros_set"), 1)
            for k in range(4):
                pe_take(pe, ("f", k // 2, k % 2))
                ins = pe.matmul(bank[4 + k][:, :], zeros[:, 0:P], zeros[:, P:P + TN], start=True, stop=False)
            ins.then_inc(sem("scattered"), 1)

            def expert(e, last):
                pe.wait_ge(sem("tokens"), e + 1)
                for s in range(4):
                    pe.wait_ge(landed[s], (e + (expert_turn0[s] + 1)) * 16)
                pe.wait_ge(freed[0], e + exp_base[0])
                w = [slot_view(s, J, TN) for s in range(SLOTS)]
                for j in range(J):
                    for t in range(4):
                        ins = pe.matmul(bank[0][32 * t:32 * t + 32, :], xin_cur[:, j, :], w[t][:, j, :],
                                        start=j == 0, stop=j == J - 1)
                ins.then_inc(filled[0], 1)
                pe.wait_ge(freed[0], e + (exp_base[0] + 1))
                pe.wait_ge(freed[1], e + exp_base[1])
                for k in range(4):
                    ins = pe.transpose(bank[1][:, k * P:(k + 1) * P], hidden_rows[:, k * P:(k + 1) * P], ident)
                ins.then_inc(filled[1], 1)
                pe.wait_ge(freed[1], e + (exp_base[1] + 1))
                for n in range(2):
                    pe.wait_ge(landed[4 + n], (e + (expert_turn0[4 + n] + 1)) * 16)
                    pe.wait_ge(freed[2 + n], e + exp_base[2 + n])
                    for c in range(2):
                        for q in range(4):
                            k = 2 * q + c
                            ins = pe.matmul(bank[2 + n][32 * q:32 * q + 32, :],
                                            hmT[:, k % 4, 32 * (k // 4):32 * (k // 4) + 32], w[4 + n][:, k, :],
                                            start=c == 0, stop=c == 1)
                    ins.then_inc(filled[2 + n], 1)
                pe.wait_ge(sem("scatter_matrix"), e + 1)
                for n in range(2):
                    pe.wait_ge(freed[2 + n], e + (exp_base[2 + n] + 1))
                for n in range(2):
                    for b in range(TB):
                        ins = pe.matmul(bank[4 + 2 * b + n][:, :], s_cur[:, b * P:(b + 1) * P], yb[n],
                                        start=False, stop=last)
                        if last:
                            fills(ins, ("f", b, n))
                if not last:
                    ins.then_inc(sem("scattered"), 1)

            with pe.Fori(0, E - 1) as e:
                expert(e, False)
            expert(E - 1, True)

            for b in range(TB):
                pe.wait_ge(sem("x2_normed"), b + 1)
                for g in range(2):
                    turn_chunks(("x2T", b, g), xn[:, b, :], g)
            w = wait_tile(pe, ("min", 0), J, 448)
            for b in range(TB):
                for g in range(2):
                    wait_copied(pe, ("x2T", b, g))
            for b in range(TB):
                tokens_out(("pa", b), w, u2T, b, 448)
            lat2 = [u2T[:, j, :] for j in range(J)]

            def mla_gate(m):
                w = wait_tile(pe, ("min", 1 + m // 2))
                heads_out(("g2", m), w, (2 * (m % 2), 2 * (m % 2) + 1), lat2, T)

            mla_gate(0)
            mla_gate(1)
            pe.wait_ge(sem("lat_normed"), 1)
            o = pe_take(pe, ("cqT",))
            for c in range(2):
                for b in range(TB):
                    ins = pe.transpose(o[:, c * T + b * P:c * T + (b + 1) * P], cqn[:, b, c * P:(c + 1) * P], ident)
            fills(ins, ("cqT",))
            o = pe_take(pe, ("ckT",))
            for b in range(TB):
                pe.transpose(o[:, b * P:(b + 1) * P], kvl[:, b, 0:KVL], ident)
            for b in range(TB):
                ins = pe.transpose(o[:, T + b * P:T + (b + 1) * P], kpl[:, b, :], ident)
            fills(ins, ("ckT",))
            mla_gate(2)
            mla_gate(3)
            wq = wait_tile(pe, ("qup",), 2, MH * (NOPE + ROPE))
            wkv = wait_tile(pe, ("kvup",), 1, MH * (NOPE + KVL))
            pe.wait_ge(sem("latT_ready"), 1)
            HW = NOPE + ROPE
            for m in range(MH // 2):
                o = pe_take(pe, ("qn", m))
                for i in range(2):
                    h = 2 * m + i
                    ins = sum_of(o[:, i * T:(i + 1) * T],
                                 [(wq[:, c, h * HW:h * HW + NOPE], cqT[:, c, :]) for c in range(2)])
                fills(ins, ("qn", m))
            wqh = wq.rearrange("p c (h w) -> p c h w", w=HW)
            for m in range(MH // 2):
                o = pe_take(pe, ("qr", m))
                for i in range(2):
                    ins = sum_of(o[64 * i:64 * i + 64, 0:T],
                                 [(wqh[:, c, 2 * m + i, NOPE:HW], cqT[:, c, :]) for c in range(2)])
                fills(ins, ("qr", m))
            for m in range(MH // 2):
                wait_copied(pe, ("qr", m))
                o = pe_take(pe, ("qrot", m))
                fills(pe.matmul(o[:, 0:T], C("rotate"), qraw[:, m * T:(m + 1) * T], start=True, stop=True),
                      ("qrot", m))
            o = pe_take(pe, ("krot",))
            fills(pe.matmul(o[:, 0:T], C("rotate"), kp_all[:, 0:T], start=True, stop=True), ("krot",))
            for h in range(MH):
                o = pe_take(pe, ("kn", h))
                fills(pe.matmul(o[:, :], wkv[:, 0, h * 2 * P:h * 2 * P + P], ckv_all, start=True, stop=True),
                      ("kn", h))
            wvh = wkv.rearrange("p j (h w) -> p (j h) w", w=2 * P)
            for b in range(2 * TB):
                for g in range(2):
                    o = pe_take(pe, ("v2", b, g))
                    fills(pe.matmul(o[:, :], ckv_all[:, b * P:(b + 1) * P], wvh[:, 4 * g:4 * g + 4, P:2 * P],
                                    start=True, stop=True), ("v2", b, g))
            pe.wait_ge(sem("qk2_ready"), 1)
            for m in range(MH // 2):
                wait_copied(pe, ("qn", m))

            def mla_scores(h, b):
                if b == 0:
                    wait_copied(pe, ("kn", h))
                o = pe_take(pe, ("s2", h, b))
                fills(sum_of(o[:, :], [(qnT[:, h, b * P:(b + 1) * P], knT[:, h, :]),
                                       (qrz[:, h, b * P:(b + 1) * P], kp_all)]), ("s2", h, b))

            ml = [(h, b) for h in range(MH) for b in range(TB)]
            mla_scores(*ml[0])
            mla_scores(*ml[1])
            for b in range(2 * TB):
                for g in range(2):
                    wait_copied(pe, ("v2", b, g))
            for n, (h, b) in enumerate(ml):
                pe.wait_ge(sem("p2_ready"), n + 1)
                o = pe_take(pe, ("pT", h, b))
                for k in range(4):
                    ins = pe.transpose(o[:, k * P:(k + 1) * P], p2[n % 2][:, k * P:(k + 1) * P], ident)
                fills(ins, ("pT", h, b))
                if n + 2 < len(ml):
                    mla_scores(*ml[n + 2])
                if b == TB - 1:
                    wait_copied(pe, ("pT", h, 0))
                    wait_copied(pe, ("pT", h, 1))
                    o = pe_take(pe, ("o2", h))
                    fills(sum_of(o[:, 0:T], [(v2[:, k, h * P:(h + 1) * P], pTs[h % 2][:, k, :]) for k in range(4)]),
                          ("o2", h))
            for h in range(MH):
                wait_copied(pe, ("o2", h))
            for b in range(TB):
                for n in range(2):
                    tokens_out(("y2", b, n), wait_tile(pe, ("mout", n)), oT, b)

            for b in range(TB):
                pe.wait_ge(sem("x3_normed"), b + 1)
                for g in range(2):
                    turn_chunks(("x3T", b, g), xn[:, b, :], g)
            for b in range(TB):
                for g in range(2):
                    wait_copied(pe, ("x3T", b, g))
            for n in range(2):
                w = wait_tile(pe, ("fin", n))
                for b in range(TB):
                    tokens_out(("fz", b, n), w, u2T, b)
            for m in range(MH // 2):
                w = wait_tile(pe, ("fin", 2 + m // 2))
                heads_out(("fg", m), w, (2 * (m % 2), 2 * (m % 2) + 1), lat2, T)
            for b in range(TB):
                for n in range(2):
                    wait_copied(pe, ("fz", b, n))
            pe.wait_ge(sem("fft_in"), 16)
            for g in range(8):
                o = pe_take(pe, ("fa", g))
                fills(sum_of(o[:, :], [(z3[:, b, g * P:(g + 1) * P], fft[:, b * TN:(b + 1) * TN])
                                       for b in range(TB)]), ("fa", g))
                if g % 2:
                    m = g // 2
                    wait_copied(pe, ("fa", g - 1))
                    wait_copied(pe, ("fa", g))
                    o = pe_take(pe, ("fb", m))
                    for i in range(2):
                        x = faT[(g - 1 + i) % 4]
                        ins = sum_of(o[:, i * T:(i + 1) * T], [(fft[:, 2 * TN:2 * TN + P], x[:, 0:T]),
                                                               (fft[:, 2 * TN + P:2 * TN + 2 * P], x[:, T:2 * T])])
                    fills(ins, ("fb", m))
            for m in range(4):
                wait_copied(pe, ("fb", m))
            for b in range(TB):
                for n in range(2):
                    tokens_out(("y3", b, n), wait_tile(pe, ("fout", n)), oT3, b)

        @block.scalar
        def _(act):
            st = Steps(act, sem("act_step"), reached)

            def root_inverse(c0, n, width, signal, pairs=False):
                st.settle()
                if pairs:
                    for i in range(n):
                        st.did(act.activation(ssq[:, c0 + i:c0 + i + 1], ssq[:, c0 + 2 * i:c0 + 2 * i + 1],
                                              ACT.Identity, bias=ssq[:, c0 + 2 * i + 1:c0 + 2 * i + 2]))
                        st.settle()
                st.did(act.activation(lnb[:, c0:c0 + n], ssq[:, c0:c0 + n], ACT.Ln, bias=epsc, scale=1.0 / width))
                st.settle()
                st.did(act.activation(rr[:, c0:c0 + n], lnb[:, c0:c0 + n], ACT.Exp, scale=-0.5), sem(signal))

            def square(src, c, n=None):
                n = n or src.shape[1]
                st.did(act.activation(junk[:, 0:n], src, ACT.Square, accum_out=ssq[:, c:c + 1]))
                st.settle()

            act.wait_ge(sem("eps_set"), 1)
            wait_copied(act, "rows")
            st.did(act.activation(ecol[:, 0:32], cols[:, 0:32], ACT.Exp, scale=-1.0), sem("exp_c"))
            st.settle()
            def input_norm(s, x, name):
                act.wait_ge(sem(name), 16)
                for b in range(TB):
                    square(x[:, b, :], 2 * s + b)
                root_inverse(2 * s, 2, D, "rstd_in")

            def turned_modulated(tag, dst, s, t0=0, tail=()):
                for b in range(TB):
                    name = tag + (b, 0)
                    o = wait_filled(act, name)
                    for j in range(4):
                        ins = act.activation(dst[:, j, t0 + b * P:t0 + (b + 1) * P], o[:, j * P:(j + 1) * P],
                                             ACT.Identity, bias=mc[:, s, 0, j:j + 1], scale=mc[:, s, 1, j:j + 1])
                        frees(st, ins, name) if j == 3 else st.did(ins)

            input_norm(0, xr3, "x_in")
            for b in range(TB):
                o = wait_filled(act, ("xT", 0, b, 0))
                frees(st, act.activation(hT3[:, 0:4, b * P:(b + 1) * P],
                                         o[:, :].rearrange("p (j t) -> p j t", j=4), ACT.Copy), ("xT", 0, b, 0))

            def take_mod(i):
                k = mod_turn[i]
                if k >= 2:
                    p = mod_seq[k - 2]
                    wait_filled(act, ("gt" if p in GATE_MODS else "modT", p))
                o = wait_filled(act, ("mod", i))
                frees(st, act.activation(modr_of(i), o[:, :], ACT.Copy), ("mod", i))

            for i in FIRST_MODS:
                take_mod(i)
            input_norm(1, cx3, "ctx_in")
            act.wait_ge(sem("mc_ready"), 1)
            turned_modulated(("xT", 1), hT3, MIXC, T)
            act.wait_ge(sem("lb_shift"), 1)
            st.did(act.activation(lbt[:, 0:16], lbt[:, 0:16], ACT.Exp), sem("lb_exp"))
            act.wait_ge(sem("lbrow_shift"), 1)
            for l in range(2):
                st.did(act.activation(lbrow[l][:, :], lbrow[l][:, :], ACT.Exp), sem("lbrow_exp"))
            act.wait_ge(sem("lam_dot"), 1)
            st.did(act.activation(cf[:, 0:2], cf[:, 0:2], ACT.Exp), sem("lam_exp"))
            for d in range(2):
                for hp in range(2):
                    o = wait_filled(act, ("z", d, hp))
                    frees(st, act.activation(kg[d][:, hp * TN:(hp + 1) * TN], o[:, :], ACT.Exp, scale=-1.0),
                          ("z", d, hp))
                for b in range(TB):
                    o = wait_filled(act, ("zc", d, b))
                    frees(st, act.activation(kc[d][:, b * TN:(b + 1) * TN], o[:, :], ACT.Exp, scale=-1.0),
                          ("zc", d, b))
                take_mod(COLUMN_MODS[d])
                act.wait_ge(sem("f_ready"), d + 1)
                st.did(act.activation(ebuf[d], kg[d], ACT.Ln), sem("lf_ready"))
                act.wait_ge(sem("fc_ready"), d + 1)
                st.did(act.activation(lfc[d], kc[d], ACT.Ln), sem("lfc_ready"))
            for hp in range(2):
                o = wait_filled(act, ("hq", hp))
                frees(st, act.activation(qh[:, hp * TN:(hp + 1) * TN], o[:, :], ACT.Copy), ("hq", hp))
            take_mod(COLUMN_MODS[2])
            for d in range(2):
                for b in range(TB):
                    o = wait_filled(act, ("dsum", d, b))
                    frees(st, act.activation(kd[d][:, b * TN:(b + 1) * TN], o[:, :], ACT.Exp), ("dsum", d, b))
            for b in range(2 * TB):
                o = wait_filled(act, ("i", b))
                dst = (ilat if b < TB else ictx)[:, (b % TB) * TN:(b % TB + 1) * TN]
                frees(st, act.activation(dst, o[:, :], ACT.Copy), ("i", b))
            take_mod(COLUMN_MODS[3])
            for d in range(2):
                o = wait_filled(act, ("S", d))
                frees(st, act.activation(state[:, d * TN:(d + 1) * TN], o[:, :], ACT.Copy), ("S", d))

            def decays(lo, hi):
                for k in range(lo, hi):
                    act.wait_ge(sem("distance"), k + 1)
                    st.did(act.activation(ebuf[k % 2], ebuf[k % 2], ACT.Exp), sem("decay"))

            def take_heads(tag, h):
                o = wait_filled(act, (tag, h))
                dst = k3[:, h, :] if tag == "k" else qT[:, h * TN:(h + 1) * TN]
                frees(st, act.activation(dst, o[:, :], ACT.Copy), (tag, h))

            decays(0, 4)
            take_mod(COLUMN_MODS[4])
            decays(4, 7)
            take_heads("k", 0)
            take_heads("k", 1)
            take_mod(COLUMN_MODS[5])
            take_heads("k", 2)
            take_heads("k", 3)
            decays(7, 8)
            take_mod(COLUMN_MODS[6])
            decays(8, 11)
            take_heads("q", 0)
            take_mod(COLUMN_MODS[7])
            take_heads("q", 1)
            decays(11, 12)
            take_mod(COLUMN_MODS[8])
            decays(12, 14)
            take_mod(COLUMN_MODS[9])
            st.did(act.activation(QF_.rearrange("p (h t) -> p h t", t=P), Bc[0][:, :, 1:P + 1], ACT.Exp))
            kb3 = Bc[1].rearrange("p (h b) t -> p h b t", b=TB)
            kf3 = Bc[0].rearrange("p (h b) t -> p h b t", b=TB)
            st.did(act.activation(KFB[:, TN:2 * TN].rearrange("p (h t) -> p h t", t=P), kb3[:, :, 1, 0:P], ACT.Exp))
            st.did(act.activation(dec[:, 0:4], kf3[:, :, 0, P:P + 1].rearrange("p h t -> p (h t)"), ACT.Exp))
            st.did(act.activation(dec[:, 4:8], kb3[:, :, 1, P:P + 1].rearrange("p h t -> p (h t)"), ACT.Exp),
                   sem("end_decay"))
            act.wait_ge(sem("end_distance"), 1)
            st.did(act.activation(KFB[:, 0:TN], KFB[:, 0:TN], ACT.Exp))
            st.did(act.activation(QB_, QB_, ACT.Exp), sem("end_decay"))
            take_mod(COLUMN_MODS[10])
            for b in range(2 * TB):
                o = wait_filled(act, ("v", b))
                frees(st, act.activation(v3[:, b, :], o[:, :], ACT.Copy), ("v", b))
                if b == 1:
                    take_mod(COLUMN_MODS[11])
            for d in range(2):
                o = wait_filled(act, ("cross", d))
                frees(st, act.activation(XFB[:, d * TN:(d + 1) * TN], o[:, :], ACT.Copy), ("cross", d))
            for b in range(TB):
                o = wait_filled(act, ("oh", b))
                for h in range(HEADS):
                    square(o[:, h * P:(h + 1) * P], 4 * b + h)
            root_inverse(0, 8, P, "rstd_oh")
            st.settle()
            act.wait_ge(sem("ctx2_in"), 16)
            for b in range(TB):
                wait_copied(act, ("oh", b))
            for b in range(TB):
                square(c2[:, b, :], b)
            root_inverse(0, 2, D, "rstd_c2")
            st.settle()

            for b in range(TB):
                o = wait_filled(act, ("g", b))
                st.did(act.activation(gb[:, b * TN:(b + 1) * TN], o[:, :], ACT.Exp, scale=-1.0), sem("gb_exp"))
                frees(st, act.activation(zb[:, b * TN:(b + 1) * TN], o[:, :], ACT.Copy), ("g", b))

            da = [(b, h) for b in range(TB) for h in range(HEADS)]

            def da_exp(n):
                b, h = da[n]
                if n >= 2:
                    wait_filled(act, ("aT",) + da[n - 2])
                for i in range(2):
                    act.wait_ge(sem("da_max"), 2 * n + i + 1)
                    o = bank[turns[("s", b, h, i)][0]]
                    c = (2 * n + i) % 4
                    frees(st, act.activation(pbuf[c], o[:, :], ACT.Exp, bias=mx[:, c:c + 1], scale=DH ** -0.5,
                                             accum_out=rs[:, c:c + 1]), ("s", b, h, i))

            def take_context(kind, b=None, g=None):
                if kind == "c2T":
                    o = wait_filled(act, ("c2T", b, g))
                    for jj in range(4):
                        j = 4 * g + jj
                        ins = act.activation(uT[:, j, b * P:(b + 1) * P], o[:, jj * P:(jj + 1) * P], ACT.Identity,
                                             bias=mc[:, MLAC, 0, j:j + 1], scale=mc[:, MLAC, 1, j:j + 1])
                        frees(st, ins, ("c2T", b, g)) if jj == 3 else st.did(ins)
                elif kind == "kvc":
                    o = wait_filled(act, ("kvc", b))
                    square(o[:, 0:KVL], b)
                    root_inverse(b, 1, KVL, "rstd_kvc")
                    st.settle()

            da_exp(0)
            da_exp(1)
            for n, (b, h) in enumerate(da):
                o = wait_filled(act, ("aT", b, h))
                frees(st, act.activation(aTb[n % 2], o[:, :], ACT.Copy), ("aT", b, h))
                if n + 2 < len(da):
                    da_exp(n + 2)
                if h == HEADS - 1:
                    o = wait_filled(act, ("o", b))
                    for i in range(HEADS):
                        square(o[:, i * P:(i + 1) * P], 4 * b + i)
                    root_inverse(4 * b, 4, P, "rstd_o")
                    st.settle()
                for name in context_work[n]:
                    take_context(*name)
                take_mod(GATE_MODS[n])
            for b in range(TB):
                for g in range(2):
                    o = wait_filled(act, ("mixT", b, g))
                    frees(st, act.activation(mixT[:, 4 * g:4 * g + 4, b * P:(b + 1) * P],
                                             o[:, :].rearrange("p (j t) -> p j t", j=4), ACT.Copy), ("mixT", b, g))

            def branch_norm(tag, b):
                for n in range(2):
                    o = wait_filled(act, (tag, b, n))
                    square(o[:, :], 2 * b + n)
                st.did(act.activation(ssum[:, b:b + 1], ssq[:, 2 * b:2 * b + 1], ACT.Identity,
                                      bias=ssq[:, 2 * b + 1:2 * b + 2]))
                st.settle()
                st.did(act.activation(lnb[:, b:b + 1], ssum[:, b:b + 1], ACT.Ln, bias=epsc, scale=1.0 / D))
                st.settle()
                st.did(act.activation(rr[:, b:b + 1], lnb[:, b:b + 1], ACT.Exp, scale=-0.5), sem("rstd_y"))

            def residual_norm(k, b):
                act.wait_ge(sem("x_updated"), TB * k + b + 1)
                square(xr3[:, b, :], 4 + b)
                root_inverse(4 + b, 1, D, "rstd_x")
                st.settle()

            for b in range(TB):
                branch_norm("y", b)
                residual_norm(0, b)
            turned_modulated(("x1T",), h2T, FFN)
            for b in range(TB):
                act.wait_ge(sem("logit_max"), b + 1)
                frees(st, act.activation(aff[:, b, :], bank[turns[("logit", b)][0]][:, 0:E], ACT.Exp,
                                         bias=mx[:, b:b + 1], accum_out=rs[:, b:b + 1]), ("logit", b))
            for j in range(1, J, 2):
                o = wait_filled(act, ("xin", j))
                frees(st, act.activation(xin_all[:, j, :], o[:, :], ACT.Identity, bias=mc[:, FFN, 0, j:j + 1],
                                         scale=mc[:, FFN, 1, j:j + 1]), ("xin", j))
            for e in range(0, E, 2):
                o = wait_filled(act, ("ST", e))
                frees(st, act.activation(s_all[:, e * T:(e + 2) * T], o[:, :], ACT.Copy), ("ST", e))
            with act.Fori(0, E) as e:
                act.wait_ge(filled[0], e + (exp_base[0] + 1))
                act.activation(eg, bank[0][0:64, :], ACT.Exp, scale=-1.0).then_inc(sem("gate_exp"), 1)
                act.wait_ge(filled[1], e + (exp_base[1] + 1))
                act.activation(hmT, bank[1][:, :].rearrange("p (j n) -> p j n", j=4)[:, :, 0:64], ACT.Copy)\
                   .then_inc(freed[1], 1)
                act.wait_ge(filled[2], e + (exp_base[2] + 1))
                act.activation(yb[0], bank[2][:, :], ACT.Copy).then_inc(freed[2], 1)

            for b in range(TB):
                branch_norm("f", b)
            for b in range(TB):
                residual_norm(1, b)
            turned_modulated(("x2T",), u2T, MLA)
            for b in range(TB):
                o = wait_filled(act, ("pa", b))
                square(o[:, 0:QL], b)
                square(o[:, QL:QL + KVL], 2 + b)
            root_inverse(0, 2, QL, "rstd_lat")
            root_inverse(2, 2, KVL, "rstd_lat")
            st.settle()
            for m in range(MH // 2):
                o = wait_filled(act, ("g2", m))
                st.did(act.activation(tmpb[:, m * TN:(m + 1) * TN], o[:, :], ACT.Exp, scale=-1.0), sem("g2_exp"))
            for m in range(MH // 2):
                o = wait_filled(act, ("qn", m))
                frees(st, act.activation(ctxb[:, m * TN:(m + 1) * TN], o[:, :], ACT.Copy), ("qn", m))
            for m in range(MH // 2):
                o = wait_filled(act, ("qr", m))
                frees(st, act.activation(qraw[:, m * T:(m + 1) * T], o[:, 0:T], ACT.Copy), ("qr", m))
            for h in range(MH):
                o = wait_filled(act, ("kn", h))
                frees(st, act.activation(knT[:, h, :], o[:, :], ACT.Copy), ("kn", h))
            for b in range(2 * TB):
                for g in range(2):
                    o = wait_filled(act, ("v2", b, g))
                    if g == 0:
                        frees(st, act.activation(v2[:, b, 0:TN], o[:, :], ACT.Copy), ("v2", b, g))
            ml = [(h, b) for h in range(MH) for b in range(TB)]

            def mla_exp(n):
                if n >= 2:
                    wait_filled(act, ("pT",) + ml[n - 2])
                act.wait_ge(sem("mla_max"), n + 1)
                frees(st, act.activation(p2[n % 2], bank[turns[("s2",) + ml[n]][0]][:, :], ACT.Exp,
                                         bias=mx[:, n % 2:n % 2 + 1], scale=(NOPE + ROPE) ** -0.5,
                                         accum_out=rs[:, n % 2:n % 2 + 1]), ("s2",) + ml[n])

            mla_exp(0)
            mla_exp(1)
            for n, (h, b) in enumerate(ml):
                o = wait_filled(act, ("pT", h, b))
                frees(st, act.activation(pTs[h % 2][:, :, b * P:(b + 1) * P],
                                         o[:, :].rearrange("p (k t) -> p k t", k=4), ACT.Copy), ("pT", h, b))
                if n + 2 < len(ml):
                    mla_exp(n + 2)
            for b in range(TB):
                residual_norm(2, b)
            turned_modulated(("x3T",), u2T, FNO)
            for b in range(TB):
                o = wait_filled(act, ("fz", b, 0))
                frees(st, act.activation(z3[:, b, 0:TN], o[:, :], ACT.Copy), ("fz", b, 0))
            for m in range(MH // 2):
                o = wait_filled(act, ("fg", m))
                st.did(act.activation(gates[:, m * TN:(m + 1) * TN], o[:, :], ACT.Exp, scale=-1.0), sem("fg_exp"))
            for g in range(8):
                o = wait_filled(act, ("fa", g))
                frees(st, act.activation(faT[g % 4], o[:, :], ACT.Copy), ("fa", g))
            for b in range(TB):
                residual_norm(3, b)

        @block.vector
        def _(dve):
            st = Steps(dve, sem("dve_step"), reached)

            def step(ins, signal=None):
                st.did(ins, sem(signal) if signal else None)

            def sigmoid_in_place(x, steps=2):
                step(dve.tensor_scalar(x, x, 1.0, None, ALU.add))
                st.settle()
                step(dve.reciprocal(x, x))
                st.settle()

            st_eps = dve.memset(epsc, EPS)
            step(st_eps, "eps_set")
            step(dve.memset(act32[:, :], 0.0))
            for d in range(2):
                step(dve.memset(Bc[d][:, :, 0:1], 0.0))
            o = wait_filled(dve, "rows")
            frees(st, dve.tensor_copy(cols[:, :], o[:, 0:N_ROWS]), "rows")
            o = wait_filled(dve, "bias_rows")
            frees(st, dve.tensor_copy(biasc, o[:, 0:N_BIAS]), "bias_rows")
            st.settle()
            dve.wait_ge(sem("exp_c"), 1)
            sigmoid_in_place(ecol[:, 0:32])
            for l in range(2):
                for i in range(2):
                    c0 = (2 * l + i) * J
                    ins = dve.tensor_tensor(act_cols[l][:, :, i:i + 1].rearrange("p j m -> p (j m)"),
                                            cols[:, c0:c0 + J], ecol[:, c0:c0 + J], ALU.mult)
                    step(ins, "silu_c") if (l, i) == (1, 1) else step(ins)
            def input_norm(s):
                dve.wait_ge(sem("rstd_in"), s + 1)
                for b in range(TB):
                    c = 2 * s + b
                    step(dve.tensor_scalar((tm3, cx3)[s][:, b, :], (xr3, cx3)[s][:, b, :], rr[:, c:c + 1], None,
                                           ALU.mult), "normed")
            def turned_modulated(tag, dst, s, t0=0):
                for b in range(TB):
                    name = tag + (b, 1)
                    o = wait_filled(dve, name)
                    for j in range(4, 8):
                        ins = dve.tensor_scalar(dst[:, j, t0 + b * P:t0 + (b + 1) * P],
                                                o[:, (j - 4) * P:(j - 3) * P], mc[:, s, 1, j:j + 1],
                                                mc[:, s, 0, j:j + 1], ALU.mult, ALU.add)
                        frees(st, ins, name) if j == 7 else step(ins)

            input_norm(0)
            for b in range(TB):
                o = wait_filled(dve, ("xT", 0, b, 1))
                frees(st, dve.tensor_copy(hT3[:, 4:8, b * P:(b + 1) * P],
                                          o[:, :].rearrange("p (j t) -> p j t", j=4)), ("xT", 0, b, 1))

            columns_of = {0: (MIX, MIXC), 6: (FFN,), 12: (MLA, MLAC), 18: (FNO,)}

            def mod_columns(i):
                sets = columns_of[i // 6 * 6]
                k, half = divmod(i % 6, 2)
                o = wait_filled(dve, ("modT", i))
                v = o[:, 0:8].rearrange("p (j r) -> p j r", r=2)
                for r, s in enumerate(sets):
                    c0 = (2 * s + k) * J + 4 * half
                    ins = dve.tensor_tensor(modc[:, c0:c0 + 4], v[:, :, r:r + 1].rearrange("p j r -> p (j r)"),
                                            biasc[:, 4 * i:4 * i + 4], ALU.add)
                    frees(st, ins, ("modT", i)) if r == len(sets) - 1 else step(ins)

            def fold(s, norm, signal):
                st.settle()
                step(dve.scalar_tensor_tensor(mc[:, s, 1, :], mc[:, s, 1, :], 1.0, norm, ALU.add, ALU.mult), signal)
                st.settle()

            for i in FIRST_MODS:
                mod_columns(i)
            fold(MIX, colof("pre_mix"), None)
            fold(MIXC, colof("pre_mix"), "mc_ready")
            wait_copied(dve, ("xT", 0, 1, 0))
            st.settle()
            for j in range(J):
                step(dve.tensor_scalar(hT3[:, j, 0:T], hT3[:, j, 0:T], mc[:, MIX, 1, j:j + 1], mc[:, MIX, 0, j:j + 1],
                                       ALU.mult, ALU.add), "hT_ready" if j == J - 1 else None)
            input_norm(1)
            turned_modulated(("xT", 1), hT3, MIXC, T)
            lo = colof("lower")
            step(dve.tensor_tensor(lbt[:, 16:24], lo[:, 0:8], lo[:, 8:16], ALU.max))
            st.settle()
            step(dve.tensor_tensor(lbt[:, 0:8], lo[:, 0:8], lbt[:, 16:24], ALU.subtract))
            step(dve.tensor_tensor(lbt[:, 8:16], lo[:, 8:16], lbt[:, 16:24], ALU.subtract), "lb_shift")
            dve.wait_ge(sem("side_in"), 16 * 8)
            mrow = kd[0]
            step(dve.tensor_tensor(mrow, lbrow[0][:, :], lbrow[1][:, :], ALU.max))
            st.settle()
            for l in range(2):
                step(dve.tensor_tensor(lbrow[l][:, :], lbrow[l][:, :], mrow, ALU.subtract),
                     "lbrow_shift" if l else None)
            for i in range(2):
                step(dve.tensor_tensor(lamrow[:, 2 * i * DH:(2 * i + 1) * DH], lamrow[:, 2 * i * DH:(2 * i + 1) * DH],
                                       lamrow[:, (2 * i + 1) * DH:(2 * i + 2) * DH], ALU.mult))
            st.settle()
            for i in range(2):
                step(dve.tensor_reduce(cf[:, i:i + 1], lamrow[:, 2 * i * DH:(2 * i + 1) * DH], AX, ALU.add),
                     "lam_dot" if i else None)
            dve.wait_ge(sem("lb_exp"), 1)
            step(dve.tensor_tensor(lbt[:, 16:24], lbt[:, 0:8], lbt[:, 8:16], ALU.add))
            st.settle()
            step(dve.reciprocal(lbt[:, 16:24], lbt[:, 16:24]))
            st.settle()
            step(dve.tensor_tensor(lbc, lbt[:, 0:8], lbt[:, 16:24], ALU.mult))
            st.settle()
            step(dve.tensor_scalar(omlb, lbc, -1.0, 1.0, ALU.mult, ALU.add))
            dve.wait_ge(sem("lbrow_exp"), 2)
            step(dve.tensor_tensor(mrow, lbrow[0][:, :], lbrow[1][:, :], ALU.add))
            st.settle()
            step(dve.reciprocal(mrow, mrow))
            st.settle()
            step(dve.tensor_tensor(lbrow[0][:, :], lbrow[0][:, :], mrow, ALU.mult))
            st.settle()
            step(dve.tensor_scalar(lbrow[1][:, :], lbrow[0][:, :], -1.0, 1.0, ALU.mult, ALU.add))
            dve.wait_ge(sem("lam_exp"), 1)
            step(dve.tensor_tensor(cf[:, 2:3], cf[:, 0:1], cf[:, 1:2], ALU.subtract))
            st.settle()
            step(dve.tensor_scalar(lamc, cf[:, 2:3], -1.0, -LAMBDA_INIT, ALU.mult, ALU.add))
            step(dve.tensor_scalar(subln[:, :], subln[:, :], 1.0 - LAMBDA_INIT, None, ALU.mult))

            for d in range(2):
                wait_copied(dve, ("z", d, 0))
                wait_copied(dve, ("z", d, 1))
                sigmoid_in_place(kg[d])
                for h in range(HEADS):
                    c = 4 * d + h
                    step(dve.tensor_scalar(kg[d][:, h * T:(h + 1) * T], kg[d][:, h * T:(h + 1) * T],
                                           omlb[:, c:c + 1], lbc[:, c:c + 1], ALU.mult, ALU.add),
                         "f_ready" if h == HEADS - 1 else None)
                wait_copied(dve, ("zc", d, 0))
                wait_copied(dve, ("zc", d, 1))
                if d:
                    mod_columns(COLUMN_MODS[0])
                sigmoid_in_place(kc[d])
                kc3 = kc[d].rearrange("p (b n) -> p b n", b=TB)
                for l in (1, 0):
                    r = lbrow[l][:, d * TN:(d + 1) * TN].rearrange("p (a n) -> p a n", a=1).broadcast_to([P, TB, TN])
                    step(dve.tensor_tensor(kc3, kc3, r, ALU.mult if l else ALU.add), None if l else "fc_ready")
                    st.settle()
                dve.wait_ge(sem("lf_ready"), d + 1)
                step(dve.tensor_scalar(kg[d], kg[d], -1.0, 1.0, ALU.mult, ALU.add))
                for hb in range(2 * HEADS):
                    step(dve.tensor_tensor_scan(Bc[d][:, hb, 1:P + 1], C("ones"), ebuf[d][:, hb * P:(hb + 1) * P],
                                                0.0, ALU.mult, ALU.add))
                dve.wait_ge(sem("lfc_ready"), d + 1)
                step(dve.tensor_scalar(kc[d], kc[d], -1.0, 1.0, ALU.mult, ALU.add))
            mod_columns(COLUMN_MODS[1])
            st.settle()
            for d in range(2):
                wait_copied(dve, ("dsum", d, 0))
                wait_copied(dve, ("dsum", d, 1))
                step(dve.tensor_tensor(kd[d], kd[d], kc[d], ALU.mult), "kd_ready")

            def halves(ap, L):
                return ap.rearrange("p (n x l) -> p n x l", x=2, l=L)

            def distance(k):
                i, d = divmod(k, 2)
                L = LEVELS[i]
                nb = P // (2 * L)
                e = ebuf[k % 2].rearrange("p (h n x l) -> p h n x l", h=2 * HEADS, x=2, l=L)
                shift = Bc[d][:, :, 1 - d:P + 1 - d].rearrange("p h (n x l) -> p h n x l", x=2, l=L)
                mid = Bc[d][:, :, 0:P].rearrange("p h (n x l) -> p h n x l", x=2, l=L)[:, :, :, 1, 0:1]\
                    .broadcast_to([P, 2 * HEADS, nb, L])
                step(dve.tensor_tensor(e[:, :, :, 0, :], mid, shift[:, :, :, 0, :], ALU.subtract))
                step(dve.tensor_tensor(e[:, :, :, 1, :], shift[:, :, :, 1, :], mid, ALU.subtract), "distance")

            def decayed(k):
                i, d = divmod(k, 2)
                L = LEVELS[i]
                dve.wait_ge(sem("decay"), k + 1)
                if k >= 3:
                    wait_filled(dve, ("lv", (k - 3) // 2, (k - 3) % 2, 1))
                x, e = halves(xbuf[k % 3], L), halves(ebuf[k % 2], L)
                kk, qq = halves(kg[d], L), halves(qh[:, :], L)
                first, second = (kk, qq) if d == 0 else (qq, kk)
                step(dve.tensor_tensor(x[:, :, 0, :], e[:, :, 0, :], first[:, :, 0, :], ALU.mult))
                step(dve.tensor_tensor(x[:, :, 1, :], e[:, :, 1, :], second[:, :, 1, :], ALU.mult), "x_ready")
                st.settle()

            def take(i, d, m):
                for g in range(2):
                    o = wait_filled(dve, ("lv", i, d, g))
                    st.settle()
                    mk = masks[:, m * P:(m + 1) * P].rearrange("p (a n) -> p a n", a=1).broadcast_to([P, 4, P])
                    frees(st, dve.copy_predicated(smat[:, g * TN:(g + 1) * TN].rearrange("p (a n) -> p a n", a=4),
                                                  mk, o[:, :].rearrange("p (a n) -> p a n", a=4)), ("lv", i, d, g))

            ng = colof("norm_g_2")

            def columns_before(i):
                ks = {0: (2,), 1: (3,), 2: (4,), 3: (5,), 4: (6,), 5: (7,), 6: (8,), 7: (9,)}[i]
                for k in ks:
                    mod_columns(COLUMN_MODS[k])
                if i == 1:
                    fold(FFN, colof("pre_ffn"), None)
                if i == 5:
                    fold(MLA, ng[:, 0:J], None)
                    fold(MLAC, ng[:, 0:J], None)

            wait_copied(dve, ("hq", 1))
            dve.wait_ge(sem("mask_in"), 16)
            step(dve.tensor_copy(masks[:, :], scr[:, 5120:5120 + N_MASK]))
            step(dve.memset(smat[:, :], 0.0))
            n_lv = 2 * len(LEVELS)
            distance(0)
            for k in range(n_lv):
                if k + 1 < n_lv:
                    distance(k + 1)
                decayed(k)
                if k:
                    if k % 2:
                        columns_before(k // 2)
                    take(*divmod(k - 1, 2), k - 1)
            wait_filled(dve, ("lv", (n_lv - 3) // 2, (n_lv - 3) % 2, 1))
            step(dve.tensor_tensor(xbuf[n_lv % 3], kg[0], kg[1], ALU.add), "x_ready")
            take(*divmod(n_lv - 1, 2), n_lv - 1)
            columns_before(len(LEVELS))
            take(len(LEVELS), 0, n_lv)
            kf3 = Bc[0].rearrange("p (h b) t -> p h b t", b=TB)
            step(dve.tensor_tensor(KFB[:, 0:TN].rearrange("p (h t) -> p h t", t=P),
                                   kf3[:, :, 0, P:P + 1].broadcast_to([P, HEADS, P]), kf3[:, :, 0, 1:P + 1],
                                   ALU.subtract))
            step(dve.tensor_tensor(QB_.rearrange("p (h t) -> p h t", t=P),
                                   Bc[1][:, :, P:P + 1].broadcast_to([P, 2 * HEADS, P]), Bc[1][:, :, 0:P],
                                   ALU.subtract), "end_distance")
            kgb = [kg[d].rearrange("p (h b t) -> p h b t", b=TB, t=P) for d in range(2)]
            kfb = KFB.rearrange("p (d h t) -> p d h t", d=2, t=P)
            dve.wait_ge(sem("end_decay"), 2)
            step(dve.tensor_tensor(QF_, QF_, qh[:, :], ALU.mult))
            step(dve.tensor_tensor(kfb[:, 1], kfb[:, 1], kgb[1][:, :, 1, :], ALU.mult))
            step(dve.tensor_tensor(kfb[:, 0], kfb[:, 0], kgb[0][:, :, 0, :], ALU.mult))
            step(dve.tensor_tensor(QB_, QB_, qh[:, :], ALU.mult), "cross_ready")
            for d in range(2):
                wait_copied(dve, ("S", d))
                step(dve.tensor_tensor(state1[:, d * TN:(d + 1) * TN].rearrange("p (h t) -> p h t", t=P),
                                       state[:, d * TN:(d + 1) * TN].rearrange("p (h t) -> p h t", t=P),
                                       dec[:, 4 * d:4 * d + 4].rearrange("p (h t) -> p h t", t=1)
                                       .broadcast_to([P, HEADS, P]), ALU.mult), "state1_ready" if d else None)
            mod_columns(COLUMN_MODS[10])
            dve.wait_ge(sem("rstd_oh"), 1)
            for b in range(TB):
                o = wait_filled(dve, ("oh", b))
                for h in range(HEADS):
                    ins = dve.scalar_tensor_tensor(mix[:, b, TN + h * P:TN + (h + 1) * P], o[:, h * P:(h + 1) * P],
                                                   rr[:, 4 * b + h:4 * b + h + 1], hgn[:, :], ALU.mult, ALU.mult)
                    frees(st, ins, ("oh", b)) if h == HEADS - 1 else step(ins)
            mod_columns(COLUMN_MODS[11])
            fold(FNO, ng[:, J:2 * J], None)
            step(dve.memset(qh[64:P, :], 0.0))
            step(dve.memset(smat[0:64, :], 0.0))
            cosb = C("cos").rearrange("p (a t) -> p a t", a=1).broadcast_to([P, HEADS, T])
            sin2 = C("sin").rearrange("p (a t) -> p a t", a=1).broadcast_to([P, 2, T])
            for s, (x, tag) in enumerate(((q3, "q"), (k3, "k"))):
                for n in range(2):
                    o = wait_filled(dve, ("rot", s, n))
                    frees(st, dve.tensor_tensor(rtmp[:, n * TN:(n + 1) * TN].rearrange("p (a t) -> p a t", a=2),
                                                o[:, :].rearrange("p (a t) -> p a t", a=2), sin2, ALU.mult),
                          ("rot", s, n))
                step(dve.tensor_tensor(x[:, :, 0:T], x[:, :, 0:T], cosb, ALU.mult))
                st.settle()
                r3 = rtmp.rearrange("p (a t) -> p a t", a=HEADS)
                if s == 0:
                    for i in range(2):
                        ps = slice(64 * i, 64 * i + 64)
                        step(dve.tensor_tensor(qz[i][ps, :].rearrange("p (a t) -> p a t", a=HEADS),
                                               x[ps, :, 0:T], r3[ps], ALU.add))
                    st.settle()
                else:
                    step(dve.tensor_tensor(x[:, :, 0:T], x[:, :, 0:T], r3, ALU.add), "roped")
            def output_gate(b):
                dve.wait_ge(sem("gb_exp"), b + 1)
                g_ = gb[:, b * TN:(b + 1) * TN]
                sigmoid_in_place(g_)
                wait_copied(dve, ("g", b))
                step(dve.tensor_tensor(g_, g_, zb[:, b * TN:(b + 1) * TN], ALU.mult))
                st.settle()
                step(dve.tensor_tensor(mix[:, b, TN:2 * TN], mix[:, b, TN:2 * TN], g_, ALU.mult),
                     "scratch_done" if b == TB - 1 else None)

            da = [(b, h) for b in range(TB) for h in range(HEADS)]

            def da_max(n):
                for i in range(2):
                    o = wait_filled(dve, ("s",) + da[n] + (i,))
                    c = (2 * n + i) % 4
                    step(dve.tensor_reduce(mx[:, 4 + c:5 + c], o[:, :], AX, ALU.max))
                    st.settle()
                    step(dve.tensor_scalar(mx[:, c:c + 1], mx[:, 4 + c:5 + c], -DH ** -0.5, None, ALU.mult), "da_max")

            def gate_rows(n):
                if n == 0:
                    dve.wait_ge(sem("post_in"), 16 * 6)
                i, half = n // 2, n % 2
                o = wait_filled(dve, ("gt", GATE_MODS[n]))
                cs = slice(half * TN, (half + 1) * TN)
                frees(st, dve.tensor_tensor(G[i][:, cs], o[:, :], G[i][:, cs], ALU.add), ("gt", GATE_MODS[n]))
                if i < 2:
                    st.settle()
                    step(dve.tensor_tensor(G[i][:, cs], G[i][:, cs], post_norm[i][:, cs], ALU.mult))

            def take_context(kind, b=None):
                if kind == "kvc":
                    dve.wait_ge(sem("rstd_kvc"), b + 1)
                    o = bank[turns[("kvc", b)][0]]
                    step(dve.tensor_scalar(kvn[:, b, :], o[:, 0:KVL], rr[:, b:b + 1], None, ALU.mult))
                    frees(st, dve.tensor_copy(kvn2[:, b, :].rearrange("p (a n) -> p a n", a=2),
                                              o[:, KVL:KVL + ROPE].rearrange("p (a n) -> p a n", a=1)
                                              .broadcast_to([P, 2, ROPE])), ("kvc", b))
                    st.settle()
                    step(dve.memset(cf[:, 8:9], 0.0), "kvc_normed")
                elif kind == "kvcT":
                    o = wait_filled(dve, ("kvcT",))
                    frees(st, dve.tensor_scalar(ckv_ctx, o[:, 0:T], colof("g_kva"), None, ALU.mult), ("kvcT",))
                elif kind == "kpcT":
                    o = wait_filled(dve, ("kpcT",))
                    frees(st, dve.tensor_copy(kp_ctx, o[:, 0:T]), ("kpcT",))

            dve.wait_ge(sem("rstd_c2"), 1)
            for b in range(TB):
                step(dve.tensor_scalar(c2[:, b, :], c2[:, b, :], rr[:, b:b + 1], None, ALU.mult), "c2_normed")
            def da_difference(n):
                b, h = da[n]
                wait_copied(dve, ("s", b, h, 0))
                wait_copied(dve, ("s", b, h, 1))
                c = (2 * n) % 4
                step(dve.reciprocal(cf[:, c:c + 2], rs[:, c:c + 2]))
                st.settle()
                step(dve.tensor_tensor(cf[:, 4 + c:5 + c], cf[:, c + 1:c + 2], lamc, ALU.mult))
                st.settle()
                step(dve.tensor_scalar(pbuf[c + 1], pbuf[c + 1], cf[:, 4 + c:5 + c], None, ALU.mult))
                st.settle()
                step(dve.scalar_tensor_tensor(pbuf[c], pbuf[c], cf[:, c:c + 1], pbuf[c + 1], ALU.mult, ALU.add),
                     "a_ready")

            output_gate(0)
            da_max(0)
            da_max(1)
            da_difference(0)
            for n, (b, h) in enumerate(da):
                if n + 1 < len(da):
                    da_difference(n + 1)
                if n + 2 < len(da):
                    da_max(n + 2)
                if n == 0:
                    output_gate(1)
                if n:
                    gate_rows(n - 1)
                    if context_work[n - 1] and context_work[n - 1][0][0] == "kvc":
                        take_context(*context_work[n - 1][0])
                if h == HEADS - 1:
                    dve.wait_ge(sem("rstd_o"), b + 1)
                    o = bank[turns[("o", b)][0]]
                    for i in range(HEADS):
                        ins = dve.scalar_tensor_tensor(mix[:, b, i * P:(i + 1) * P], o[:, i * P:(i + 1) * P],
                                                       rr[:, 4 * b + i:4 * b + i + 1], subln[:, :], ALU.mult, ALU.mult)
                        frees(st, ins, ("o", b)) if i == HEADS - 1 else step(ins)
                    st.settle()
                    step(dve.memset(cf[:, 8:9], 0.0), "mix_ready")

            gate_rows(len(da) - 1)

            take_context("kvcT")
            take_context("kpcT")

            step(dve.memset(hidden_rows[64:P], 0.0))

            def add_branch(tag, i, b, norm):
                if norm:
                    dve.wait_ge(sem("rstd_y"), norm)
                for n in range(2):
                    o = wait_filled(dve, (tag, b, n))
                    cs = slice(n * TN, (n + 1) * TN)
                    if norm:
                        ins = dve.scalar_tensor_tensor(xn[:, b, cs], o[:, :], rr[:, b:b + 1], G[i][:, cs],
                                                       ALU.mult, ALU.mult)
                    else:
                        ins = dve.tensor_tensor(xn[:, b, cs], o[:, :], G[i][:, cs], ALU.mult)
                    frees(st, ins, (tag, b, n))
                st.settle()
                step(dve.tensor_tensor(xr3[:, b, :], xr3[:, b, :], xn[:, b, :], ALU.add), "x_updated")

            def normalise(k, b, signal):
                dve.wait_ge(sem("rstd_x"), TB * k + b + 1)
                step(dve.tensor_scalar(xn[:, b, :], xr3[:, b, :], rr[:, 4 + b:5 + b], None, ALU.mult), signal)

            for b in range(TB):
                add_branch("y", 0, b, b + 1)
                normalise(0, b, "x1_normed")
            turned_modulated(("x1T",), h2T, FFN)
            for b in range(TB):
                o = wait_filled(dve, ("logit", b))
                step(dve.tensor_reduce(mx[:, 4 + b:5 + b], o[:, 0:E], AX, ALU.max))
                st.settle()
                step(dve.tensor_scalar(mx[:, b:b + 1], mx[:, 4 + b:5 + b], -1.0, None, ALU.mult), "logit_max")
            for b in range(TB):
                wait_copied(dve, ("logit", b))
            step(dve.reciprocal(cf[:, 0:2], rs[:, 0:2]))
            st.settle()
            for b in range(TB):
                step(dve.tensor_scalar(aff[:, b, :], aff[:, b, :], cf[:, b:b + 1], None, ALU.mult),
                     "aff_ready" if b else None)
            o = wait_filled(dve, ("affT",))
            frees(st, dve.tensor_copy(affT, o[0:E, 0:T]), ("affT",))
            st.settle()
            for r in range(CAP // 8):
                src = affT if r == 0 else work
                step(dve.max(top8, src))
                st.settle()
                step(dve.match_replace(work, top8, src, -1.0))
                st.settle()
            step(dve.tensor_scalar(affT, work, 0.0, None, ALU.is_lt))
            st.settle()
            step(dve.tensor_tensor_scan(work, affT, affT, 0.0, ALU.add, ALU.max))
            st.settle()
            step(dve.tensor_tensor(work, work, affT, ALU.mult), "rank_ready")
            o = wait_filled(dve, ("posT",))
            frees(st, dve.tensor_copy(smat[:, 128:128 + TB * E], o[:, 0:TB * E]), ("posT",))
            st.settle()
            rank = C("rank").rearrange("p (a c) -> p a c", a=1).broadcast_to([P, E, CAP])
            wide = lambda x: x.rearrange("p (e c) -> p e c", c=1).broadcast_to([P, E, CAP])
            for b in range(TB):
                step(dve.tensor_tensor(onehot[:, b], wide(pos[:, b, :]), rank, ALU.is_equal),
                     "onehot_ready" if b else None)
            st.settle()
            for part in weighted_parts:
                e0, x = weighted_of(part)
                ne = x.shape[2]
                for b in range(TB):
                    hot = onehot[:, b, e0:e0 + ne].rearrange("p e (a c) -> p e a c", a=1)\
                        .broadcast_to([P, ne, 4, CAP])
                    af = aff[:, b, e0:e0 + ne].rearrange("p (e a c) -> p e a c", a=1, c=1)\
                        .broadcast_to([P, ne, 4, CAP])
                    step(dve.tensor_tensor(x[:, b], hot, af, ALU.mult), "weighted_ready" if b else None)
            for j in range(0, J, 2):
                o = wait_filled(dve, ("xin", j))
                frees(st, dve.tensor_scalar(xin_all[:, j, :], o[:, :], mc[:, FFN, 1, j:j + 1],
                                            mc[:, FFN, 0, j:j + 1], ALU.mult, ALU.add), ("xin", j))
            wait_filled(dve, ("ST", E - 2))
            step(dve.memset(vda[:, :], 0.0))
            hidden = sem("hidden_step")
            with dve.Fori(0, E) as e:
                dve.wait_ge(sem("gate_exp"), e + 1)
                dve.tensor_scalar(eg, eg, 1.0, None, ALU.add).then_inc(hidden, 1)
                dve.wait_ge(hidden, e * 3 + 1)
                dve.reciprocal(eg, eg).then_inc(hidden, 1)
                dve.wait_ge(hidden, e * 3 + 2)
                dve.tensor_tensor(eg, eg, bank[0][0:64, :], ALU.mult).then_inc(hidden, 1)
                dve.wait_ge(hidden, e * 3 + 3)
                dve.tensor_tensor(hm, eg, bank[0][64:P, :], ALU.mult).then_inc(freed[0], 1)
                dve.wait_ge(filled[3], e + (exp_base[3] + 1))
                dve.tensor_copy(yb[1], bank[3][:, :]).then_inc(freed[3], 1)

            for b in range(TB):
                add_branch("f", 1, b, TB + b + 1)
            for b in range(TB):
                normalise(1, b, "x2_normed")
            turned_modulated(("x2T",), u2T, MLA)
            dve.wait_ge(sem("rstd_lat"), 2)
            for b in range(TB):
                o = bank[turns[("pa", b)][0]]
                step(dve.tensor_scalar(cqn[:, b, :], o[:, 0:QL], rr[:, b:b + 1], None, ALU.mult))
                step(dve.tensor_scalar(kvl[:, b, :], o[:, QL:QL + KVL], rr[:, 2 + b:3 + b], None, ALU.mult))
                frees(st, dve.tensor_copy(kpl[:, b, :].rearrange("p (a n) -> p a n", a=2),
                                          o[:, QL + KVL:448].rearrange("p (a n) -> p a n", a=1)
                                          .broadcast_to([P, 2, ROPE])), ("pa", b))
            st.settle()
            step(dve.memset(cf[:, 8:9], 0.0), "lat_normed")
            o = wait_filled(dve, ("cqT",))
            for c in range(2):
                ins = dve.tensor_scalar(cqT[:, c, :], o[:, c * T:(c + 1) * T], colof("g_qa")[:, c:c + 1], None, ALU.mult)
                frees(st, ins, ("cqT",)) if c else step(ins)
            o = wait_filled(dve, ("ckT",))
            step(dve.tensor_scalar(ckv_all[:, 0:T], o[:, 0:T], colof("g_kva"), None, ALU.mult))
            frees(st, dve.tensor_copy(kp_all[:, 0:T], o[:, T:2 * T]), ("ckT",))
            st.settle()
            step(dve.memset(cf[:, 8:9], 0.0), "latT_ready")
            st.settle()

            def silu_bank(x, name):
                sigmoid_in_place(x)
                o = bank[turns[name][0]]
                frees(st, dve.tensor_tensor(x, x, o[:, :], ALU.mult), name)

            for m in range(MH // 2):
                dve.wait_ge(sem("g2_exp"), m + 1)
                silu_bank(tmpb[:, m * TN:(m + 1) * TN], ("g2", m))
            cs_, sn = C("cos"), C("sin")
            for m in range(MH // 2):
                o = wait_filled(dve, ("qrot", m))
                t_ = rt[:, (m % 2) * T:(m % 2 + 1) * T]
                frees(st, dve.tensor_tensor(t_, o[:, 0:T], sn, ALU.mult), ("qrot", m))
                q_ = qraw[:, m * T:(m + 1) * T]
                step(dve.tensor_tensor(q_, q_, cs_, ALU.mult))
                st.settle()
                for i in range(2):
                    ps = slice(64 * i, 64 * i + 64)
                    step(dve.tensor_tensor(qrz[ps, 2 * m + i, :], q_[ps], t_[ps], ALU.add))
            o = wait_filled(dve, ("krot",))
            st.settle()
            frees(st, dve.tensor_tensor(rt[:, 0:T], o[:, 0:T], sn, ALU.mult), ("krot",))
            step(dve.tensor_tensor(kp_all[:, 0:T], kp_all[:, 0:T], cs_, ALU.mult))
            st.settle()
            step(dve.tensor_tensor(kp_all[:, 0:T], kp_all[:, 0:T], rt[:, 0:T], ALU.add), "qk2_ready")
            for b in range(2 * TB):
                o = wait_filled(dve, ("v2", b, 1))
                frees(st, dve.tensor_copy(v2[:, b, TN:2 * TN], o[:, :]), ("v2", b, 1))

            ml = [(h, b) for h in range(MH) for b in range(TB)]

            def mla_max(n):
                o = wait_filled(dve, ("s2",) + ml[n])
                c = n % 2
                step(dve.tensor_reduce(mx[:, 4 + c:5 + c], o[:, :], AX, ALU.max))
                st.settle()
                step(dve.tensor_scalar(mx[:, c:c + 1], mx[:, 4 + c:5 + c], -(NOPE + ROPE) ** -0.5, None, ALU.mult),
                     "mla_max")

            mla_max(0)
            mla_max(1)

            def mla_normalise(n):
                wait_copied(dve, ("s2",) + ml[n])
                c = n % 2
                step(dve.reciprocal(cf[:, c:c + 1], rs[:, c:c + 1]))
                st.settle()
                step(dve.tensor_scalar(p2[c], p2[c], cf[:, c:c + 1], None, ALU.mult), "p2_ready")

            mla_normalise(0)
            for n, (h, b) in enumerate(ml):
                if n + 1 < len(ml):
                    mla_normalise(n + 1)
                if n + 2 < len(ml):
                    mla_max(n + 2)
                if b == TB - 1 and h:
                    o = wait_filled(dve, ("o2", h - 1))
                    frees(st, dve.tensor_tensor(oT[:, h - 1, :], o[:, 0:T], gT[:, h - 1, :], ALU.mult),
                          ("o2", h - 1))
            o = wait_filled(dve, ("o2", MH - 1))
            frees(st, dve.tensor_tensor(oT[:, MH - 1, :], o[:, 0:T], gT[:, MH - 1, :], ALU.mult), ("o2", MH - 1))
            st.settle()
            for b in range(TB):
                add_branch("y2", 2, b, 0)
                normalise(2, b, "x3_normed")
            turned_modulated(("x3T",), u2T, FNO)
            for b in range(TB):
                o = wait_filled(dve, ("fz", b, 1))
                frees(st, dve.tensor_copy(z3[:, b, TN:2 * TN], o[:, :]), ("fz", b, 1))
            for m in range(MH // 2):
                dve.wait_ge(sem("fg_exp"), m + 1)
                silu_bank(gates[:, m * TN:(m + 1) * TN], ("fg", m))
            st.settle()
            for m in range(4):
                o = wait_filled(dve, ("fb", m))
                frees(st, dve.tensor_tensor(gates[:, 2048 + m * TN:2048 + (m + 1) * TN], o[:, :],
                                            gates[:, m * TN:(m + 1) * TN], ALU.mult), ("fb", m))
            dve.wait_ge(sem("fg_in"), 16)
            for b in range(TB):
                add_branch("y3", 3, b, 0)
                dve.wait_ge(sem("rstd_x"), TB * 3 + b + 1)
                step(dve.scalar_tensor_tensor(xr3[:, b, :], xr3[:, b, :], rr[:, 4 + b:5 + b], fgrow,
                                              ALU.mult, ALU.mult), "result")


_ROW_SOURCES = {"c": "c", "c_ctx": "c_ctx", "c_2": "c_2", "c_ctx_2": "c_ctx_2", "pre_mix": "norm_pre_mix",
                "pre_ffn": "norm_pre_ffn", "norm_g_2": "norm_g_2", "lower": "hg_lower_bound",
                "g_qa": "mla_g_qa_2", "g_kva": "mla_g_kva_2"}
_DIRECT = ["x", "ctx", "w_ada", "b_ada", "norm_post_mix", "norm_post_ffn", "w_in", "da_lambda_q1", "da_lambda_k1",
           "da_lambda_q2", "da_lambda_k2", "da_subln", "hg_lower_bound", "hg_norm", "w_out", "w_router", "w_gate",
           "w_up", "w_down", "ctx_2", "w_ada_2", "b_ada_2", "mla_w_in_2", "mla_w_qup_2", "mla_w_kvup_2",
           "mla_w_out_2", "fno_w_in_2", "fno_w_out_2", "final_g_2"]


def build(nc, arrays):
    a = {}
    for name, x in arrays.items():
        a[name] = nc.dram_tensor(name + "_dram", x.shape, mybir.dt.from_np(x.dtype), kind="ExternalInput").ap()
    out = nc.dram_tensor("out_dram", (1, T, D), F32, kind="ExternalOutput").ap()
    block_program(nc, a, out)


def laid_out(inputs):
    arrays = {n: np.ascontiguousarray(inputs[n]) for n in _DIRECT}
    arrays["rows"] = np.concatenate([np.asarray(inputs[_ROW_SOURCES[n]]).reshape(-1, P) for n in ROWS])
    arrays["bias_rows"] = np.concatenate([np.asarray(inputs[n]).reshape(-1, P) for n in ("b_ada", "b_ada_2")])
    arrays["const"], arrays["mask"], arrays["fft"] = CONST, level_masks(), fourier_constants()
    return arrays


def kernel(**inputs):
    import concourse.bacc as bacc
    from concourse.bass_utils import run_bass_kernel_spmd

    arrays = laid_out(inputs)
    nc = bacc.Bacc("TRN2", target_bir_lowering=False, num_devices=1)
    build(nc, arrays)
    r = run_bass_kernel_spmd(nc, [{n + "_dram": x for n, x in arrays.items()}], core_ids=[0])
    return r.results[0]["out_dram"]
```
